# Optimizing a Trainium2 kernel written in Bass

```python
import jax, jax.numpy as jnp
from jax import lax
import numpy as np

D_MODEL = 1024
BATCH = 1
SEQ = 2048
DEPTH = 1

DN_HEADS = 4
DN_HEAD_DIM = 128
DN_WIDTH = DN_HEADS * DN_HEAD_DIM
CONV_WIDTH = 5
CHUNK = 64
ATTN_Q_HEADS = 8
ATTN_KV_HEADS = 2
ATTN_HEAD_DIM = 64
ATTN_GROUP = ATTN_Q_HEADS // ATTN_KV_HEADS
ATTN_WIDTH = ATTN_Q_HEADS * ATTN_HEAD_DIM
WINDOW = 128
ATTN_BLOCK = 128
ROT_DIM = ATTN_HEAD_DIM // 4
ROPE_THETA = 500000.0
MIX_WIDTH = DN_WIDTH + ATTN_WIDTH
IN_SPLITS = [DN_WIDTH, DN_WIDTH, DN_WIDTH, DN_WIDTH, 2 * DN_HEADS, 2 * DN_HEADS,
             ATTN_WIDTH, ATTN_KV_HEADS * ATTN_HEAD_DIM, ATTN_KV_HEADS * ATTN_HEAD_DIM]
IN_WIDTH = sum(IN_SPLITS)
IN_OFFSETS = [int(o) for o in np.cumsum(IN_SPLITS)[:-1]]
N_GROUPS = 8
EXPERTS_PER_GROUP = 8
N_EXPERTS = N_GROUPS * EXPERTS_PER_GROUP
TOP_K = 2
EXPERT_FF = 256
EPS = 1e-6

kernel_name = "hybrid_deltanet_swa_hiermoe_encoder"

def rmsnorm(x, w):
    x32 = x.astype(jnp.float32)
    y = x32 * lax.rsqrt(jnp.mean(x32 * x32, axis=-1, keepdims=True) + EPS)
    return (y * w.astype(jnp.float32)).astype(x.dtype)

def l2norm(x):
    return x * lax.rsqrt(jnp.sum(x * x, axis=-1, keepdims=True) + EPS)

def centred_depthwise_conv(x, w):
    k, c = w.shape
    return lax.conv_general_dilated(
        x, w[:, None, :].astype(x.dtype), window_strides=(1,),
        padding=[(k // 2, k // 2)], dimension_numbers=('NWC', 'WIO', 'NWC'),
        feature_group_count=c)

def gated_delta_chunked(q, k, v, g, beta):
    b, s, h, dk = q.shape
    dv = v.shape[-1]
    n = s // CHUNK

    def chunks(t):
        return jnp.moveaxis(t.reshape((b, n, CHUNK) + t.shape[2:]), 2, 3)

    qc, kc, vc = chunks(q), chunks(k), chunks(v)
    gc = jnp.cumsum(chunks(g), axis=-1)
    bc = chunks(beta)
    kb = kc * bc[..., None]
    vb = vc * bc[..., None]
    tri = jnp.tril(jnp.ones((CHUNK, CHUNK), bool))
    strict = jnp.tril(jnp.ones((CHUNK, CHUNK), bool), -1)
    diff = gc[..., :, None] - gc[..., None, :]
    decay = jnp.where(tri, jnp.exp(jnp.where(tri, diff, 0.0)), 0.0)
    a_mat = jnp.where(strict, jnp.einsum('bnhid,bnhjd->bnhij', kb, kc) * decay, 0.0)
    eye = jnp.eye(CHUNK, dtype=jnp.float32)
    t_mat = lax.linalg.triangular_solve(eye + a_mat, jnp.broadcast_to(eye, a_mat.shape),
                                        left_side=True, lower=True)
    u = jnp.einsum('bnhij,bnhje->bnhie', t_mat, vb)
    w = jnp.einsum('bnhij,bnhjd->bnhid', t_mat, kb * jnp.exp(gc)[..., None])
    attn_intra = jnp.where(tri, jnp.einsum('bnhid,bnhjd->bnhij', qc, kc) * decay, 0.0)
    q_dec = qc * jnp.exp(gc)[..., None]
    k_dec = kc * jnp.exp(gc[..., -1:] - gc)[..., None]
    chunk_decay = jnp.exp(gc[..., -1])

    def step(state, inp):
        u_n, w_n, q_n, k_n, a_n, d_n = inp
        v_new = u_n - jnp.einsum('bhcd,bhde->bhce', w_n, state)
        o = jnp.einsum('bhcd,bhde->bhce', q_n, state) + jnp.einsum('bhij,bhje->bhie', a_n, v_new)
        state = state * d_n[..., None, None] + jnp.einsum('bhcd,bhce->bhde', k_n, v_new)
        return state, o

    xs = tuple(jnp.moveaxis(t, 1, 0) for t in (u, w, q_dec, k_dec, attn_intra, chunk_decay))
    state0 = jnp.zeros((b, h, dk, dv), jnp.float32)
    _, o = lax.scan(step, state0, xs)
    o = jnp.swapaxes(jnp.moveaxis(o, 0, 1), 2, 3)
    return o.reshape(b, s, h, dv)

def deltanet_mixer(q, k, v, z, beta_in, a_in, conv_w, a_log, dt_bias, norm_w):
    bsz, s, _ = q.shape
    qkv = jax.nn.silu(centred_depthwise_conv(jnp.concatenate([q, k, v], axis=-1), conv_w))
    qkv = qkv.astype(jnp.float32)
    q, k, v = jnp.split(qkv, 3, axis=-1)
    q = l2norm(q.reshape(bsz, s, DN_HEADS, DN_HEAD_DIM)) * (DN_HEAD_DIM ** -0.5)
    k = l2norm(k.reshape(bsz, s, DN_HEADS, DN_HEAD_DIM))
    v = v.reshape(bsz, s, DN_HEADS, DN_HEAD_DIM)
    beta = jax.nn.sigmoid(beta_in.astype(jnp.float32)).reshape(bsz, s, 2, DN_HEADS)
    a = a_in.astype(jnp.float32).reshape(bsz, s, 2, DN_HEADS)
    g = -jnp.exp(a_log.astype(jnp.float32)) * jax.nn.softplus(a + dt_bias.astype(jnp.float32))
    o_fwd = gated_delta_chunked(q, k, v, g[:, :, 0], beta[:, :, 0])
    flip = lambda t: jnp.flip(t, axis=1)
    o_bwd = flip(gated_delta_chunked(flip(q), flip(k), flip(v), flip(g[:, :, 1]), flip(beta[:, :, 1])))
    o = o_fwd + o_bwd
    o = o * lax.rsqrt(jnp.mean(o * o, axis=-1, keepdims=True) + EPS) * norm_w.astype(jnp.float32)
    o = o * jax.nn.silu(z.astype(jnp.float32).reshape(bsz, s, DN_HEADS, DN_HEAD_DIM))
    return o.reshape(bsz, s, DN_WIDTH).astype(q_dtype_of(z))

def q_dtype_of(t):
    return t.dtype

def partial_rotary(x):
    s = x.shape[1]
    pos = jnp.arange(s, dtype=jnp.float32)
    inv_freq = ROPE_THETA ** (-jnp.arange(0, ROT_DIM, 2, dtype=jnp.float32) / ROT_DIM)
    ang = pos[:, None] * inv_freq[None, :]
    cos = jnp.cos(ang)[None, :, None, :]
    sin = jnp.sin(ang)[None, :, None, :]
    x32 = x.astype(jnp.float32)
    half = ROT_DIM // 2
    x1, x2, rest = x32[..., :half], x32[..., half:ROT_DIM], x32[..., ROT_DIM:]
    out = jnp.concatenate([x1 * cos - x2 * sin, x2 * cos + x1 * sin, rest], axis=-1)
    return out.astype(x.dtype)

def window_gqa_sink(q, k, v, sink):
    bsz, s, _, d = q.shape
    nb = s // ATTN_BLOCK
    qb = q.reshape(bsz, nb, ATTN_BLOCK, ATTN_KV_HEADS, ATTN_GROUP, d)

    def band(t):
        tp = jnp.pad(t, ((0, 0), (ATTN_BLOCK, ATTN_BLOCK), (0, 0), (0, 0)))
        tr = tp.reshape(bsz, nb + 2, ATTN_BLOCK, ATTN_KV_HEADS, d)
        return jnp.concatenate([tr[:, :-2], tr[:, 1:-1], tr[:, 2:]], axis=2)

    kb, vb = band(k), band(v)
    scores = jnp.einsum('bnqkgd,bnjkd->bnkgqj', qb, kb).astype(jnp.float32) * (d ** -0.5)
    blk = jnp.arange(nb)[:, None]
    qpos = blk * ATTN_BLOCK + jnp.arange(ATTN_BLOCK)[None, :]
    kpos = (blk - 1) * ATTN_BLOCK + jnp.arange(3 * ATTN_BLOCK)[None, :]
    mask = ((jnp.abs(qpos[:, :, None] - kpos[:, None, :]) <= WINDOW)
            & (kpos[:, None, :] >= 0) & (kpos[:, None, :] < s))
    scores = jnp.where(mask[None, :, None, None], scores, -jnp.inf)
    sk = sink.astype(jnp.float32).reshape(ATTN_KV_HEADS, ATTN_GROUP)[None, None, :, :, None, None]
    m = jnp.maximum(jnp.max(scores, axis=-1, keepdims=True), sk)
    p = jnp.exp(scores - m)
    probs = p / (jnp.sum(p, axis=-1, keepdims=True) + jnp.exp(sk - m))
    o = jnp.einsum('bnkgqj,bnjkd->bnqkgd', probs.astype(v.dtype), vb)
    return o.reshape(bsz, s, ATTN_Q_HEADS * d)

def hierarchical_moe(h, w_group, b_group, w_expert, b_expert, w_gate_up, w_down):
    bsz, s, d = h.shape
    t = bsz * s
    ht = h.reshape(t, d)
    glog = (ht @ w_group).astype(jnp.float32) + b_group.astype(jnp.float32)
    p_g, g_idx = lax.top_k(jax.nn.softmax(glog, axis=-1), 1)
    elog = ((ht @ w_expert).astype(jnp.float32) + b_expert.astype(jnp.float32))
    elog = elog.reshape(t, N_GROUPS, EXPERTS_PER_GROUP)[jnp.arange(t), g_idx[:, 0]]
    p_e, e_local = lax.top_k(jax.nn.softmax(elog, axis=-1), TOP_K)
    p_e = p_e / jnp.sum(p_e, axis=-1, keepdims=True)
    gate = (p_g * p_e).reshape(-1)
    expert_ids = (g_idx * EXPERTS_PER_GROUP + e_local).reshape(-1)
    order = jnp.argsort(expert_ids)
    token_of = order // TOP_K
    sizes = jax.ops.segment_sum(jnp.ones_like(expert_ids), expert_ids,
                                num_segments=N_EXPERTS).astype(jnp.int32)
    xs = ht[token_of]
    gu = lax.ragged_dot(xs, w_gate_up, sizes)
    g_part, u_part = jnp.split(gu, 2, axis=-1)
    y = lax.ragged_dot(jax.nn.silu(g_part) * u_part, w_down, sizes)
    y = y.astype(jnp.float32) * gate[order][:, None]
    out = jax.ops.segment_sum(y, token_of, num_segments=t)
    return out.reshape(bsz, s, d).astype(h.dtype)

def hybrid_layer(x, ln_mix, w_in, dn_conv, dn_A_log, dn_dt_bias, dn_norm, attn_sink, w_out,
                 ln_ffn, w_group, b_group, w_expert, b_expert, w_gate_up, w_down):
    bsz, s, _ = x.shape
    h = rmsnorm(x, ln_mix)
    proj = h @ w_in
    dq, dk_, dv_, dz, dbeta, da, aq, ak, av = jnp.split(proj, IN_OFFSETS, axis=-1)
    out_a = deltanet_mixer(dq, dk_, dv_, dz, dbeta, da, dn_conv, dn_A_log, dn_dt_bias, dn_norm)
    aq = partial_rotary(aq.reshape(bsz, s, ATTN_Q_HEADS, ATTN_HEAD_DIM))
    ak = partial_rotary(ak.reshape(bsz, s, ATTN_KV_HEADS, ATTN_HEAD_DIM))
    av = av.reshape(bsz, s, ATTN_KV_HEADS, ATTN_HEAD_DIM)
    out_b = window_gqa_sink(aq, ak, av, attn_sink)
    x = x + jnp.concatenate([out_a.astype(x.dtype), out_b.astype(x.dtype)], axis=-1) @ w_out
    x = x + hierarchical_moe(rmsnorm(x, ln_ffn), w_group, b_group, w_expert, b_expert, w_gate_up, w_down)
    return x

def setup_inputs(seed: int = 0) -> dict:
    key = jax.random.key(seed)
    ks = jax.random.split(key, 20)
    f32 = jnp.float32
    nrm = lambda k, shape, scale: jax.random.normal(k, shape, f32) * scale
    dt = jnp.exp(jax.random.uniform(ks[5], (DEPTH, 2, DN_HEADS), f32, np.log(1e-3), np.log(1e-1)))
    return {
        'x': nrm(ks[0], (BATCH, SEQ, D_MODEL), 1.0),
        'ln_mix': 1.0 + nrm(ks[1], (DEPTH, D_MODEL), 0.02),
        'w_in': nrm(ks[2], (DEPTH, D_MODEL, IN_WIDTH), D_MODEL ** -0.5),
        'dn_conv': nrm(ks[3], (DEPTH, CONV_WIDTH, 3 * DN_WIDTH), CONV_WIDTH ** -0.5),
        'dn_A_log': jnp.log(jax.random.uniform(ks[4], (DEPTH, 2, DN_HEADS), f32, 1.0, 16.0)),
        'dn_dt_bias': dt + jnp.log(-jnp.expm1(-dt)),
        'dn_norm': 1.0 + nrm(ks[6], (DEPTH, DN_HEAD_DIM), 0.02),
        'attn_sink': nrm(ks[7], (DEPTH, ATTN_Q_HEADS), 0.5),
        'w_out': nrm(ks[8], (DEPTH, MIX_WIDTH, D_MODEL), MIX_WIDTH ** -0.5),
        'ln_ffn': 1.0 + nrm(ks[9], (DEPTH, D_MODEL), 0.02),
        'w_group': nrm(ks[10], (DEPTH, D_MODEL, N_GROUPS), D_MODEL ** -0.5),
        'b_group': nrm(ks[11], (DEPTH, N_GROUPS), 0.01),
        'w_expert': nrm(ks[12], (DEPTH, D_MODEL, N_EXPERTS), D_MODEL ** -0.5),
        'b_expert': nrm(ks[13], (DEPTH, N_EXPERTS), 0.01),
        'w_gate_up': nrm(ks[14], (DEPTH, N_EXPERTS, D_MODEL, 2 * EXPERT_FF), D_MODEL ** -0.5),
        'w_down': nrm(ks[15], (DEPTH, N_EXPERTS, EXPERT_FF, D_MODEL), EXPERT_FF ** -0.5),
        'ln_final': 1.0 + nrm(ks[16], (D_MODEL,), 0.02),
    }

def reference(x, ln_mix, w_in, dn_conv, dn_A_log, dn_dt_bias, dn_norm, attn_sink, w_out,
              ln_ffn, w_group, b_group, w_expert, b_expert, w_gate_up, w_down, ln_final):
    for l in range(DEPTH):
        x = hybrid_layer(x, ln_mix[l], w_in[l], dn_conv[l], dn_A_log[l], dn_dt_bias[l], dn_norm[l],
                         attn_sink[l], w_out[l], ln_ffn[l], w_group[l], b_group[l], w_expert[l],
                         b_expert[l], w_gate_up[l], w_down[l])
    return rmsnorm(x, ln_final)


_drawn_inputs = setup_inputs


def setup_inputs(seed=0):
    import zlib

    import numpy as np

    out = dict(_drawn_inputs(seed))
    spreads = {}
    factors = {'dn_norm': 3.463,
     'attn_sink': 64.0,
     'b_group': 17.44,
     'b_expert': 20.897,
     'ln_final': 8.171,
     'ln_ffn': 3.963}
    for name, (base, spread) in spreads.items():
        noise = np.random.default_rng([zlib.crc32(name.encode()), seed]).standard_normal(out[name].shape)
        drawn = base * np.exp(spread * noise) if base else spread * noise
        out[name] = __import__('jax').numpy.asarray(drawn.astype(out[name].dtype))
    for name, factor in factors.items():
        out[name] = (out[name] * factor).astype(out[name].dtype)
    return out
```

```python
from contextlib import ExitStack

import numpy as np

import concourse.bass as bass
from concourse import mybir

F32 = mybir.dt.float32
I32 = mybir.dt.int32
ALU = mybir.AluOpType
ACT = mybir.ActivationFunctionType
AX = mybir.AxisListType

P = 128
S = 2048
D = 1024
KD = D // P
NT = S // P
EPS = 1e-6

HEADS = 4
DH = 128
DN = HEADS * DH
TAPS = 5
QH = 8
KVH = 2
AD = 64
ROT = AD // 4
HALF = ROT // 2
THETA = 500000.0
WINDOW = 128

QKV = 3 * DN
TOKW = DN + 16 + QH * AD + 2 * KVH * AD
Z0, BA0, Q0 = 0, DN, DN + 16
K0 = Q0 + QH * AD
V0 = K0 + KVH * AD
GROUPS = 3
GW = TOKW // GROUPS

NG = 8
NE = 64
FF = 256
CAP = S
LISTS = NE * CAP
NOWHERE = 1 << 20
BIG = 1.0e30
LEVELS = (2, 3, 4, 5, 6, 7)
TILE = P
MORE = 2 * S // TILE - 1
NR = (S - 1) // TILE


def done(t, k=1, per=1):
    return per * (t + 2) + k


def landed(uses):
    return 16 * (uses + 1)



def tables():
    r = np.arange(P)
    row, col = r[:, None], r[None, :]
    square = {
        "eye": row == col, "le": row <= col, "ge": row >= col, "lt": row < col, "gt": row > col,
        "ones": row >= 0 * col,
    }
    for level in (1,) + LEVELS:
        half = 1 << (level - 1)
        same = row // (2 * half) == col // (2 * half)
        low = same & (row // half % 2 == 1) & (col // half % 2 == 0)
        square[f"low{level}"] = low
        square[f"up{level}"] = low.T
    names = list(square)
    tab = np.concatenate([np.broadcast_to(square[n], (P, P)).astype(np.float32) for n in names], 1)
    freq = np.float32(THETA) ** (-np.arange(0, ROT, 2, dtype=np.float32) / ROT)
    ang = np.arange(S, dtype=np.float32)[:, None] * freq[None, :].astype(np.float32)
    trig = np.concatenate([np.cos(ang), np.sin(ang)], 1).astype(np.float32)
    kpos = np.arange(3 * P)[None, :] - P
    qpos = r[:, None]
    band = np.zeros((NT, P, 3 * P), np.float32)
    for n in range(NT):
        bad = (abs(qpos - kpos) > WINDOW) | (kpos + n * P < 0) | (kpos + n * P >= S)
        band[n] = np.where(bad, -BIG, 0.0)
    count = np.concatenate([np.arange(NG, 0, -1), np.arange(NE, 0, -1), np.arange(NE), 
                            np.arange(1, NR + 1) * TILE]).astype(np.float32)
    count = np.broadcast_to(count[None], (P, count.size)).copy()
    token = (np.arange(NT)[None, :] * P + r[:, None]).astype(np.float32)
    token = np.concatenate([token, r[:, None].astype(np.float32)], 1)
    return names, {"tab": tab, "trig": trig, "band": band, "count": count, "token": token}


NAMES, TABLES = tables()


def program(nc, io, out):
    top = ExitStack()
    with top:
        named = []

        def sem(name):
            named.append(nc.alloc_semaphore(name=name))
            return named[-1]

        def recycle():
            nc.clear_and_free_semaphores(named)
            named.clear()
            nc.all_engine_barrier()

        dram = lambda name, shape, dt=F32: nc.dram_tensor(name, shape, dt).ap()
        scr = {
            "tok": dram("s_tok", (S, TOKW)),
            "ch": dram("s_ch", (NT, P, 2, HEADS, DH)),
            "kv": dram("s_kv", (NT, P, 2, HEADS, DH)),
            "o": dram("s_o", (2, S, DN)),
            "attn": dram("s_attn", (S, QH * AD)),
            "x1": dram("s_x1", (S, D)),
            "h2": dram("s_h2", (S, D)),
            "list": dram("s_list", (LISTS + P, 4), I32),
            "items": dram("s_items", (P, 2), I32),
            "y": dram("s_y", (2 * S, D)),
        }
        ps = top.enter_context(nc.psum_tensor("ps", [P, 8, 512], F32))
        with ExitStack() as keep:
            h_all = keep.enter_context(nc.sbuf_tensor("h_all", [P, KD, S], F32))
            project_tokens(nc, io, scr, ps, sem, h_all)
            project_channels(nc, io, scr, ps, sem, h_all)
        delta_net(nc, io, scr, ps, sem)
        recycle()
        attention(nc, io, scr, ps, sem)
        with ExitStack() as keep:
            n_more = keep.enter_context(nc.sbuf_tensor("n_more", [1, 1], I32))
            mix_and_route(nc, io, scr, ps, sem, n_more)
            experts(nc, io, scr, ps, sem, n_more)
        finish(nc, io, scr, ps, sem, out)




def load_tab(nc, keep, names, prefix):
    t = keep.enter_context(nc.sbuf_tensor(prefix + "_tab", [P, len(names), P], F32))
    return t, {n: t[:, i, :] for i, n in enumerate(names)}


def issue_tab(eng, io, t, names, semaphore):
    for i, n in enumerate(names):
        j = NAMES.index(n)
        eng.dma_start(t[:, i, :], io["tab"][:, j * P:(j + 1) * P]).then_inc(semaphore, 16)
    return 16 * len(names)



def project_tokens(nc, io, scr, ps, sem, h_all):
    with ExitStack() as keep:
        sb = lambda n, s, dt=F32: keep.enter_context(nc.sbuf_tensor(n, s, dt))
        w = sb("a_w", [P, KD, TOKW])
        ln = sb("a_ln", [P, KD])
        eye = sb("a_eye", [P, P])
        x = sb("a_x", [P, 2, D])
        sq = sb("a_sq", [P, D])
        ss = sb("a_ss", [P, 2, 1])
        ms = sb("a_ms", [P, 2, 1])
        rstd = sb("a_rstd", [P, 2, 1])
        xn = sb("a_xn", [P, 2, D])
        hT = sb("a_hT", [P, 2, KD, P])
        o = sb("a_o", [P, 2, TOKW])
        fill = sb("a_fill", [P, P + 1, 2, 4], I32)
        power = sb("a_power", [P, 1])

        consts = sem("a_consts")
        x_in = [sem("a_x_in0"), sem("a_x_in1")]
        squared, mean, rooted, normed = sem("a_squared"), sem("a_mean"), sem("a_rooted"), sem("a_normed")
        turned, hT_act, hT_dve, kept = sem("a_turned"), sem("a_hT_act"), sem("a_hT_dve"), sem("a_kept")
        product, out_act, out_dve = sem("a_product"), sem("a_out_act"), sem("a_out_dve")
        stored = [sem("a_stored0"), sem("a_stored1")]
        blank, filled = sem("a_blank"), sem("a_filled")
        turn = [ps[:, b, :].rearrange("p (k t) -> p k t", k=4) for b in (0, 1)]

        def each(eng, step):
            with eng.Fori(0, NT // 2) as i:
                for p in range(2):
                    step(i, p, 2 * i + p)

        with nc.Block() as block:

            @block.sync
            def _(sp):
                sp.dma_start(ln[:], io["ln_mix"][0].rearrange("(k p) -> p k", p=P), allow_slow_non_contiguous=True).then_inc(consts, 16)
                j = NAMES.index("eye")
                sp.dma_start(eye[:], io["tab"][:, j * P:(j + 1) * P]).then_inc(consts, 16)
                for k in range(KD):
                    sp.dma_start(w[:, k, :], io["w_in"][0, k * P:(k + 1) * P, QKV:]).then_inc(consts, 16)

                def step(i, p, t):
                    row = sp.snap(t * P)
                    sp.wait_ge(squared, done(t - 2))
                    sp.wait_ge(normed, done(t - 2))
                    sp.dma_start(x[:, p, :], io["x"][0, bass.ds(row, P), :]).then_inc(x_in[p], 16)
                each(sp, step)
                sp.wait_ge(blank, 2)
                for e in range(8):
                    rows = LISTS // 8
                    sp.dma_start(scr["list"][e * rows:(e + 1) * rows, :].rearrange("(p r) c -> p r c", p=P),
                                 fill[:, 0:P, 0, :]).then_inc(filled, 16)
                sp.dma_start(scr["list"][LISTS:, :], fill[:, P, 0, :]).then_inc(filled, 16)
                sp.wait_ge(filled, 16 * 9)

            @block.gpsimd
            def _(pool):
                pool.memset(power[:], -0.5)
                pool.memset(fill[:], 0).then_inc(blank, 1)
                pool.wait_ge(blank, 1)
                pool.memset(fill[:, :, :, 0:2], NOWHERE).then_inc(blank, 1)
                pool.wait_ge(blank, 2)
                for s in (rooted, kept):
                    pool.sem_inc(s, 2)

                def step(i, p, t):
                    pool.wait_ge(mean, done(t))
                    pool.wait_ge(normed, done(t - 2))
                    pool.tensor_tensor(rstd[:, p, :], ms[:, p, :], power[:], ALU.pow).then_inc(rooted, 1)
                    pool.wait_ge(hT_act, done(t))
                    pool.wait_ge(hT_dve, done(t))
                    pool.tensor_copy(h_all[:, :, bass.ds(t * P, P)], hT[:, p, :, :]).then_inc(kept, 1)
                each(pool, step)

            @block.scalar
            def _(act):
                for s in (squared, hT_act):
                    act.sem_inc(s, 2)
                act.sem_inc(out_act, 4)
                for p in range(2):
                    act.sem_inc(stored[p], 16)
                act.wait_ge(consts, 16 * (2 + KD))

                def step(i, p, t):
                    act.wait_ge(x_in[p], 16 * (i + 1))
                    act.wait_ge(squared, done(t - 1))
                    act.wait_ge(mean, done(t - 2))
                    act.activation(sq[:], x[:, p, :], ACT.Square, accum_out=ss[:, p, :]).then_inc(squared, 1)
                    act.wait_ge(turned, done(t, 1, 2))
                    act.wait_ge(product, done(t - 2, 3, 3))
                    act.wait_ge(kept, done(t - 2))
                    for k in range(4):
                        last = act.mul(hT[:, p, k, :], turn[0][:, k, :], ln[:, k:k + 1])
                    last.then_inc(hT_act, 1)
                    act.wait_ge(stored[p], landed(i))
                    for g in range(2):
                        act.wait_ge(product, done(t, g + 1, 3))
                        act.copy(o[:, p, g * GW:(g + 1) * GW], ps[:, 2 + 3 * p + g, 0:GW]).then_inc(out_act, 1)
                    act.wait_ge(out_act, done(t, 2, 2))
                    act.wait_ge(out_dve, done(t))
                    act.dma_start(scr["tok"][bass.ds(t * P, P), :], o[:, p, :]).then_inc(stored[p], 16)
                each(act, step)
                for p in range(2):
                    act.wait_ge(stored[p], landed(NT // 2))

            @block.vector
            def _(dve):
                for s in (mean, normed, hT_dve, out_dve):
                    dve.sem_inc(s, 2)
                dve.wait_ge(consts, 16 * (2 + KD))

                def step(i, p, t):
                    dve.wait_ge(squared, done(t))
                    dve.wait_ge(rooted, done(t - 2))
                    dve.tensor_scalar(ms[:, p, :], ss[:, p, :], 1.0 / D, EPS, ALU.mult, ALU.add).then_inc(mean, 1)
                    dve.wait_ge(x_in[p], 16 * (i + 1))
                    dve.wait_ge(rooted, done(t))
                    dve.wait_ge(turned, done(t - 2, 2, 2))
                    dve.tensor_scalar(xn[:, p, :], x[:, p, :], rstd[:, p, :], None, ALU.mult).then_inc(normed, 1)
                    dve.wait_ge(turned, done(t, 2, 2))
                    dve.wait_ge(product, done(t - 2, 3, 3))
                    dve.wait_ge(kept, done(t - 2))
                    for k in range(4):
                        last = dve.tensor_scalar(hT[:, p, 4 + k, :], turn[1][:, k, :], ln[:, 4 + k:5 + k], None, ALU.mult)
                    last.then_inc(hT_dve, 1)
                    dve.wait_ge(stored[p], landed(i))
                    dve.wait_ge(product, done(t, 3, 3))
                    dve.tensor_copy(o[:, p, 2 * GW:], ps[:, 2 + 3 * p + 2, 0:GW]).then_inc(out_dve, 1)
                each(dve, step)

            @block.tensor
            def _(pe):
                pe.sem_inc(turned, 4)
                pe.sem_inc(product, 6)
                pe.wait_ge(consts, 16 * (2 + KD))

                def step(i, p, t):
                    pe.wait_ge(normed, done(t))
                    for half, evacuated in ((0, hT_act), (1, hT_dve)):
                        pe.wait_ge(evacuated, done(t - 1))
                        for k in range(4):
                            kk = 4 * half + k
                            last = pe.transpose(turn[half][:, k, :], xn[:, p, kk * P:(kk + 1) * P], eye[:])
                        last.then_inc(turned, 1)
                    pe.wait_ge(hT_act, done(t))
                    pe.wait_ge(hT_dve, done(t))
                    pe.wait_ge(out_act, done(t - 2, 2, 2))
                    pe.wait_ge(out_dve, done(t - 2))
                    for g in range(GROUPS):
                        for k in range(KD):
                            last = pe.matmul(ps[:, 2 + 3 * p + g, 0:GW], hT[:, p, k, :], w[:, k, g * GW:(g + 1) * GW],
                                             start=(k == 0), stop=(k == KD - 1))
                        last.then_inc(product, 1)
                each(pe, step)



def project_channels(nc, io, scr, ps, sem, h_all):
    with ExitStack() as keep:
        sb = lambda n, s, dt=F32: keep.enter_context(nc.sbuf_tensor(n, s, dt))
        w = sb("b_w", [P, 3, KD, P])
        taps_in = sb("b_taps_in", [TAPS, QKV])
        taps = sb("b_taps", [P, 3 * HEADS, TAPS])
        eye = sb("b_eye", [P, P])
        raw = sb("b_raw", [P, 3, S + 4])
        act_x = sb("b_act", [P, 3, S])
        tok = sb("b_tok", [P, 3, NT, P])
        sq = sb("b_sq", [P, NT, P])
        ch = sb("b_ch", [P, S])
        ssum = sb("b_ssum", [P, NT])
        ms = sb("b_ms", [P, NT])
        rs = sb("b_rs", [P, NT])
        power = sb("b_power", [P, NT])

        consts, padded, taps_up, taps_out = sem("b_consts"), sem("b_padded"), sem("b_taps_up"), sem("b_taps_out")
        w_in = [sem(f"b_w_in{y}") for y in range(3)]
        product, emptied = sem("b_product"), sem("b_emptied")
        conved, silued = sem("b_conved"), sem("b_silued")
        turned, tok_out = sem("b_turned"), sem("b_tok_out")
        squared, summed, rooted, scaled = sem("b_squared"), sem("b_summed"), sem("b_rooted"), sem("b_scaled")
        back, ch_out = sem("b_back"), sem("b_ch_out")
        tok_stored, ch_stored = [sem(f"b_tok_stored{y}") for y in range(3)], sem("b_ch_stored")
        chain, passed = sem("b_conv_taps"), sem("b_passed")
        QT, KT_, VT = range(3)
        qb = lambda b: ps[:, 4 + b, :].rearrange("p (c t) -> p c t", c=4)

        def each(eng, slot):
            slot((QT, 0), None)
            with eng.Fori(0, HEADS - 1) as h:
                slot((KT_, h), (QT, h))
                slot((VT, h), (KT_, h))
                slot((QT, h + 1), (VT, h))
            last = HEADS - 1
            slot((KT_, last), (QT, last))
            slot((VT, last), (KT_, last))
            slot(None, (VT, last))

        num = lambda item: 3 * item[1] + item[0]

        with nc.Block() as block:

            @block.sync
            def _(sp):
                sp.dma_start(taps_in[:], io["dn_conv"][0]).then_inc(consts, 16)
                j = NAMES.index("eye")
                sp.dma_start(eye[:], io["tab"][:, j * P:(j + 1) * P]).then_inc(consts, 16)
                def load(y, column):
                    src = io["w_in"][0, :, y * DN:(y + 1) * DN].rearrange("(k p) n -> p k n", p=P)
                    sp.dma_start(w[:, y, :, :], src[:, :, bass.ds(column, P)]).then_inc(w_in[y], 16)

                def slot(cur, old):
                    if old is None:
                        return
                    y, h = old
                    n = num(old)
                    m = 2 * h + y
                    if not (isinstance(h, int) and h == HEADS - 1):
                        column = sp.snap((h + 1) * P)
                        sp.wait_ge(product, done(n, 4, 4))
                        load(y, column)
                    head, tok_is_out, tok_is_scaled = [
                        v if isinstance(v, int) else sp.snap(v) for v in (h, done(n, 4, 4), done(m))]
                    if y != QT:
                        sp.wait_ge(tok_out, tok_is_out)
                        sp.sem_inc(passed, 1)
                        if y == KT_:
                            sp.wait_ge(scaled, tok_is_scaled)
                        sp.sem_inc(passed, 1)
                        sp.dma_start(scr["kv"][:, :, y - 1, bass.ds(head, 1), :].rearrange("c p o d -> p c (o d)"),
                                     tok[:, y]).then_inc(tok_stored[y], 16)
                    if y != VT:
                        sp.wait_ge(ch_out, done(m, 4, 4))
                        sp.dma_start(scr["ch"][:, :, 1 - y, bass.ds(head, 1), :].rearrange("c p o d -> p c (o d)"),
                                     ch[:].rearrange("p (c d) -> p c d", c=NT)).then_inc(ch_stored, 16)

                for s in (tok_stored[KT_], tok_stored[VT], ch_stored):
                    sp.sem_inc(s, 16)
                for y in range(3):
                    load(y, 0)
                each(sp, slot)
                for y in (KT_, VT):
                    sp.wait_ge(tok_stored[y], landed(HEADS))
                sp.wait_ge(ch_stored, landed(2 * HEADS))

            @block.gpsimd
            def _(pool):
                pool.memset(power[:], -0.5)
                pool.memset(raw[:, :, 0:2], 0.0)
                pool.memset(raw[:, :, S + 2:S + 4], 0.0).then_inc(padded, 1)
                pool.wait_ge(padded, 1)
                for s in (squared, scaled):
                    pool.sem_inc(s, 2)
                pool.sem_inc(rooted, 2)

                def slot(cur, old):
                    if old is None:
                        return
                    y, h = old
                    n = num(old)
                    m = 2 * h + y
                    pool.wait_ge(tok_out, done(n, 4, 4))
                    if y != VT:
                        pool.wait_ge(summed, done(m - 1, 2, 2))
                        pool.tensor_tensor(sq[:], tok[:, y], tok[:, y], ALU.mult).then_inc(squared, 1)
                        pool.wait_ge(summed, done(m, 2, 2))
                        pool.wait_ge(scaled, done(m - 1))
                        pool.tensor_tensor(rs[:], ms[:], power[:], ALU.pow).then_inc(rooted, 1)
                        pool.wait_ge(rooted, done(m))
                        pool.tensor_tensor(tok[:, y], tok[:, y], rs[:].unsqueeze(2).to_broadcast([P, NT, P]),
                                           ALU.mult).then_inc(scaled, 1)
                        pool.wait_ge(scaled, done(m))
                each(pool, slot)

            @block.scalar
            def _(act):
                act.sem_inc(silued, 2)
                act.sem_inc(emptied, 8)
                act.sem_inc(tok_out, 8)
                act.wait_ge(padded, 1)

                def slot(cur, old):
                    if cur is not None:
                        y, h = cur
                        n = num(cur)
                        for q in range(4):
                            act.wait_ge(product, done(n, q + 1, 4))
                            if q == 0:
                                act.wait_ge(conved, done(n - 2))
                            act.copy(raw[:, y, 2 + q * 512:2 + (q + 1) * 512], ps[:, q, :]).then_inc(emptied, 1)
                    if old is not None:
                        y, h = old
                        n = num(old)
                        m = 2 * h + y
                        for q in range(4):
                            act.wait_ge(turned, done(n, q + 1, 4))
                            if q == 0 and y != QT:
                                act.wait_ge(tok_stored[y], landed(h))
                            act.copy(tok[:, y, 4 * q:4 * q + 4, :], qb(q)).then_inc(tok_out, 1)
                    if cur is not None:
                        y, h = cur
                        n = num(cur)
                        act.wait_ge(conved, done(n))
                        act.activation(act_x[:, y], act_x[:, y], ACT.Silu).then_inc(silued, 1)
                each(act, slot)

            @block.vector
            def _(dve):
                dve.sem_inc(conved, 2)
                dve.sem_inc(summed, 4)
                dve.sem_inc(ch_out, 8)
                dve.wait_ge(taps_up, 1)
                dve.tensor_copy(taps[:], ps[:, 0, 0:3 * HEADS * 8].rearrange("p (b j) -> p b j", j=8)[:, :, 0:TAPS]).then_inc(taps_out, 1)
                dve.wait_ge(taps_out, 1)

                def slot(cur, old):
                    if cur is not None:
                        y, h = cur
                        n = num(cur)
                        dve.wait_ge(emptied, done(n, 4, 4))
                        dve.wait_ge(turned, done(n - 2, 4, 4))
                        b = y * HEADS + h
                        at = (lambda j: taps[:, b:b + 1, j]) if isinstance(b, int) else (lambda j: taps[:, bass.ds(b, 1), j])
                        dve.tensor_scalar(act_x[:, y], raw[:, y, 0:S], at(0), None, ALU.mult).then_inc(chain, 1)
                        for j in range(1, TAPS):
                            dve.wait_ge(chain, (TAPS - 1) * n + j)
                            dve.scalar_tensor_tensor(act_x[:, y], raw[:, y, j:j + S], at(j), act_x[:, y],
                                                     ALU.mult, ALU.add).then_inc(chain if j < TAPS - 1 else conved, 1)
                    if old is not None:
                        y, h = old
                        n = num(old)
                        m = 2 * h + y
                        if y != VT:
                            dve.wait_ge(squared, done(m))
                            dve.wait_ge(rooted, done(m - 1))
                            dve.tensor_reduce(ssum[:], sq[:], AX.X, ALU.add).then_inc(summed, 1)
                            dve.wait_ge(summed, done(m, 1, 2))
                            by = DH if y == QT else 1.0
                            dve.tensor_scalar(ms[:], ssum[:], by, by * EPS, ALU.mult, ALU.add).then_inc(summed, 1)
                    if old is not None:
                        y, h = old
                        n = num(old)
                        m = 2 * h + y
                        if y != VT:
                            dve.wait_ge(ch_stored, landed(2 * h + y))
                            for q in range(4):
                                dve.wait_ge(back, done(m, q + 1, 4))
                                dve.tensor_copy(ch[:, q * 512:(q + 1) * 512], ps[:, 4 + q, :]).then_inc(ch_out, 1)
                each(dve, slot)

            @block.tensor
            def _(pe):
                pe.sem_inc(product, 8)
                pe.sem_inc(turned, 8)
                pe.sem_inc(back, 8)
                pe.wait_ge(consts, 32)
                for b in range(3 * HEADS):
                    last = pe.transpose(ps[:, 0, 8 * b:8 * b + TAPS], taps_in[:, b * P:(b + 1) * P], eye[0:TAPS, 0:TAPS])
                last.then_inc(taps_up, 1)
                pe.wait_ge(taps_out, 1)

                def slot(cur, old):
                    if cur is not None:
                        y, h = cur
                        n = num(cur)
                        pe.wait_ge(w_in[y], 16 * (h + 1))
                        for q in range(4):
                            pe.wait_ge(emptied, done(n - 1, q + 1, 4))
                            for k in range(KD):
                                last = pe.matmul(ps[:, q, :], w[:, y, k, :], h_all[:, k, q * 512:(q + 1) * 512],
                                                 start=(k == 0), stop=(k == KD - 1))
                            last.then_inc(product, 1)
                    if old is not None:
                        y, h = old
                        n = num(old)
                        m = 2 * h + y
                        pe.wait_ge(silued, done(n))
                        for q in range(4):
                            if y != QT:
                                pe.wait_ge(ch_out, done(m - 1, q + 1, 4))
                            for c in range(4):
                                t = 4 * q + c
                                last = pe.transpose(qb(q)[:, c, :], act_x[:, y, t * P:(t + 1) * P], eye[:])
                            last.then_inc(turned, 1)
                        pe.wait_ge(tok_out, done(n, 4, 4))
                        if y != VT:
                            pe.wait_ge(scaled, done(m))
                            for q in range(4):
                                for c in range(4):
                                    last = pe.transpose(qb(q)[:, c, :], tok[:, y, 4 * q + c, :], eye[:])
                                last.then_inc(back, 1)
                each(pe, slot)



def delta_net(nc, io, scr, ps, sem):
    with ExitStack() as keep:
        sb = lambda n, s, dt=F32: keep.enter_context(nc.sbuf_tensor(n, s, dt))
        DIR = ((0, "low", "up", "gt", "le", "lt"), (1, "up", "low", "lt", "ge", "gt"))
        names = ["eye", "le", "ge", "lt", "gt", "ones"] + [f"{d}{l}" for d in ("low", "up") for l in (1,) + LEVELS]
        tab_t, tab = load_tab(nc, keep, names, "d")
        ba = sb("d_ba", [P, NT, 16])
        dtb = sb("d_dtb", [P, 2 * HEADS])
        alog = sb("d_alog", [P, 2 * HEADS])
        decay_rate = sb("d_rate", [P, 2 * HEADS])
        beta = sb("d_beta", [P, NT, 2 * HEADS])
        g = sb("d_g", [P, NT, 2 * HEADS])
        e1 = sb("d_e1", [P, NT, 16])
        e2 = sb("d_e2", [P, NT, 2 * HEADS])
        eg, ekd, dn, nb, neg = [[sb(f"d_{x}{d}", [P, NT, HEADS]) for d in range(2)] for x in ("eg", "ekd", "dn", "nb", "neg")]
        ch = sb("d_ch", [P, 2, 2, 2, HEADS, DH])
        kv = sb("d_kv", [P, 2, 2, 2, HEADS, DH])
        o = sb("d_o", [P, 2, 2, HEADS, DH])
        four = lambda x: [sb(f"d_{x}{d}", [P, HEADS, P]) for d in range(2)]
        gm, E, E1, E2, E3, NA, AT, XT, X, T, R, VN, QS, KD_, ST = [four(x) for x in (
            "gm", "ee", "e_incl", "e_strict", "e_beta", "na", "at", "xt", "x", "t", "r", "vn", "qs", "kd", "state")]
        pl = [[sb(f"d_p{d}_{l}", [P, HEADS, P]) for l in LEVELS] for d in range(2)]
        bank = lambda d, b: ps[:, 4 * d + b, :].rearrange("p (h t) -> p h t", h=HEADS)
        over = lambda m: m.unsqueeze(1).to_broadcast([P, HEADS, P])

        tabs_in, gates_in, step_done, sums_up = sem("d_tabs_in"), sem("d_gates_in"), sem("d_gate_steps"), sem("d_sums_up")
        gate_exp, set_up = sem("d_gate_exp"), sem("d_set_up")
        passed, passed_sp, passed_pool = sem("d_passed"), sem("d_passed_sp"), sem("d_passed_pool")
        ch_in = [[sem(f"d_ch_in{d}{p}") for p in range(2)] for d in range(2)]
        o_stored = [[sem(f"d_o_stored{d}{p}") for p in range(2)] for d in range(2)]

        PE_STEPS = ["gram", "decay", "turn"] + [f"{x}{l}" for l in LEVELS for x in ("P", "X")] + ["ks", "vn", "o", "su"]
        ACT_STEPS = ["exp", "X1"] + [f"X{l}" for l in LEVELS[:-1]]
        POOL_STEPS = ["gm", "incl", "strict", "beta", "eye", "kd"]
        DVE_STEPS = ["na", "at", "xt1"] + [f"{x}{l}" for l in LEVELS for x in ("P", "XT")] + ["r", "vn", "qs", "o", "s"]
        pe_did, act_did, pool_did, dve_did = [[sem(f"d_{e}_did{d}") for d in range(2)] for e in ("pe", "act", "pool", "dve")]

        def at(steps, name, t):
            return len(steps) * (t + 2) + steps.index(name) + 1

        pe_at = lambda name, t: at(PE_STEPS, name, t)
        act_at = lambda name, t: at(ACT_STEPS, name, t)
        pool_at = lambda name, t: at(POOL_STEPS, name, t)
        dve_at = lambda name, t: at(DVE_STEPS, name, t)

        def each(eng, step):
            with eng.Fori(0, NT // 2) as i:
                for p in range(2):
                    t = 2 * i + p
                    step(i, p, t, (t, NT - 1 - t))

        with nc.Block() as block:

            @block.sync
            def _(sp):
                n = issue_tab(sp, io, tab_t, names, tabs_in)
                sp.dma_start(ba[:], scr["tok"][:, BA0:BA0 + 16].rearrange("(c p) w -> p c w", p=P)).then_inc(gates_in, 16)
                sp.dma_start(dtb[:], io["dn_dt_bias"].rearrange("a d h -> a (d h)").to_broadcast([P, 2 * HEADS])).then_inc(gates_in, 16)
                sp.dma_start(alog[:], io["dn_A_log"].rearrange("a d h -> a (d h)").to_broadcast([P, 2 * HEADS])).then_inc(gates_in, 16)

                def step(i, p, t, chunk):
                    for d in range(2):
                        c, turned, decayed, summed = [sp.snap(v) for v in (
                            chunk[d], pe_at("o", t - 2), pool_at("kd", t - 2), dve_at("r", t - 2))]
                        sp.wait_ge(pe_did[d], turned)
                        sp.wait_ge(pool_did[d], decayed)
                        sp.wait_ge(dve_did[d], summed)
                        sp.sem_inc(passed_sp, 1)
                        sp.dma_start(ch[:, d, p], scr["ch"][bass.ds(c, 1)].rearrange("o p a h n -> (o p) a h n")).then_inc(ch_in[d][p], 16)
                        sp.dma_start(kv[:, d, p], scr["kv"][bass.ds(c, 1)].rearrange("o p a h n -> (o p) a h n")).then_inc(ch_in[d][p], 16)
                each(sp, step)

            @block.gpsimd
            def _(pool):
                for d in range(2):
                    pool.sem_inc(pool_did[d], 2 * len(POOL_STEPS))
                pool.wait_ge(tabs_in, 16 * len(names))
                for d in range(2):
                    pool.memset(ST[d][:], 0.0).then_inc(set_up, 1)
                    for pb in pl[d]:
                        pool.tensor_copy(pb[:], over(tab["eye"])).then_inc(set_up, 1)
                pool.wait_ge(step_done, 9)

                def step(i, p, t, chunk):
                    for d, low, up, gmask, cmask, smask in DIR:
                        c = chunk[d]
                        gates = lambda a: a[:, bass.ds(c, 1), :].rearrange("p o h -> p (o h)").unsqueeze(2).to_broadcast([P, HEADS, P])
                        pool.wait_ge(pe_did[d], pe_at("decay", t - 1))
                        pool.sem_inc(passed_pool, 1)
                        pool.tensor_tensor(gm[d][:], over(tab[gmask]), g[:, bass.ds(c, 1), d * HEADS:(d + 1) * HEADS].rearrange(
                            "p o h -> p (o h)").unsqueeze(2).to_broadcast([P, HEADS, P]), ALU.mult).then_inc(pool_did[d], 1)
                    for d, low, up, gmask, cmask, smask in DIR:
                        c = chunk[d]
                        gates = lambda a: a[:, bass.ds(c, 1), :].rearrange("p o h -> p (o h)").unsqueeze(2).to_broadcast([P, HEADS, P])
                        pool.wait_ge(act_did[d], act_at("exp", t))
                        pool.wait_ge(dve_did[d], dve_at("at", t - 1))
                        pool.tensor_tensor(E1[d][:], E[d][:], over(tab[cmask]), ALU.mult).then_inc(pool_did[d], 1)
                        pool.tensor_tensor(E2[d][:], E[d][:], over(tab[smask]), ALU.mult).then_inc(pool_did[d], 1)
                        pool.wait_ge(pool_did[d], pool_at("strict", t))
                        pool.wait_ge(dve_did[d], dve_at("na", t - 1))
                        pool.tensor_tensor(E3[d][:], E2[d][:], gates(nb[d]), ALU.mult).then_inc(pool_did[d], 1)
                        pool.wait_ge(pe_did[d], pe_at("X7", t - 1))
                        pool.sem_inc(passed_pool, 1)
                        pool.tensor_copy(XT[d][:], over(tab["eye"])).then_inc(pool_did[d], 1)
                        pool.wait_ge(ch_in[d][p], 32 * (i + 1))
                        pool.wait_ge(pe_did[d], pe_at("su", t - 1))
                        pool.tensor_tensor(KD_[d][:], kv[:, d, p, 0], gates(ekd[d]), ALU.mult).then_inc(pool_did[d], 1)
                each(pool, step)

            @block.scalar
            def _(act):
                for d in range(2):
                    act.sem_inc(act_did[d], 2 * len(ACT_STEPS))
                    for p in range(2):
                        act.sem_inc(o_stored[d][p], 16)
                act.wait_ge(gates_in, 48)
                act.activation(e1[:, :, 0:8], ba[:, :, 0:8], ACT.Exp, scale=-1.0)
                act.activation(decay_rate[:], alog[:], ACT.Exp).then_inc(gate_exp, 1)
                act.wait_ge(step_done, 2)
                act.activation(e1[:, :, 8:16], e2[:], ACT.Exp, scale=-1.0).then_inc(gate_exp, 1)
                act.wait_ge(gate_exp, 2)
                act.activation(e1[:, :, 8:16], e1[:, :, 8:16], ACT.Ln, bias=1.0).then_inc(gate_exp, 1)
                act.wait_ge(sums_up, 1)
                for d in range(2):
                    for n, dst in enumerate((eg, ekd, dn)):
                        act.activation(dst[d][:], ps[:, 0, (3 * d + n) * 64:(3 * d + n + 1) * 64].rearrange("p (c h) -> p c h", h=HEADS),
                                       ACT.Exp).then_inc(gate_exp, 1)

                def step(i, p, t, chunk):
                    for d in range(2):
                        act.wait_ge(pe_did[d], pe_at("decay", t))
                        act.wait_ge(pool_did[d], pool_at("strict", t - 1))
                        act.activation(E[d][:], bank(d, 2), ACT.Exp).then_inc(act_did[d], 1)
                    for d in range(2):
                        act.wait_ge(pe_did[d], pe_at("turn", t))
                        act.copy(X[d][:], bank(d, 3)).then_inc(act_did[d], 1)
                    for l in LEVELS[:-1]:
                        for d in range(2):
                            act.wait_ge(pe_did[d], pe_at(f"X{l}", t))
                            act.copy(X[d][:], bank(d, 1)).then_inc(act_did[d], 1)
                    for d in range(2):
                        act.wait_ge(dve_did[d], dve_at("o", t))
                        act.dma_start(scr["o"][d, bass.ds(chunk[d] * P, P), :], o[:, d, p].rearrange("p h n -> p (h n)")).then_inc(o_stored[d][p], 16)
                each(act, step)
                for d in range(2):
                    for p in range(2):
                        act.wait_ge(o_stored[d][p], landed(NT // 2))

            @block.vector
            def _(dve):
                for d in range(2):
                    dve.sem_inc(dve_did[d], 2 * len(DVE_STEPS))
                dve.wait_ge(gates_in, 48)
                a_in = ba[:, :, 8:16]
                across = lambda a: a.unsqueeze(1).to_broadcast([P, NT, 2 * HEADS])
                dve.tensor_tensor(g[:], a_in, across(dtb[:]), ALU.add).then_inc(step_done, 1)
                dve.wait_ge(step_done, 1)
                dve.scalar_tensor_tensor(e2[:], g[:], -1.0, g[:], ALU.mult, ALU.max).then_inc(step_done, 1)
                dve.wait_ge(step_done, 2)
                dve.tensor_scalar(g[:], g[:], 0.0, None, ALU.max).then_inc(step_done, 1)
                dve.wait_ge(gate_exp, 1)
                dve.tensor_scalar(beta[:], e1[:, :, 0:8], 1.0, None, ALU.add).then_inc(step_done, 1)
                dve.wait_ge(step_done, 4)
                dve.reciprocal(beta[:], beta[:]).then_inc(step_done, 1)
                dve.wait_ge(gate_exp, 3)
                dve.tensor_tensor(g[:], g[:], e1[:, :, 8:16], ALU.add).then_inc(step_done, 1)
                dve.wait_ge(step_done, 6)
                dve.scalar_tensor_tensor(g[:], g[:], -1.0, across(decay_rate[:]), ALU.mult, ALU.mult).then_inc(step_done, 1)
                for d in range(2):
                    dve.tensor_scalar(nb[d][:], beta[:, :, d * HEADS:(d + 1) * HEADS], -1.0, None, ALU.mult).then_inc(step_done, 1)
                dve.wait_ge(gate_exp, 9)
                dve.wait_ge(set_up, 2 * (1 + len(LEVELS)))
                for d in range(2):
                    dve.tensor_scalar(neg[d][:], eg[d][:], -1.0, None, ALU.mult).then_inc(step_done, 1)
                dve.wait_ge(step_done, 11)

                def step(i, p, t, chunk):
                    for d, low, up, gmask, cmask, smask in DIR:
                        dve.wait_ge(pe_did[d], pe_at("gram", t))
                        dve.wait_ge(pe_did[d], pe_at("P7", t - 1))
                        dve.wait_ge(pool_did[d], pool_at("beta", t))
                        dve.tensor_tensor(NA[d][:], bank(d, 0), E3[d][:], ALU.mult).then_inc(dve_did[d], 1)
                        dve.wait_ge(pe_did[d], pe_at("o", t - 1))
                        dve.tensor_tensor(AT[d][:], bank(d, 1), E1[d][:], ALU.mult).then_inc(dve_did[d], 1)
                        dve.wait_ge(dve_did[d], dve_at("na", t))
                        dve.wait_ge(pool_did[d], pool_at("eye", t))
                        dve.sem_inc(passed, 1)
                        dve.copy_predicated(XT[d][:], over(tab[up + "1"].bitcast(I32)), NA[d][:]).then_inc(dve_did[d], 1)
                    for n, l in enumerate(LEVELS):
                        for d, low, up, gmask, cmask, smask in DIR:
                            dve.wait_ge(pe_did[d], pe_at(f"P{l}", t))
                            dve.sem_inc(passed, 1)
                            dve.copy_predicated(pl[d][n][:], over(tab[f"{low}{l}"].bitcast(I32)), bank(d, 0)).then_inc(dve_did[d], 1)
                        for d in range(2):
                            dve.wait_ge(pe_did[d], pe_at(f"X{l}", t))
                            dst = XT[d] if l < LEVELS[-1] else T[d]
                            dve.tensor_copy(dst[:], bank(d, 2)).then_inc(dve_did[d], 1)
                    for d in range(2):
                        c = chunk[d]
                        dve.wait_ge(pe_did[d], pe_at("ks", t))
                        dve.wait_ge(dve_did[d], dve_at("s", t - 1))
                        dve.sem_inc(passed, 1)
                        for h in range(HEADS):
                            last = dve.scalar_tensor_tensor(R[d][:, h], bank(d, 3)[:, h], neg[d][:, bass.ds(c, 1), h], kv[:, d, p, 1, h],
                                                            ALU.mult, ALU.add)
                        last.then_inc(dve_did[d], 1)
                    for d in range(2):
                        c = chunk[d]
                        gates = lambda a: a.rearrange("p o h -> p (o h)").unsqueeze(2).to_broadcast([P, HEADS, P])
                        dve.wait_ge(pe_did[d], pe_at("vn", t))
                        dve.tensor_tensor(VN[d][:], bank(d, 1), gates(beta[:, bass.ds(c, 1), d * HEADS:(d + 1) * HEADS]),
                                          ALU.mult).then_inc(dve_did[d], 1)
                        dve.tensor_tensor(QS[d][:], bank(d, 0), gates(eg[d][:, bass.ds(c, 1), :]), ALU.mult).then_inc(dve_did[d], 1)
                    for d in range(2):
                        c = chunk[d]
                        dve.wait_ge(pe_did[d], pe_at("o", t))
                        dve.wait_ge(dve_did[d], dve_at("qs", t))
                        dve.wait_ge(o_stored[d][p], landed(i))
                        dve.tensor_tensor(o[:, d, p], QS[d][:], bank(d, 2), ALU.add).then_inc(dve_did[d], 1)
                        dve.wait_ge(pe_did[d], pe_at("su", t))
                        for h in range(HEADS):
                            last = dve.scalar_tensor_tensor(ST[d][:, h], ST[d][:, h], dn[d][:, bass.ds(c, 1), h], bank(d, 3)[:, h],
                                                            ALU.mult, ALU.add)
                        last.then_inc(dve_did[d], 1)
                each(dve, step)

            @block.tensor
            def _(pe):
                for d in range(2):
                    pe.sem_inc(pe_did[d], 2 * len(PE_STEPS))
                pe.wait_ge(tabs_in, 16 * len(names))
                pe.wait_ge(step_done, 9)
                for d, low, up, gmask, cmask, smask in DIR:
                    gd = g[:, :, d * HEADS:(d + 1) * HEADS]
                    for n, mask in enumerate((cmask, gmask, "ones")):
                        last = pe.matmul(ps[:, 0, (3 * d + n) * 64:(3 * d + n + 1) * 64], tab[mask], gd, start=True, stop=True)
                last.then_inc(sums_up, 1)
                pe.wait_ge(gate_exp, 9)
                pe.wait_ge(set_up, 2 * (1 + len(LEVELS)))

                def step(i, p, t, chunk):
                    mm = lambda out, a, b: pe.matmul(out, a, b, start=True, stop=True)
                    for d, low, up, gmask, cmask, smask in DIR:
                        pe.wait_ge(ch_in[d][p], 32 * (i + 1))
                        pe.wait_ge(dve_did[d], dve_at("qs", t - 1))
                        for h in range(HEADS):
                            mm(bank(d, 0)[:, h], ch[:, d, p, 0, h], ch[:, d, p, 0, h])
                            last = mm(bank(d, 1)[:, h], ch[:, d, p, 0, h], ch[:, d, p, 1, h])
                        last.then_inc(pe_did[d], 1)
                        pe.wait_ge(dve_did[d], dve_at("o", t - 1))
                        pe.wait_ge(pool_did[d], pool_at("gm", t))
                        for h in range(HEADS):
                            last = mm(bank(d, 2)[:, h], gm[d][:, h], tab[cmask])
                        last.then_inc(pe_did[d], 1)
                    for d in range(2):
                        pe.wait_ge(dve_did[d], dve_at("xt1", t))
                        for h in range(HEADS):
                            last = pe.transpose(bank(d, 3)[:, h], XT[d][:, h], tab["eye"])
                        last.then_inc(pe_did[d], 1)
                    for n, l in enumerate(LEVELS):
                        for d in range(2):
                            pe.wait_ge(act_did[d], act_at(f"X{l - 1}", t))
                            for h in range(HEADS):
                                last = mm(bank(d, 0)[:, h], NA[d][:, h], X[d][:, h])
                            last.then_inc(pe_did[d], 1)
                        for d in range(2):
                            pe.wait_ge(dve_did[d], dve_at(f"P{l}", t))
                            if l == LEVELS[0]:
                                pe.wait_ge(act_did[d], act_at("exp", t))
                            for h in range(HEADS):
                                if l < LEVELS[-1]:
                                    mm(bank(d, 1)[:, h], XT[d][:, h], pl[d][n][:, h])
                                last = mm(bank(d, 2)[:, h], pl[d][n][:, h], XT[d][:, h])
                            last.then_inc(pe_did[d], 1)
                    for d in range(2):
                        pe.wait_ge(dve_did[d], dve_at("s", t - 1))
                        pe.wait_ge(dve_did[d], dve_at("P7", t))
                        for h in range(HEADS):
                            mm(bank(d, 3)[:, h], ch[:, d, p, 0, h], ST[d][:, h])
                            last = mm(bank(d, 0)[:, h], ch[:, d, p, 1, h], ST[d][:, h])
                        last.then_inc(pe_did[d], 1)
                    for d in range(2):
                        pe.wait_ge(dve_did[d], dve_at("r", t))
                        for h in range(HEADS):
                            last = mm(bank(d, 1)[:, h], T[d][:, h], R[d][:, h])
                        last.then_inc(pe_did[d], 1)
                    for d in range(2):
                        pe.wait_ge(dve_did[d], dve_at("vn", t))
                        for h in range(HEADS):
                            last = mm(bank(d, 2)[:, h], AT[d][:, h], VN[d][:, h])
                        last.then_inc(pe_did[d], 1)
                        pe.wait_ge(pool_did[d], pool_at("kd", t))
                        for h in range(HEADS):
                            last = mm(bank(d, 3)[:, h], KD_[d][:, h], VN[d][:, h])
                        last.then_inc(pe_did[d], 1)
                each(pe, step)



def lagged(eng, slot):
    slot(0, 0, None)
    with eng.Fori(0, NT // 2 - 1) as i:
        slot(1, 2 * i + 1, 2 * i)
        slot(0, 2 * i + 2, 2 * i + 1)
    slot(1, NT - 1, NT - 2)
    slot(0, None, NT - 1)


def attention(nc, io, scr, ps, sem):
    with ExitStack() as keep:
        sb = lambda n, s, dt=F32: keep.enter_context(nc.sbuf_tensor(n, s, dt))
        HH = QH + KVH
        eye = sb("e_eye", [P, P])
        qk = sb("e_qk", [P, 2, HH, AD])
        trig = sb("e_trig", [P, 2, 2, HALF])
        rot = sb("e_rot", [P, 4, HH, HALF])
        qkT = sb("e_qkT", [AD, HH, NT + 2, P])
        v = sb("e_v", [P, NT + 2, KVH * AD])
        qT = sb("e_qT", [AD, 2, QH, P])
        band = sb("e_band", [P, 2, 3 * P])
        sink = sb("e_sink", [P, QH])
        sc = sb("e_sc", [P, QH, 3 * P])
        pr = sb("e_pr", [P, QH, 3 * P])
        pT = sb("e_pT", [P, QH, 3, P])
        m = sb("e_m", [P, QH])
        negm = sb("e_negm", [P, QH])
        ds = sb("e_ds", [P, QH])
        es = sb("e_es", [P, QH])
        sums = sb("e_sums", [P, QH])
        den = sb("e_den", [P, 2, QH])
        o = sb("e_o", [P, 2, QH, AD])

        consts, padded, passed = sem("e_consts"), sem("e_padded"), sem("e_passed")
        qk_in, band_in, stored = [[sem(f"e_{x}{p}") for p in range(2)] for x in ("qk_in", "band_in", "stored")]
        multiplied, rotated, turned, all_out = sem("e_multiplied"), sem("e_rotated"), sem("e_turned"), sem("e_all_out")
        q_copied, scored, masked = sem("e_q_copied"), sem("e_scored"), sem("e_masked")
        maxed, sunk, exped, denned = sem("e_maxed"), sem("e_sunk"), sem("e_exped"), sem("e_denned")
        p_turned, pT_act, pT_dve, mixed, o_out = [sem("e_" + x) for x in ("p_turned", "pT_act", "pT_dve", "mixed", "o_out")]

        def each(eng, step):
            with eng.Fori(0, NT // 2) as i:
                for p in range(2):
                    step(i, p, 2 * i + p)

        with nc.Block() as block:

            @block.sync
            def _(sp):
                j = NAMES.index("eye")
                sp.dma_start(eye[:], io["tab"][:, j * P:(j + 1) * P]).then_inc(consts, 16)
                sp.dma_start(sink[:], io["attn_sink"].to_broadcast([P, QH])).then_inc(consts, 16)
                sp.dma_start(v[:, 1:NT + 1, :], scr["tok"][:, V0:V0 + KVH * AD].rearrange("(c p) w -> p c w", p=P)).then_inc(consts, 16)

                def prepare(i, p, t):
                    row, free = sp.snap(t * P), sp.snap(done(t - 2))
                    sp.wait_ge(turned, free)
                    sp.dma_start(qk[:, p], scr["tok"][bass.ds(row, P), Q0:V0].rearrange("p (h d) -> p h d", d=AD)).then_inc(qk_in[p], 16)
                    sp.dma_start(trig[:, p], io["trig"][bass.ds(row, P), :].rearrange("p (a f) -> p a f", a=2)).then_inc(qk_in[p], 16)
                each(sp, prepare)

                def step(i, p, t):
                    row, free = sp.snap(t), sp.snap(done(t - 2, QH, QH))
                    sp.wait_ge(masked, free)
                    sp.dma_start(band[:, p], io["band"][bass.ds(row, 1)].rearrange("o p k -> (o p) k")).then_inc(band_in[p], 16)
                each(sp, step)

            @block.gpsimd
            def _(pool):
                pool.sem_inc(q_copied, 2)
                pool.memset(qkT[:, :, 0, :], 0.0)
                pool.memset(qkT[:, :, NT + 1, :], 0.0)
                pool.memset(v[:, 0, :], 0.0)
                pool.memset(v[:, NT + 1, :], 0.0).then_inc(padded, 1)
                pool.wait_ge(all_out, done(NT - 1))

                def step(i, p, t):
                    pool.wait_ge(scored, done(t - 2, QH, QH))
                    pool.tensor_copy(qT[:, p], qkT[:, 0:QH, bass.ds(t + 1, 1), :].rearrange("d h o t -> d h (o t)")).then_inc(q_copied, 1)
                each(pool, step)

            @block.scalar
            def _(act):
                for s, per in ((all_out, 1), (exped, QH + 1), (pT_act, 4)):
                    act.sem_inc(s, 2 * per)
                for p in range(2):
                    act.sem_inc(stored[p], 16)
                act.wait_ge(consts, 48)

                def prepare(i, p, t):
                    act.wait_ge(turned, done(t))
                    for b, (lo, hi) in enumerate(((0, 4), (4, 8), (8, HH))):
                        last = act.copy(qkT[:, lo:hi, bass.ds(t + 1, 1), :].rearrange("d h o t -> d h (o t)"),
                                        ps[0:AD, 4 * p + b, 0:(hi - lo) * P].rearrange("d (h t) -> d h t", t=P))
                    last.then_inc(all_out, 1)
                each(act, prepare)

                def slot(p, t, old):
                    if old is not None:
                        for n, h in enumerate(range(0, QH, 2)):
                            act.wait_ge(p_turned, done(old, h + 1, QH))
                            act.wait_ge(mixed, done(old - 1))
                            act.copy(pT[:, h], ps[:, 4, 0:3 * P].rearrange("k (j q) -> k j q", j=3)).then_inc(pT_act, 1)
                    if t is not None:
                        act.wait_ge(sunk, done(t, 2, 2))
                        act.activation(es[:], ds[:], ACT.Exp).then_inc(exped, 1)
                        act.wait_ge(p_turned, done(t - 1, QH, QH))
                        act.wait_ge(denned, done(t - 1, 2, 2))
                        for h in range(QH):
                            act.activation(pr[:, h], sc[:, h], ACT.Exp, bias=negm[:, h:h + 1], accum_out=sums[:, h:h + 1]).then_inc(exped, 1)
                    if old is not None:
                        q = 1 - p
                        act.wait_ge(o_out, done(old))
                        act.dma_start(scr["attn"][bass.ds(old * P, P), :], o[:, q].rearrange("p h d -> p (h d)")).then_inc(stored[q], 16)
                lagged(act, slot)
                for p in range(2):
                    act.wait_ge(stored[p], landed(NT // 2))

            @block.vector
            def _(dve):
                for s, per in ((rotated, 2), (multiplied, 1), (masked, QH), (maxed, 2), (sunk, 2), (denned, 2), (pT_dve, 4), (o_out, 1)):
                    dve.sem_inc(s, 2 * per)
                dve.wait_ge(consts, 48)

                def prepare(i, p, t):
                    dve.wait_ge(qk_in[p], 32 * (i + 1))
                    lo, hi = qk[:, p, :, 0:HALF], qk[:, p, :, HALF:ROT]
                    cos = trig[:, p, 0, :].unsqueeze(1).to_broadcast([P, HH, HALF])
                    sin = trig[:, p, 1, :].unsqueeze(1).to_broadcast([P, HH, HALF])
                    dve.wait_ge(rotated, done(t - 1, 2, 2))
                    for n, (a, b) in enumerate(((lo, cos), (hi, sin), (hi, cos), (lo, sin))):
                        last = dve.tensor_tensor(rot[:, n], a, b, ALU.mult)
                    last.then_inc(multiplied, 1)
                    dve.wait_ge(multiplied, done(t))
                    dve.tensor_tensor(lo, rot[:, 0], rot[:, 1], ALU.subtract).then_inc(rotated, 1)
                    dve.tensor_tensor(hi, rot[:, 2], rot[:, 3], ALU.add).then_inc(rotated, 1)
                each(dve, prepare)

                def slot(p, t, old):
                    if t is not None:
                        i = (t - p) // 2 if isinstance(t, int) else None
                        for h in range(QH):
                            dve.wait_ge(scored, done(t, h + 1, QH))
                            if h == 0:
                                dve.wait_ge(band_in[p], 8 * (t - p) + 16)
                                dve.wait_ge(exped, done(t - 1, QH + 1, QH + 1))
                            dve.scalar_tensor_tensor(sc[:, h], ps[:, h % 4, 0:3 * P], AD ** -0.5, band[:, p], ALU.mult, ALU.add).then_inc(masked, 1)
                    if old is not None:
                        for h in range(1, QH, 2):
                            dve.wait_ge(p_turned, done(old, h + 1, QH))
                            dve.wait_ge(mixed, done(old - 1))
                            dve.tensor_copy(pT[:, h], ps[:, 5, 0:3 * P].rearrange("k (j q) -> k j q", j=3)).then_inc(pT_dve, 1)
                    if t is not None:
                        dve.wait_ge(masked, done(t, QH, QH))
                        dve.tensor_reduce(m[:], sc[:], AX.X, ALU.max).then_inc(maxed, 1)
                        dve.wait_ge(maxed, done(t, 1, 2))
                        dve.tensor_tensor(m[:], m[:], sink[:], ALU.max).then_inc(maxed, 1)
                        dve.wait_ge(maxed, done(t, 2, 2))
                        dve.tensor_scalar(negm[:], m[:], -1.0, None, ALU.mult).then_inc(sunk, 1)
                        dve.tensor_tensor(ds[:], sink[:], m[:], ALU.subtract).then_inc(sunk, 1)
                    if old is not None:
                        q = 1 - p
                        dve.wait_ge(mixed, done(old))
                        dve.wait_ge(denned, done(old, 2, 2))
                        dve.wait_ge(stored[q], 8 * (old - q) + 16)
                        dve.tensor_tensor(o[:, q], ps[:, 6, :].rearrange("p (h d) -> p h d", d=AD),
                                          den[:, q, :].unsqueeze(2).to_broadcast([P, QH, AD]), ALU.mult).then_inc(o_out, 1)
                    if t is not None:
                        dve.wait_ge(exped, done(t, QH + 1, QH + 1))
                        dve.tensor_tensor(den[:, p], sums[:], es[:], ALU.add).then_inc(denned, 1)
                        dve.wait_ge(denned, done(t, 1, 2))
                        dve.reciprocal(den[:, p], den[:, p]).then_inc(denned, 1)
                lagged(dve, slot)

            @block.tensor
            def _(pe):
                for s, per in ((turned, 1), (scored, QH), (p_turned, QH), (mixed, 1)):
                    pe.sem_inc(s, 2 * per)
                pe.wait_ge(consts, 48)
                pe.wait_ge(padded, 1)

                def prepare(i, p, t):
                    pe.wait_ge(rotated, done(t, 2, 2))
                    pe.wait_ge(all_out, done(t - 2))
                    pe.sem_inc(passed, 1)
                    for h in range(HH):
                        last = pe.transpose(ps[0:AD, 4 * p + h // 4, (h % 4) * P:(h % 4 + 1) * P], qk[:, p, h, :], eye[:])
                    last.then_inc(turned, 1)
                each(pe, prepare)
                pe.wait_ge(all_out, done(NT - 1))

                def slot(p, t, old):
                    if t is not None:
                        pe.wait_ge(q_copied, done(t))
                        for h in range(QH):
                            pe.wait_ge(masked, done(t, h - 3, QH))
                            pe.sem_inc(passed, 1)
                            kv = QH + h // (QH // KVH)
                            keys = qkT[:, kv, bass.ds(t, 3), :].rearrange("d j t -> d (j t)")
                            pe.matmul(ps[:, h % 4, 0:3 * P], qT[:, p, h, :], keys, start=True, stop=True).then_inc(scored, 1)
                    if old is not None:
                        for h in range(QH):
                            pe.wait_ge(exped, done(old, h + 2, QH + 1))
                            pe.wait_ge(pT_dve if h % 2 else pT_act, done(old, h // 2, 4))
                            for j in range(3):
                                last = pe.transpose(ps[:, 4 + h % 2, j * P:(j + 1) * P], pr[:, h, j * P:(j + 1) * P], eye[:])
                            last.then_inc(p_turned, 1)
                        pe.wait_ge(o_out, done(old - 1))
                        for h in range(QH):
                            pe.wait_ge(pT_dve if h % 2 else pT_act, done(old, h // 2 + 1, 4))
                            kv = h // (QH // KVH)
                            for j in range(3):
                                last = pe.matmul(ps[:, 6, h * AD:(h + 1) * AD], pT[:, h, j, :],
                                                 v[:, bass.ds(old + j, 1), kv * AD:(kv + 1) * AD].rearrange("k o d -> k (o d)"),
                                                 start=(j == 0), stop=(j == 2))
                        last.then_inc(mixed, 1)
                lagged(pe, slot)






def mix_and_route(nc, io, scr, ps, sem, n_more):
    with ExitStack() as keep:
        sb = lambda n, s, dt=F32: keep.enter_context(nc.sbuf_tensor(n, s, dt))
        names = ["eye", "lt", "ones", "le"]
        tab_t, tab = load_tab(nc, keep, names, "f")
        w = sb("f_w", [P, KD, D])
        wr = sb("f_wr", [P, KD, NG + NE])
        bias = sb("f_bias", [P, NG + NE])
        count = sb("f_count", [P, NG + NE + NE + NR])
        token = sb("f_token", [P, NT + 1])
        nw = sb("f_nw", [P, HEADS, DH])
        lnf = sb("f_lnf", [P, D])
        power = sb("f_power", [P, HEADS])
        oo = sb("f_oo", [P, 2, 2, DN])
        za = sb("f_za", [P, 2, 2, DN])
        x = sb("f_x", [P, 2, D])
        osum = sb("f_osum", [P, HEADS, DH])
        junk = sb("f_junk", [P, D])
        ssq, ms, rstd = sb("f_ssq", [P, HEADS]), sb("f_ms", [P, HEADS]), sb("f_rstd", [P, HEADS])
        ez = sb("f_ez", [P, DN])
        mT = sb("f_mT", [P, KD, P])
        x1 = sb("f_x1", [P, 2, D])
        ss2, ms2, rstd2 = sb("f_ss2", [P, 1]), sb("f_ms2", [P, 1]), sb("f_rstd2", [P, 1])
        h2 = sb("f_h2", [P, 2, D])
        h2T = sb("f_h2T", [P, KD, P])
        lg = sb("f_lg", [P, NG + NE])
        gexp = sb("f_gexp", [P, NG])
        pick = sb("f_pick", [P, NG])
        em = sb("f_em", [P, NE])
        score = sb("f_score", [P, NE])
        oh = sb("f_oh", [P, 3, NE])
        pos = sb("f_pos", [P, NE])
        col = sb("f_col", [P, 16])
        total = sb("f_total", [P, NE])
        exceed, extra, extraT = sb("f_exceed", [P, NE, NR]), sb("f_extra", [P, NE]), sb("f_extraT", [NE, P])
        csum, before, items = sb("f_csum", [P, NE]), sb("f_before", [P, NE]), sb("f_items", [P, 2], I32)
        slot_id = sb("f_slot", [P, 2], I32)
        rec = sb("f_rec", [P, 2, 4], I32)

        consts = sem("f_consts")
        loaded, stored_x, stored_h = [[sem(f"f_{n}{p}") for p in range(2)] for n in ("loaded", "x1_stored", "h2_stored")]
        osummed, osquared, omean, orooted = [sem("f_" + n) for n in ("osummed", "osquared", "omean", "orooted")]
        zexp, zdone, odone, onormed = [sem("f_" + n) for n in ("zexp", "zdone", "odone", "onormed")]
        mturned, mT_out, product, added = [sem("f_" + n) for n in ("mturned", "mT_out", "product", "added")]
        squared, mean, rooted, normed, h2_out = [sem("f_" + n) for n in ("squared", "mean", "rooted", "normed", "h2_out")]
        hturned, hT_act, hT_dve, logits, gexped, rexped = [sem("f_" + n) for n in ("hturned", "hT_act", "hT_dve", "logits", "gexped", "rexped")]
        routed, counted, scattered, freed = [sem("f_" + n) for n in ("routed", "counted", "scattered", "freed")]
        zexp_act, total_set, planned, extra_up, items_out, powered, passed = [
            sem("f_" + n) for n in ("zexp_act", "total_set", "planned", "extra_up", "items_out", "powered", "passed")]
        N8 = count[:, 0:NG]
        N64 = count[:, NG:NG + NE]
        turn = lambda b: ps[:, b, :].rearrange("p (k t) -> p k t", k=4)
        LOADS = 16 * 5
        ROUTE = ["logits", "best", "shift", "ties", "first", "group", "penalty", "masked", "top0", "ties0", "first0", "mask0",
                 "drop0", "top1", "ties1", "first1", "mask1", "gap", "both", "spread", "gate0", "gate1", "place", "total",
                 "place0", "place1", "base", "token", "dest0", "dest1", "gates", "spare", "slots"]

        def route_at(name, t):
            return len(ROUTE) * (t + 2) + ROUTE.index(name) + 1

        with nc.Block() as block:

            @block.sync
            def _(sp):
                issue_tab(sp, io, tab_t, names, consts)
                for k in range(KD):
                    sp.dma_start(w[:, k, :], io["w_out"][0, k * P:(k + 1) * P, :]).then_inc(consts, 16)
                sp.dma_start(wr[:, :, 0:NG], io["w_group"][0].rearrange("(k p) n -> p k n", p=P)).then_inc(consts, 16)
                sp.dma_start(wr[:, :, NG:], io["w_expert"][0].rearrange("(k p) n -> p k n", p=P)).then_inc(consts, 16)
                sp.dma_start(bias[:, 0:NG], io["b_group"].to_broadcast([P, NG])).then_inc(consts, 16)
                sp.dma_start(bias[:, NG:], io["b_expert"].to_broadcast([P, NE])).then_inc(consts, 16)
                sp.dma_start(count[:], io["count"]).then_inc(consts, 16)
                sp.dma_start(token[:], io["token"]).then_inc(consts, 16)
                sp.dma_start(lnf[:], io["ln_ffn"].to_broadcast([P, D])).then_inc(consts, 16)
                for h in range(HEADS):
                    sp.dma_start(nw[:, h, :], io["dn_norm"].to_broadcast([P, DH])).then_inc(consts, 16)

                with sp.Fori(0, NT // 2) as i:
                    for p in range(2):
                        t = 2 * i + p
                        row, turned, added_ = sp.snap(t * P), sp.snap(done(t - 2, 2, 2)), sp.snap(done(t - 2))
                        sp.wait_ge(mturned, turned)
                        sp.wait_ge(added, turned)
                        for d in range(2):
                            sp.dma_start(oo[:, p, d], scr["o"][d, bass.ds(row, P), :]).then_inc(loaded[p], 16)
                        sp.dma_start(za[:, p, 0], scr["tok"][bass.ds(row, P), Z0:Z0 + DN]).then_inc(loaded[p], 16)
                        sp.dma_start(za[:, p, 1], scr["attn"][bass.ds(row, P), :]).then_inc(loaded[p], 16)
                        sp.dma_start(x[:, p], io["x"][0, bass.ds(row, P), :]).then_inc(loaded[p], 16)

                sp.wait_ge(planned, 13)
                sp.dma_start(scr["items"], items[:]).then_inc(items_out, 16)
                sp.wait_ge(items_out, 16)

            ALL = 16 * (len(names) + KD + 7 + HEADS)

            @block.gpsimd
            def _(pool):
                for s, per in ((orooted, 1), (zdone, 2), (onormed, 1), (rooted, 1), (h2_out, 1)):
                    pool.sem_inc(s, 2 * per)
                pool.sem_inc(freed, 2)
                pool.memset(power[:], -0.5).then_inc(powered, 1)
                pool.wait_ge(powered, 1)
                pool.wait_ge(consts, ALL)

                def slot(p, t, old):
                    if t is not None:
                        pool.wait_ge(omean, done(t))
                        pool.wait_ge(odone, done(t - 1))
                        pool.tensor_tensor(rstd[:], ms[:], power[:], ALU.pow).then_inc(orooted, 1)
                        pool.wait_ge(zexp, done(t, 2, 2))
                        pool.tensor_tensor(ez[:], ez[:], za[:, p, 0], ALU.mult).then_inc(zdone, 1)
                        pool.wait_ge(zdone, done(t, 1, 2))
                        pool.tensor_tensor(ez[:], ez[:], nw[:].rearrange("p h d -> p (h d)"), ALU.mult).then_inc(zdone, 1)
                        pool.wait_ge(zdone, done(t, 2, 2))
                        pool.wait_ge(odone, done(t))
                        pool.tensor_tensor(osum[:], osum[:], ez[:].rearrange("p (h d) -> p h d", h=HEADS), ALU.mult).then_inc(onormed, 1)
                    if old is not None:
                        q = 1 - p
                        pool.wait_ge(mean, done(old))
                        pool.wait_ge(normed, done(old - 1))
                        pool.tensor_tensor(rstd2[:], ms2[:], power[:, 0:1], ALU.pow).then_inc(rooted, 1)
                        pool.wait_ge(normed, done(old))
                        pool.tensor_tensor(h2[:, q], h2[:, q], lnf[:], ALU.mult).then_inc(h2_out, 1)
                        for c in range(2):
                            if c == 0:
                                pool.wait_ge(routed, route_at("slots", old))
                                pool.sem_inc(passed, 1)
                            pool.indirect_dma_start(scr["list"][:, :], bass.IndirectOffsetOnAxis(slot_id[:, c:c + 1], 0), rec[:, c, :], None,
                                                    bounds_check=LISTS - 1, oob_is_err=False).then_inc(scattered, 16)
                        pool.wait_ge(scattered, 32 * (old + 1))
                        pool.sem_inc(freed, 1)
                lagged(pool, slot)

            @block.scalar
            def _(act):
                for s, per in ((osquared, 1), (mT_out, 2), (squared, 1), (hT_act, 1), (gexped, 1), (rexped, 1)):
                    act.sem_inc(s, 2 * per)
                act.sem_inc(zexp_act, 2)
                for p in range(2):
                    act.sem_inc(stored_x[p], 16)
                    act.sem_inc(stored_h[p], 16)

                def slot(p, t, old):
                    if t is not None:
                        act.wait_ge(loaded[p], 8 * 5 * (t - p) + LOADS)
                        act.wait_ge(onormed, done(t - 1))
                        act.activation(ez[:], za[:, p, 0], ACT.Exp, scale=-1.0).then_inc(zexp_act, 1)
                        act.wait_ge(osummed, done(t))
                        act.wait_ge(squared, done(t - 2))
                        act.wait_ge(omean, done(t - 1))
                        for h in range(HEADS):
                            last = act.activation(junk[:, h * DH:(h + 1) * DH], osum[:, h], ACT.Square, accum_out=ssq[:, h:h + 1])
                        last.then_inc(osquared, 1)
                    if t is not None:
                        for b in range(2):
                            act.wait_ge(mturned, done(t, b + 1, 2))
                            act.wait_ge(product, done(t - 1, 2, 2))
                            act.copy(mT[:, 4 * b:4 * b + 4], turn(b)).then_inc(mT_out, 1)
                    if old is not None:
                        q = 1 - p
                        act.wait_ge(added, done(old, 2, 2))
                        act.wait_ge(osquared, done(old))
                        act.wait_ge(mean, done(old - 1))
                        act.activation(junk[:], x1[:, q], ACT.Square, accum_out=ss2[:]).then_inc(squared, 1)
                        act.dma_start(scr["x1"][bass.ds(old * P, P), :], x1[:, q]).then_inc(stored_x[q], 16)
                        act.wait_ge(hturned, done(old, 1, 2))
                        act.wait_ge(logits, done(old - 1))
                        act.copy(h2T[:, 0:4], turn(4)).then_inc(hT_act, 1)
                        act.wait_ge(h2_out, done(old))
                        act.dma_start(scr["h2"][bass.ds(old * P, P), :], h2[:, q]).then_inc(stored_h[q], 16)
                    if old is not None:
                        act.wait_ge(routed, route_at("shift", old))
                        act.activation(gexp[:], pick[:], ACT.Exp, accum_out=col[:, 1:2]).then_inc(gexped, 1)
                        act.wait_ge(routed, route_at("gap", old))
                        act.activation(col[:, 8:9], col[:, 7:8], ACT.Exp).then_inc(rexped, 1)
                lagged(act, slot)
                for p in range(2):
                    act.wait_ge(stored_x[p], landed(NT // 2))
                    act.wait_ge(stored_h[p], landed(NT // 2))

            @block.vector
            def _(dve):
                for s, per in ((osummed, 1), (omean, 1), (zexp, 2), (odone, 1), (added, 2), (mean, 1), (normed, 1), (hT_dve, 1), (routed, len(ROUTE))):
                    dve.sem_inc(s, 2 * per)
                dve.wait_ge(consts, ALL)
                dve.memset(total[:], 0.0).then_inc(total_set, 1)
                dve.wait_ge(total_set, 1)

                def slot(p, t, old):
                    if t is not None:
                        dve.wait_ge(loaded[p], 8 * 5 * (t - p) + LOADS)
                        dve.wait_ge(mturned, done(t - 1, 2, 2))
                        dve.tensor_tensor(osum[:], oo[:, p, 0].rearrange("p (h d) -> p h d", h=HEADS),
                                          oo[:, p, 1].rearrange("p (h d) -> p h d", h=HEADS), ALU.add).then_inc(osummed, 1)
                        dve.wait_ge(zexp_act, done(t))
                        dve.tensor_scalar(ez[:], ez[:], 1.0, None, ALU.add).then_inc(zexp, 1)
                        dve.wait_ge(zexp, done(t, 1, 2))
                        dve.reciprocal(ez[:], ez[:]).then_inc(zexp, 1)
                        dve.wait_ge(osquared, done(t))
                        dve.wait_ge(orooted, done(t - 1))
                        dve.tensor_scalar(ms[:], ssq[:], 1.0 / DH, EPS, ALU.mult, ALU.add).then_inc(omean, 1)
                        dve.wait_ge(orooted, done(t))
                        dve.wait_ge(osummed, done(t))
                        dve.tensor_tensor(osum[:], osum[:], rstd[:].unsqueeze(2).to_broadcast([P, HEADS, DH]), ALU.mult).then_inc(odone, 1)
                    if old is not None:
                        q = 1 - p
                        dve.wait_ge(loaded[q], 8 * 5 * (old - q) + LOADS)
                        dve.wait_ge(stored_x[q], 8 * (old - q) + 16)
                        for b in range(2):
                            dve.wait_ge(product, done(old, b + 1, 2))
                            dve.tensor_tensor(x1[:, q, b * 512:(b + 1) * 512], ps[:, 2 + b, :], x[:, q, b * 512:(b + 1) * 512], ALU.add).then_inc(added, 1)
                        dve.wait_ge(squared, done(old))
                        dve.wait_ge(rooted, done(old - 1))
                        dve.tensor_scalar(ms2[:], ss2[:], 1.0 / D, EPS, ALU.mult, ALU.add).then_inc(mean, 1)
                        dve.wait_ge(rooted, done(old))
                        dve.wait_ge(added, done(old, 2, 2))
                        dve.wait_ge(stored_h[q], 8 * (old - q) + 16)
                        dve.wait_ge(hturned, done(old - 2, 2, 2))
                        dve.tensor_scalar(h2[:, q], x1[:, q], rstd2[:], None, ALU.mult).then_inc(normed, 1)
                        dve.wait_ge(hturned, done(old, 2, 2))
                        dve.wait_ge(logits, done(old - 1))
                        dve.tensor_copy(h2T[:, 4:8], turn(5)).then_inc(hT_dve, 1)

                        def then(name, ins):
                            ins.then_inc(routed, 1)
                            dve.wait_ge(routed, route_at(name, old))

                        gl = lg[:, 0:NG]
                        C = lambda n: col[:, n:n + 1]
                        by_group = lambda a: a.rearrange("p (g e) -> p g e", g=NG)
                        dve.wait_ge(logits, done(old))
                        then("logits", dve.tensor_tensor(lg[:], ps[:, 6, 0:NG + NE], bias[:], ALU.add))
                        then("best", dve.tensor_reduce(C(0), gl, AX.X, ALU.max))
                        then("shift", dve.tensor_scalar(pick[:], gl, C(0), None, ALU.subtract))
                        dve.wait_ge(gexped, done(old))
                        then("ties", dve.scalar_tensor_tensor(pick[:], pick[:], 0.0, N8, ALU.is_ge, ALU.mult))
                        then("first", dve.tensor_reduce(C(2), pick[:], AX.X, ALU.max))
                        then("group", dve.tensor_scalar(pick[:], N8, C(2), None, ALU.is_equal))
                        then("penalty", dve.tensor_scalar(pick[:], pick[:], -1.0, BIG, ALU.add, ALU.mult))
                        then("masked", dve.tensor_tensor(by_group(em[:]), by_group(lg[:, NG:]),
                                                         pick[:].unsqueeze(2).to_broadcast([P, NG, NE // NG]), ALU.add))
                        for c in range(2):
                            then(f"top{c}", dve.tensor_reduce(C(3 + c), em[:], AX.X, ALU.max))
                            then(f"ties{c}", dve.scalar_tensor_tensor(score[:], em[:], C(3 + c), N64, ALU.is_ge, ALU.mult))
                            then(f"first{c}", dve.tensor_reduce(C(5 + c), score[:], AX.X, ALU.max))
                            then(f"mask{c}", dve.tensor_scalar(oh[:, c], N64, C(5 + c), None, ALU.is_equal))
                            if c == 0:
                                then("drop0", dve.scalar_tensor_tensor(em[:], oh[:, 0], -BIG, em[:], ALU.mult, ALU.add))
                        then("gap", dve.tensor_tensor(C(7), C(4), C(3), ALU.subtract))
                        then("both", dve.tensor_tensor(oh[:, 2], oh[:, 0], oh[:, 1], ALU.add))
                        dve.wait_ge(rexped, done(old))
                        then("spread", dve.scalar_tensor_tensor(C(9), C(8), 1.0, C(1), ALU.add, ALU.mult))
                        then("gate0", dve.reciprocal(C(10), C(9)))
                        then("gate1", dve.tensor_tensor(C(11), C(10), C(8), ALU.mult))
                        dve.wait_ge(counted, done(old))
                        then("place", dve.tensor_tensor(pos[:], ps[:, 7, 0:NE], total[:], ALU.add))
                        then("total", dve.tensor_tensor(total[:], ps[:, 7, NE:2 * NE], total[:], ALU.add))
                        for c in range(2):
                            then(f"place{c}", dve.scalar_tensor_tensor(score[:], oh[:, c], 1.0, pos[:], ALU.mult, ALU.mult,
                                                                       accum_out=C(12 + c)))
                        then("base", dve.tensor_scalar(col[:, 14:16], col[:, 5:7], float(-CAP), float(LISTS), ALU.mult, ALU.add))
                        dve.wait_ge(freed, done(old - 1))
                        tok = token[:, bass.ds(old, 1)]
                        then("token", dve.tensor_scalar(rec[:, :, 0], tok.to_broadcast([P, 2]), 0.0, None, ALU.add))
                        then("dest0", dve.tensor_scalar(rec[:, 0, 1:2], tok, 0.0, None, ALU.add))
                        then("dest1", dve.tensor_scalar(rec[:, 1, 1:2], tok, float(S), None, ALU.add))
                        then("gates", dve.tensor_copy(rec[:].bitcast(F32)[:, :, 2], col[:, 10:12]))
                        then("spare", dve.tensor_scalar(rec[:, :, 3], col[:, 10:12], 0.0, None, ALU.mult))
                        then("slots", dve.tensor_tensor(slot_id[:], col[:, 14:16], col[:, 12:14], ALU.add))
                lagged(dve, slot)

                def plan(n, ins):
                    ins.then_inc(planned, 1)
                    dve.wait_ge(planned, n)

                plan(1, dve.tensor_tensor(exceed[:], total[:].unsqueeze(2).to_broadcast([P, NE, NR]),
                                          count[:, NG + 2 * NE:].unsqueeze(1).to_broadcast([P, NE, NR]), ALU.is_gt))
                plan(2, dve.tensor_reduce(extra[:], exceed[:], AX.X, ALU.add))
                dve.wait_ge(extra_up, 1)
                plan(3, dve.tensor_copy(extraT[:], ps[0:NE, 0, 0:P]))
                dve.wait_ge(extra_up, 2)
                plan(4, dve.tensor_copy(csum[:], ps[:, 1, 0:NE]))
                k = token[:, NT:NT + 1]
                plan(5, dve.tensor_scalar(before[:], csum[:], k, None, ALU.is_le))
                plan(6, dve.tensor_reduce(col[:, 0:1], before[:], AX.X, ALU.add))
                plan(7, dve.tensor_tensor(score[:], before[:], extra[:], ALU.mult))
                plan(8, dve.tensor_reduce(col[:, 1:2], score[:], AX.X, ALU.add))
                plan(9, dve.tensor_tensor(col[:, 2:3], k, col[:, 1:2], ALU.subtract))
                plan(10, dve.tensor_scalar(col[:, 3:4], col[:, 2:3], float(TILE), float(TILE), ALU.mult, ALU.add))
                plan(11, dve.scalar_tensor_tensor(col[:, 4:5], col[:, 0:1], float(CAP), col[:, 3:4], ALU.mult, ALU.add))
                plan(12, dve.tensor_scalar(items[:, 0:1], col[:, 0:1], float(NE - 1), None, ALU.min))
                plan(13, dve.tensor_scalar(items[:, 1:2], col[:, 4:5], float(LISTS), None, ALU.min))
                plan(14, dve.tensor_copy(n_more[:], csum[0:1, NE - 1:NE]))

            @block.tensor
            def _(pe):
                for s, per in ((mturned, 2), (product, 2), (hturned, 2), (logits, 1), (counted, 1)):
                    pe.sem_inc(s, 2 * per)
                pe.wait_ge(consts, ALL)

                def product_half(p, t, b):
                    for k in range(KD):
                        last = pe.matmul(ps[:, 2 + b, :], mT[:, k], w[:, k, b * 512:(b + 1) * 512], start=(k == 0), stop=(k == KD - 1))
                    last.then_inc(product, 1)

                def slot(p, t, old):
                    if t is not None:
                        pe.wait_ge(onormed, done(t))
                        pe.wait_ge(mT_out, done(t - 1, 2, 2))
                        for b in range(2):
                            for k in range(4):
                                src = osum[:, k] if b == 0 else za[:, p, 1, k * P:(k + 1) * P]
                                last = pe.transpose(turn(b)[:, k], src, tab["eye"])
                            last.then_inc(mturned, 1)
                        pe.wait_ge(mT_out, done(t, 2, 2))
                        pe.wait_ge(added, done(t - 1, 2, 2))
                        product_half(p, t, 0)
                    if old is not None:
                        q = 1 - p
                        pe.wait_ge(h2_out, done(old))
                        for b, out_ in ((0, hT_act), (1, hT_dve)):
                            pe.wait_ge(out_, done(old - 1))
                            for k in range(4):
                                last = pe.transpose(turn(4 + b)[:, k], h2[:, q, (4 * b + k) * P:(4 * b + k + 1) * P], tab["eye"])
                            last.then_inc(hturned, 1)
                        pe.wait_ge(hT_act, done(old))
                        pe.wait_ge(hT_dve, done(old))
                        pe.wait_ge(routed, route_at("logits", old - 1))
                        for k in range(KD):
                            last = pe.matmul(ps[:, 6, 0:NG + NE], h2T[:, k], wr[:, k], start=(k == 0), stop=(k == KD - 1))
                        last.then_inc(logits, 1)
                    if t is not None:
                        product_half(p, t, 1)
                    if old is not None:
                        pe.wait_ge(routed, route_at("both", old))
                        pe.matmul(ps[:, 7, 0:NE], tab["lt"], oh[:, 2], start=True, stop=True)
                        pe.matmul(ps[:, 7, NE:2 * NE], tab["ones"], oh[:, 2], start=True, stop=True).then_inc(counted, 1)
                lagged(pe, slot)
                pe.wait_ge(planned, 2)
                pe.transpose(ps[0:NE, 0, 0:P], extra[:], tab["eye"]).then_inc(extra_up, 1)
                pe.wait_ge(planned, 3)
                pe.matmul(ps[:, 1, 0:NE], extraT[:], tab["le"][0:NE, 0:NE], start=True, stop=True).then_inc(extra_up, 1)




def experts(nc, io, scr, ps, sem, n_more):
    with ExitStack() as keep:
        sb = lambda n, s, dt=F32: keep.enter_context(nc.sbuf_tensor(n, s, dt))
        BUF = 4
        FT = FF // P
        eye = sb("g_eye", [P, P])
        wgu = [sb(f"g_wgu{b}", [P, KD, 2 * FF]) for b in range(BUF)]
        wd = [sb(f"g_wd{b}", [P, FT, D]) for b in range(BUF)]
        lists = sb("g_lists", [P, NE, 4], I32)
        rec = [sb(f"g_rec{b}", [P, 4], I32) for b in range(BUF)]
        xg = [sb(f"g_xg{b}", [P, D]) for b in range(2)]
        xT = [sb(f"g_xT{b}", [P, KD, TILE]) for b in range(2)]
        sig = sb("g_sig", [P, FT, TILE])
        hid = [sb(f"g_hid{b}", [P, FT, TILE]) for b in range(2)]
        y = [sb(f"g_y{b}", [P, D]) for b in range(2)]
        items = sb("g_items", [1, P, 2], I32)

        consts, items_in = sem("g_consts"), sem("g_items_in")
        turn = lambda b: ps[:, b, 0:4 * TILE].rearrange("p (k t) -> p k t", k=4)
        up = lambda b: ps[:, 2 + b, 0:4 * TILE].rearrange("p (f t) -> p f t", f=4)
        down = lambda b, n: ps[:, 4 + 2 * b + n, :]

        class Signals:

            def __init__(self, pre):
                s = lambda n: sem(f"g_{pre}_{n}")
                self.gu_in, self.d_in = [s(f"gu_in{b}") for b in range(BUF)], [s(f"d_in{b}") for b in range(BUF)]
                self.listed, self.gathered = s("listed"), [s(f"gathered{b}") for b in range(2)]
                self.scattered, self.freed = s("scattered"), s("freed")
                self.turned, self.xT_act, self.xT_dve = s("turned"), s("xT_act"), s("xT_dve")
                self.upped, self.sig_act, self.hidden = s("upped"), s("sig_act"), s("hidden")
                self.passed = s("passed")
                self.downed, self.y_act, self.y_dve = s("downed"), s("y_act"), s("y_dve")

        first, more = Signals("first"), Signals("more")


        def weights(sp, s, b4, expert, free):
            if free is not None:
                sp.wait_ge(s.upped, free)
            sp.dma_start(wgu[b4][:], io["w_gate_up"][0, bass.ds(expert, 1)].rearrange("o (k p) n -> p (o k) n", p=P)).then_inc(s.gu_in[b4], 16)
            if free is not None:
                sp.wait_ge(s.downed, free)
            sp.dma_start(wd[b4][:], io["w_down"][0, bass.ds(expert, 1)].rearrange("o (j p) n -> p (o j) n", p=P)).then_inc(s.d_in[b4], 16)

        def gather(pool, s, b4, b2, t):
            pool.wait_ge(s.turned, done(t - 2, 2, 2))
            pool.sem_inc(s.passed, 1)
            pool.indirect_dma_start(xg[b2][:], None, scr["h2"][:, :], bass.IndirectOffsetOnAxis(rec[b4][:, 0:1], 0),
                                    bounds_check=S - 1, oob_is_err=False).then_inc(s.gathered[b2], 16)

        def landed_scatter(pool, s, t):
            pool.wait_ge(s.scattered, 16 * (t + 1))
            pool.sem_inc(s.freed, 1)

        def scatter(pool, s, b4, b2, t):
            pool.wait_ge(s.y_act, done(t))
            pool.wait_ge(s.y_dve, done(t))
            pool.sem_inc(s.passed, 1)
            pool.indirect_dma_start(scr["y"][:, :], bass.IndirectOffsetOnAxis(rec[b4][:, 1:2], 0), y[b2][:], None,
                                    bounds_check=2 * S - 1, oob_is_err=False).then_inc(s.scattered, 16)

        def act_turn(act, s, b2, t):
            act.wait_ge(s.turned, done(t, 1, 2))
            act.wait_ge(s.upped, done(t - 2))
            act.copy(xT[b2][:, 0:4], turn(0)).then_inc(s.xT_act, 1)

        def act_up(act, s, b2, t):
            act.wait_ge(s.upped, done(t))
            act.wait_ge(s.hidden, done(t - 1))
            act.activation(sig[:], up(b2)[:, 0:FT], ACT.Silu).then_inc(s.sig_act, 1)

        def act_down(act, s, b4, b2, t):
            act.wait_ge(s.downed, done(t))
            act.wait_ge(s.freed, done(t - 2))
            act.mul(y[b2][:, 0:512], down(b2, 0), rec[b4][:].bitcast(F32)[:, 2:3]).then_inc(s.y_act, 1)

        def dve_turn(dve, s, b2, t):
            dve.wait_ge(s.turned, done(t, 2, 2))
            dve.wait_ge(s.upped, done(t - 2))
            dve.tensor_copy(xT[b2][:, 4:8], turn(1)).then_inc(s.xT_dve, 1)

        def dve_up(dve, s, b2, t):
            dve.wait_ge(s.sig_act, done(t))
            dve.wait_ge(s.downed, done(t - 2))
            dve.tensor_tensor(hid[b2][:], up(b2)[:, FT:2 * FT], sig[:], ALU.mult).then_inc(s.hidden, 1)

        def dve_down(dve, s, b4, b2, t):
            dve.wait_ge(s.downed, done(t))
            dve.wait_ge(s.freed, done(t - 2))
            dve.tensor_scalar(y[b2][:, 512:], down(b2, 1), rec[b4][:].bitcast(F32)[:, 2:3], None, ALU.mult).then_inc(s.y_dve, 1)

        def pe_turn(pe, s, b2, t, r2):
            pe.wait_ge(s.gathered[b2], 16 * (r2 + 1))
            for half, emptied in ((0, s.xT_act), (1, s.xT_dve)):
                pe.wait_ge(emptied, done(t - 1))
                for k in range(4):
                    kk = 4 * half + k
                    last = pe.transpose(turn(half)[:, k], xg[b2][0:TILE, kk * P:(kk + 1) * P], eye[0:TILE, 0:TILE])
                last.then_inc(s.turned, 1)

        def pe_up(pe, s, b4, b2, t, r4):
            pe.wait_ge(s.xT_act, done(t))
            pe.wait_ge(s.xT_dve, done(t))
            pe.wait_ge(s.hidden, done(t - 2))
            pe.wait_ge(s.gu_in[b4], 16 * (r4 + 1))
            for f in range(2 * FT):
                for k in range(KD):
                    last = pe.matmul(up(b2)[:, f], wgu[b4][:, k, f * P:(f + 1) * P], xT[b2][:, k], start=(k == 0), stop=(k == KD - 1))
            last.then_inc(s.upped, 1)

        def pe_down(pe, s, b4, b2, t, r4):
            pe.wait_ge(s.hidden, done(t))
            pe.wait_ge(s.y_act, done(t - 2))
            pe.wait_ge(s.y_dve, done(t - 2))
            pe.wait_ge(s.d_in[b4], 16 * (r4 + 1))
            for n in range(2):
                for j in range(FT):
                    last = pe.matmul(down(b2, n), hid[b2][:, j], wd[b4][:, j, n * 512:(n + 1) * 512], start=(j == 0), stop=(j == FT - 1))
            last.then_inc(s.downed, 1)

        def each(eng, slot):
            for c in range(-2, 2):
                slot(lambda n, c=c: tile(c + n))
            with eng.Fori(0, NE // 4 - 1) as j:
                for q in range(2, 6):
                    slot(lambda n: (4 * j + q + n, (q + n) % 4, (q + n) % 2, j + (q + n) // 4, 2 * j + (q + n) // 2))
            for c in range(NE - 2, NE + 1):
                slot(lambda n, c=c: tile(c + n))

        def tile(t):
            return (t, t % 4, t % 2, t // 4, t // 2) if 0 <= t < NE else None

        def again(eng, body):
            n = eng.value_load(n_more[0:1, 0:1], min_val=0, max_val=MORE)
            with eng.If(n > 0):
                body()

        with nc.Block() as block:

            @block.sync
            def _(sp):
                j = NAMES.index("eye")
                sp.dma_start(eye[:], io["tab"][:, j * P:(j + 1) * P]).then_inc(consts, 16)
                sp.dma_start(lists[:], scr["list"][0:LISTS, :].rearrange("(e r) c -> r e c", r=CAP)[0:P]).then_inc(consts, 16)
                sp.dma_start(items[:], scr["items"].unsqueeze(0)).then_inc(items_in, 16)
                for b in range(BUF):
                    weights(sp, first, b, b, None)
                with sp.Fori(1, NE // BUF) as j:
                    for b in range(BUF):
                        e, free = sp.snap(BUF * j + b), sp.snap(done(BUF * j + b - BUF))
                        weights(sp, first, b, e, free)

                def body():
                    sp.wait_ge(first.downed, done(NE - 1))
                    sp.wait_ge(items_in, 16)
                    with sp.Fori(0, MORE) as k:
                        e = sp.value_load(items[0:1, bass.ds(k, 1), 0], min_val=0, max_val=NE - 1)
                        free = sp.snap(done(k - 1))
                        weights(sp, more, 0, e, free)
                again(sp, body)

            @block.gpsimd
            def _(pool):
                for s in (first, more):
                    pool.sem_inc(s.freed, 2)
                pool.wait_ge(consts, 32)
                pool.wait_ge(items_in, 16)

                for b in range(2):
                    pool.memset(xg[b][:], 0.0).then_inc(first.listed, 1)

                def slot(at):
                    if at(-2) is not None:
                        landed_scatter(pool, first, at(-2)[0])
                    if at(2) is not None:
                        t, b4, b2, r4, r2 = at(2)
                        pool.sem_inc(first.passed, 1)
                        pool.tensor_copy(rec[b4][:], lists[:, bass.ds(t, 1), :].rearrange("p o c -> p (o c)")).then_inc(first.listed, 1)
                        pool.wait_ge(first.listed, t + 3)
                        gather(pool, first, b4, b2, t)
                    if at(-1) is not None:
                        t, b4, b2, r4, r2 = at(-1)
                        scatter(pool, first, b4, b2, t)
                each(pool, slot)
                landed_scatter(pool, first, NE - 1)

                def body():
                    pool.wait_ge(items_in, 16)
                    with pool.Fori(0, MORE) as k:
                        row = pool.value_load(items[0:1, bass.ds(k, 1), 1], min_val=0, max_val=LISTS)
                        pool.dma_start(rec[0][:], scr["list"][bass.ds(row, P), :]).then_inc(more.listed, 16)
                        pool.wait_ge(more.listed, 16 * (k + 1))
                        gather(pool, more, 0, 0, k)
                        scatter(pool, more, 0, 0, k)
                        landed_scatter(pool, more, k)
                again(pool, body)

            @block.scalar
            def _(act):
                for s in (first, more):
                    for q in (s.xT_act, s.sig_act, s.y_act):
                        act.sem_inc(q, 2)

                def slot(at):
                    if at(0) is not None:
                        act_up(act, first, at(0)[2], at(0)[0])
                    if at(1) is not None:
                        act_turn(act, first, at(1)[2], at(1)[0])
                    if at(-1) is not None:
                        t, b4, b2, r4, r2 = at(-1)
                        act_down(act, first, b4, b2, t)
                each(act, slot)

                def body():
                    with act.Fori(0, MORE) as k:
                        act_turn(act, more, 0, k)
                        act_up(act, more, 0, k)
                        act_down(act, more, 0, 0, k)
                again(act, body)

            @block.vector
            def _(dve):
                for s in (first, more):
                    for q, per in ((s.xT_dve, 1), (s.hidden, 1), (s.y_dve, 1)):
                        dve.sem_inc(q, 2 * per)

                def slot(at):
                    if at(0) is not None:
                        dve_up(dve, first, at(0)[2], at(0)[0])
                    if at(1) is not None:
                        dve_turn(dve, first, at(1)[2], at(1)[0])
                    if at(-1) is not None:
                        t, b4, b2, r4, r2 = at(-1)
                        dve_down(dve, first, b4, b2, t)
                each(dve, slot)

                def body():
                    with dve.Fori(0, MORE) as k:
                        dve_turn(dve, more, 0, k)
                        dve_up(dve, more, 0, k)
                        dve_down(dve, more, 0, 0, k)
                again(dve, body)

            @block.tensor
            def _(pe):
                for s in (first, more):
                    for q, per in ((s.turned, 2), (s.upped, 1), (s.downed, 1)):
                        pe.sem_inc(q, 2 * per)
                pe.wait_ge(consts, 32)

                def slot(at):
                    if at(0) is not None:
                        t, b4, b2, r4, r2 = at(0)
                        pe_up(pe, first, b4, b2, t, r4)
                    if at(1) is not None:
                        t, b4, b2, r4, r2 = at(1)
                        pe_turn(pe, first, b2, t, r2)
                    if at(-1) is not None:
                        t, b4, b2, r4, r2 = at(-1)
                        pe_down(pe, first, b4, b2, t, r4)
                each(pe, slot)

                def body():
                    with pe.Fori(0, MORE) as k:
                        pe_turn(pe, more, 0, k, k)
                        pe_up(pe, more, 0, 0, k, k)
                        pe_down(pe, more, 0, 0, k, k)
                again(pe, body)



def finish(nc, io, scr, ps, sem, out):
    with ExitStack() as keep:
        sb = lambda n, s, dt=F32: keep.enter_context(nc.sbuf_tensor(n, s, dt))
        ln = sb("h_ln", [P, D])
        x = sb("h_x", [P, 2, 3, D])
        s1 = sb("h_sum", [P, 2, D])
        sq = sb("h_sq", [P, D])
        power = sb("h_power", [P, 1])
        ss, ms, rstd = sb("h_ss", [P, 1]), sb("h_ms", [P, 1]), sb("h_rstd", [P, 1])
        o = sb("h_o", [P, 2, D])
        consts, powered = sem("h_consts"), sem("h_powered")
        loaded, stored = [[sem(f"h_{n}{p}") for p in range(2)] for n in ("loaded", "stored")]
        summed, squared, mean, rooted, normed, scaled = [sem("h_" + n) for n in ("summed", "squared", "mean", "rooted", "normed", "scaled")]

        def each(eng, step):
            with eng.Fori(0, NT // 2) as i:
                for p in range(2):
                    step(i, p, 2 * i + p)

        with nc.Block() as block:

            @block.sync
            def _(sp):
                sp.dma_start(ln[:], io["ln_final"].unsqueeze(0).to_broadcast([P, D])).then_inc(consts, 16)

                def step(i, p, t):
                    row, row1, free = sp.snap(t * P), sp.snap(t * P + S), sp.snap(done(t - 2, 2, 2))
                    sp.wait_ge(summed, free)
                    sp.dma_start(x[:, p, 0], scr["x1"][bass.ds(row, P), :]).then_inc(loaded[p], 16)
                    sp.dma_start(x[:, p, 1], scr["y"][bass.ds(row, P), :]).then_inc(loaded[p], 16)
                    sp.dma_start(x[:, p, 2], scr["y"][bass.ds(row1, P), :]).then_inc(loaded[p], 16)
                each(sp, step)

            @block.gpsimd
            def _(pool):
                pool.sem_inc(rooted, 2)
                pool.sem_inc(scaled, 2)
                pool.memset(power[:], -0.5).then_inc(powered, 1)
                pool.wait_ge(powered, 1)
                pool.wait_ge(consts, 16)

                def step(i, p, t):
                    pool.wait_ge(mean, done(t))
                    pool.wait_ge(normed, done(t - 1))
                    pool.tensor_tensor(rstd[:], ms[:], power[:], ALU.pow).then_inc(rooted, 1)
                    pool.wait_ge(normed, done(t))
                    pool.wait_ge(stored[p], landed(i))
                    pool.tensor_tensor(o[:, p], s1[:, p], ln[:], ALU.mult).then_inc(scaled, 1)
                each(pool, step)

            @block.scalar
            def _(act):
                act.sem_inc(squared, 2)
                for p in range(2):
                    act.sem_inc(stored[p], 16)

                def step(i, p, t):
                    act.wait_ge(summed, done(t, 2, 2))
                    act.wait_ge(mean, done(t - 1))
                    act.wait_ge(squared, done(t - 1))
                    act.activation(sq[:], s1[:, p], ACT.Square, accum_out=ss[:]).then_inc(squared, 1)
                    act.wait_ge(scaled, done(t))
                    act.dma_start(out[0, bass.ds(t * P, P), :], o[:, p]).then_inc(stored[p], 16)
                each(act, step)
                for p in range(2):
                    act.wait_ge(stored[p], landed(NT // 2))

            @block.vector
            def _(dve):
                for s, per in ((summed, 2), (mean, 1), (normed, 1)):
                    dve.sem_inc(s, 2 * per)

                def step(i, p, t):
                    dve.wait_ge(loaded[p], 48 * (i + 1))
                    dve.wait_ge(scaled, done(t - 2))
                    dve.tensor_tensor(s1[:, p], x[:, p, 1], x[:, p, 2], ALU.add).then_inc(summed, 1)
                    dve.wait_ge(summed, done(t, 1, 2))
                    dve.tensor_tensor(s1[:, p], s1[:, p], x[:, p, 0], ALU.add).then_inc(summed, 1)
                    dve.wait_ge(squared, done(t))
                    dve.wait_ge(rooted, done(t - 1))
                    dve.tensor_scalar(ms[:], ss[:], 1.0 / D, EPS, ALU.mult, ALU.add).then_inc(mean, 1)
                    dve.wait_ge(rooted, done(t))
                    dve.tensor_scalar(s1[:, p], s1[:, p], rstd[:], None, ALU.mult).then_inc(normed, 1)
                each(dve, step)


INPUTS = ["x", "ln_mix", "w_in", "dn_conv", "dn_A_log", "dn_dt_bias", "dn_norm", "attn_sink", "w_out", "ln_ffn", "w_group", "b_group",
          "w_expert", "b_expert", "w_gate_up", "w_down", "ln_final"]


def kernel(**inputs):
    import concourse.bacc as bacc
    from concourse.bass_utils import run_bass_kernel_spmd

    nc = bacc.Bacc("TRN2", target_bir_lowering=False, num_devices=1)
    arrays = {"in_" + n: np.ascontiguousarray(inputs[n]) for n in INPUTS}
    arrays.update({"in_" + n: a for n, a in TABLES.items()})
    io = {n[3:]: nc.dram_tensor(n, a.shape, mybir.dt.from_np(a.dtype), kind="ExternalInput").ap() for n, a in arrays.items()}
    out = nc.dram_tensor("out", (1, S, D), F32, kind="ExternalOutput").ap()
    program(nc, io, out)
    r = run_bass_kernel_spmd(nc, [arrays], core_ids=[0])
    return r.results[0]["out"]
```

```python
from contextlib import ExitStack

import numpy as np

import concourse.bass as bass
from concourse import mybir

F32 = mybir.dt.float32
I32 = mybir.dt.int32
ALU = mybir.AluOpType
ACT = mybir.ActivationFunctionType
AX = mybir.AxisListType

P = 128
S = 2048
D = 1024
KD = D // P
NT = S // P
EPS = 1e-6

HEADS = 4
DH = 128
DN = HEADS * DH
TAPS = 5
QH = 8
KVH = 2
AD = 64
ROT = AD // 4
HALF = ROT // 2
THETA = 500000.0
WINDOW = 128

QKV = 3 * DN
TOKW = DN + 16 + QH * AD + 2 * KVH * AD
Z0, BA0, Q0 = 0, DN, DN + 16
K0 = Q0 + QH * AD
V0 = K0 + KVH * AD
GROUPS = 3
GW = TOKW // GROUPS

NG = 8
NE = 64
FF = 256
CAP = S
LISTS = NE * CAP
NOWHERE = 1 << 20
BIG = 1.0e30
LEVELS = (2, 3, 4, 5, 6, 7)
TILE = P
MORE = 2 * S // TILE - 1
EARLY = 2
NR = (S - 1) // TILE


def done(t, k=1, per=1):
    return per * (t + 2) + k


def landed(uses):
    return 16 * (uses + 1)


def uses(t, p):
    return 8 * (t - p)


def staged(eng, slot, behind=1):
    there = lambda t: (t, t % 2) if 0 <= t < NT else None
    slot(lambda n: there(-1 + n))
    slot(lambda n: there(n))
    with eng.Fori(0, NT // 2 - 1) as i:
        for q in (1, 2):
            slot(lambda n: (2 * i + q + n, (q + n) % 2))
    for c in range(NT - 1, NT + behind):
        slot(lambda n: there(c + n))



def tables():
    r = np.arange(P)
    row, col = r[:, None], r[None, :]
    square = {
        "eye": row == col, "le": row <= col, "ge": row >= col, "lt": row < col, "gt": row > col,
        "ones": row >= 0 * col,
    }
    for level in (1,) + LEVELS:
        half = 1 << (level - 1)
        same = row // (2 * half) == col // (2 * half)
        low = same & (row // half % 2 == 1) & (col // half % 2 == 0)
        square[f"low{level}"] = low
        square[f"up{level}"] = low.T
    names = list(square)
    tab = np.concatenate([np.broadcast_to(square[n], (P, P)).astype(np.float32) for n in names], 1)
    freq = np.float32(THETA) ** (-np.arange(0, ROT, 2, dtype=np.float32) / ROT)
    ang = np.arange(S, dtype=np.float32)[:, None] * freq[None, :].astype(np.float32)
    trig = np.concatenate([np.cos(ang), np.sin(ang)], 1).astype(np.float32)
    kpos = np.arange(3 * P)[None, :] - P
    qpos = r[:, None]
    band = np.zeros((NT, P, 3 * P), np.float32)
    for n in range(NT):
        bad = (abs(qpos - kpos) > WINDOW) | (kpos + n * P < 0) | (kpos + n * P >= S)
        band[n] = np.where(bad, -BIG, 0.0)
    count = np.concatenate([np.arange(NG, 0, -1), np.arange(NE, 0, -1),
                            np.arange(1, NR + 1) * TILE]).astype(np.float32)
    count = np.broadcast_to(count[None], (P, count.size)).copy()
    token = (np.arange(NT)[None, :] * P + r[:, None]).astype(np.float32)
    token = np.concatenate([token, r[:, None].astype(np.float32)], 1)
    return names, {"tab": tab, "trig": trig, "band": band, "count": count, "token": token}


NAMES, TABLES = tables()


def program(nc, io, out):
    top = ExitStack()
    with top:
        named = []

        def sem(name):
            named.append(nc.alloc_semaphore(name=name))
            return named[-1]

        def recycle():
            nc.clear_and_free_semaphores(named)
            named.clear()
            nc.all_engine_barrier()

        dram = lambda name, shape, dt=F32: nc.dram_tensor(name, shape, dt).ap()
        scr = {
            "tok": dram("s_tok", (S, TOKW)),
            "ch": dram("s_ch", (NT, P, 2, HEADS, DH)),
            "kv": dram("s_kv", (NT, P, 2, HEADS, DH)),
            "o": dram("s_o", (2, S, DN)),
            "attn": dram("s_attn", (S, QH * AD)),
            "x1": dram("s_x1", (S, D)),
            "h2": dram("s_h2", (S, D)),
            "list": dram("s_list", (LISTS + P, 4), I32),
            "items": dram("s_items", (P, 2), I32),
            "y": dram("s_y", (2 * S, D)),
        }
        ps = top.enter_context(nc.psum_tensor("ps", [P, 8, 512], F32))
        with ExitStack() as keep:
            h_all = keep.enter_context(nc.sbuf_tensor("h_all", [P, KD, S], F32))
            project_tokens(nc, io, scr, ps, sem, h_all)
            project_channels(nc, io, scr, ps, sem, h_all)
        delta_net(nc, io, scr, ps, sem)
        recycle()
        attention(nc, io, scr, ps, sem)
        with ExitStack() as keep:
            n_more = keep.enter_context(nc.sbuf_tensor("n_more", [1, 1], I32))
            wgu = [keep.enter_context(nc.sbuf_tensor(f"g_wgu{b}", [P, KD, 2 * FF], F32)) for b in range(EARLY)]
            wd = [keep.enter_context(nc.sbuf_tensor(f"g_wd{b}", [P, FF // P, D], F32)) for b in range(EARLY)]
            early = [(sem(f"g_gu_early{b}"), sem(f"g_d_early{b}")) for b in range(EARLY)]
            mix_and_route(nc, io, scr, ps, sem, n_more, wgu, wd, early)
            experts(nc, io, scr, ps, sem, n_more, wgu, wd, early)
        finish(nc, io, scr, ps, sem, out)




def load_tab(nc, keep, names, prefix):
    t = keep.enter_context(nc.sbuf_tensor(prefix + "_tab", [P, len(names), P], F32))
    return t, {n: t[:, i, :] for i, n in enumerate(names)}


def issue_tab(eng, io, t, names, semaphore):
    for i, n in enumerate(names):
        j = NAMES.index(n)
        eng.dma_start(t[:, i, :], io["tab"][:, j * P:(j + 1) * P]).then_inc(semaphore, 16)
    return 16 * len(names)



def project_tokens(nc, io, scr, ps, sem, h_all):
    with ExitStack() as keep:
        sb = lambda n, s, dt=F32: keep.enter_context(nc.sbuf_tensor(n, s, dt))
        w = sb("a_w", [P, KD, TOKW])
        ln = sb("a_ln", [P, KD])
        eye = sb("a_eye", [P, P])
        x = sb("a_x", [P, 2, D])
        sq = sb("a_sq", [P, D])
        ss = sb("a_ss", [P, 2, 1])
        ms = sb("a_ms", [P, 2, 1])
        rstd = sb("a_rstd", [P, 2, 1])
        xn = sb("a_xn", [P, 2, D])
        hT = sb("a_hT", [P, 2, KD, P])
        o = sb("a_o", [P, 2, TOKW])
        fill = sb("a_fill", [P, P + 1, 2, 4], I32)
        power = sb("a_power", [P, 1])

        consts, w_in = sem("a_consts"), sem("a_w_in")
        x_in = [sem("a_x_in0"), sem("a_x_in1")]
        squared, mean, rooted, normed = sem("a_squared"), sem("a_mean"), sem("a_rooted"), sem("a_normed")
        turned, hT_act, hT_dve, kept = sem("a_turned"), sem("a_hT_act"), sem("a_hT_dve"), sem("a_kept")
        product, out_act, out_dve = sem("a_product"), sem("a_out_act"), sem("a_out_dve")
        stored = [sem("a_stored0"), sem("a_stored1")]
        blank, filled = sem("a_blank"), sem("a_filled")
        turn = [ps[:, b, :].rearrange("p (k t) -> p k t", k=4) for b in (0, 1)]

        def each(eng, step, start=0):
            with eng.Fori(start, NT // 2) as i:
                for p in range(2):
                    step(i, p, 2 * i + p)

        with nc.Block() as block:

            @block.sync
            def _(sp):
                sp.dma_start(ln[:], io["ln_mix"][0].rearrange("(k p) -> p k", p=P), allow_slow_non_contiguous=True).then_inc(consts, 16)
                j = NAMES.index("eye")
                sp.dma_start(eye[:], io["tab"][:, j * P:(j + 1) * P]).then_inc(consts, 16)

                def step(i, p, t):
                    row = t * P if isinstance(t, int) else sp.snap(t * P)
                    sp.wait_ge(squared, done(t - 2))
                    sp.wait_ge(normed, done(t - 2))
                    sp.dma_start(x[:, p, :], io["x"][0, bass.ds(row, P), :]).then_inc(x_in[p], 16)
                for t in range(2):
                    step(0, t, t)
                for k in range(KD):
                    sp.dma_start(w[:, k, :], io["w_in"][0, k * P:(k + 1) * P, QKV:]).then_inc(w_in, 16)
                each(sp, step, 1)
                sp.wait_ge(blank, 2)
                for e in range(8):
                    rows = LISTS // 8
                    sp.dma_start(scr["list"][e * rows:(e + 1) * rows, :].rearrange("(p r) c -> p r c", p=P),
                                 fill[:, 0:P, 0, :]).then_inc(filled, 16)
                sp.dma_start(scr["list"][LISTS:, :], fill[:, P, 0, :]).then_inc(filled, 16)
                sp.wait_ge(filled, 16 * 9)

            @block.gpsimd
            def _(pool):
                pool.memset(power[:], -0.5)
                pool.memset(fill[:], 0).then_inc(blank, 1)
                pool.wait_ge(blank, 1)
                pool.memset(fill[:, :, :, 0:2], NOWHERE).then_inc(blank, 1)
                pool.wait_ge(blank, 2)
                for s in (rooted, kept):
                    pool.sem_inc(s, 2)

                def step(i, p, t):
                    pool.wait_ge(mean, done(t))
                    pool.wait_ge(normed, done(t - 2))
                    pool.tensor_tensor(rstd[:, p, :], ms[:, p, :], power[:], ALU.pow).then_inc(rooted, 1)
                    pool.wait_ge(hT_act, done(t))
                    pool.wait_ge(hT_dve, done(t))
                    pool.tensor_copy(h_all[:, :, bass.ds(t * P, P)], hT[:, p, :, :]).then_inc(kept, 1)
                each(pool, step)

            @block.scalar
            def _(act):
                for s in (squared, hT_act):
                    act.sem_inc(s, 2)
                act.sem_inc(out_act, 4)
                for p in range(2):
                    act.sem_inc(stored[p], 16)
                act.wait_ge(consts, 16 * 2)

                def slot(at):
                    if at(1) is not None:
                        t, p = at(1)
                        act.wait_ge(x_in[p], uses(t, p) + 16)
                        act.wait_ge(squared, done(t - 1))
                        act.wait_ge(mean, done(t - 2))
                        act.activation(sq[:], x[:, p, :], ACT.Square, accum_out=ss[:, p, :]).then_inc(squared, 1)
                        act.wait_ge(turned, done(t, 1, 2))
                        act.wait_ge(product, done(t - 2, 3, 3))
                        act.wait_ge(kept, done(t - 2))
                        for k in range(4):
                            last = act.mul(hT[:, p, k, :], turn[0][:, k, :], ln[:, k:k + 1])
                        last.then_inc(hT_act, 1)
                    if at(0) is None:
                        return
                    t, p = at(0)
                    act.wait_ge(stored[p], uses(t, p) + 16)
                    act.wait_ge(product, done(t, 1, 3))
                    act.activation(o[:, p, 0:GW], ps[:, 2 + 3 * p, 0:GW], ACT.Silu).then_inc(out_act, 1)
                    act.wait_ge(product, done(t, 2, 3))
                    act.activation(o[:, p, GW:DN], ps[:, 3 + 3 * p, 0:DN - GW], ACT.Silu)
                    act.copy(o[:, p, DN:2 * GW], ps[:, 3 + 3 * p, DN - GW:GW]).then_inc(out_act, 1)
                    act.wait_ge(out_act, done(t, 2, 2))
                    act.wait_ge(out_dve, done(t))
                    act.dma_start(scr["tok"][bass.ds(t * P, P), :], o[:, p, :]).then_inc(stored[p], 16)
                staged(act, slot, 0)
                for p in range(2):
                    act.wait_ge(stored[p], landed(NT // 2))

            @block.vector
            def _(dve):
                for s in (mean, normed, hT_dve, out_dve):
                    dve.sem_inc(s, 2)
                dve.wait_ge(consts, 16 * 2)

                def slot(at):
                    if at(1) is not None:
                        t, p = at(1)
                        dve.wait_ge(squared, done(t))
                        dve.wait_ge(rooted, done(t - 2))
                        dve.tensor_scalar(ms[:, p, :], ss[:, p, :], 1.0 / D, EPS, ALU.mult, ALU.add).then_inc(mean, 1)
                        dve.wait_ge(x_in[p], uses(t, p) + 16)
                        dve.wait_ge(rooted, done(t))
                        dve.wait_ge(turned, done(t - 2, 2, 2))
                        dve.tensor_scalar(xn[:, p, :], x[:, p, :], rstd[:, p, :], None, ALU.mult).then_inc(normed, 1)
                        dve.wait_ge(turned, done(t, 2, 2))
                        dve.wait_ge(product, done(t - 2, 3, 3))
                        dve.wait_ge(kept, done(t - 2))
                        for k in range(4):
                            last = dve.tensor_scalar(hT[:, p, 4 + k, :], turn[1][:, k, :], ln[:, 4 + k:5 + k], None, ALU.mult)
                        last.then_inc(hT_dve, 1)
                    if at(0) is not None:
                        t, p = at(0)
                        dve.wait_ge(stored[p], uses(t, p) + 16)
                        dve.wait_ge(product, done(t, 3, 3))
                        dve.tensor_copy(o[:, p, 2 * GW:], ps[:, 2 + 3 * p + 2, 0:GW]).then_inc(out_dve, 1)
                staged(dve, slot, 0)

            @block.tensor
            def _(pe):
                pe.sem_inc(turned, 4)
                pe.sem_inc(product, 6)
                pe.wait_ge(consts, 16 * 2)

                def product_group(t, p, g):
                    for k in range(KD):
                        last = pe.matmul(ps[:, 2 + 3 * p + g, 0:GW], hT[:, p, k, :], w[:, k, g * GW:(g + 1) * GW],
                                         start=(k == 0), stop=(k == KD - 1))
                    last.then_inc(product, 1)

                def slot(at):
                    if at(0) is not None:
                        t, p = at(0)
                        if isinstance(t, int) and t == 0:
                            pe.wait_ge(w_in, 16 * KD)
                        pe.wait_ge(hT_act, done(t))
                        pe.wait_ge(hT_dve, done(t))
                        pe.wait_ge(out_act, done(t - 2, 2, 2))
                        pe.wait_ge(out_dve, done(t - 2))
                        product_group(t, p, 0)
                    if at(1) is not None:
                        t, p = at(1)
                        pe.wait_ge(normed, done(t))
                        for half, evacuated in ((0, hT_act), (1, hT_dve)):
                            pe.wait_ge(evacuated, done(t - 1))
                            for k in range(4):
                                kk = 4 * half + k
                                last = pe.transpose(turn[half][:, k, :], xn[:, p, kk * P:(kk + 1) * P], eye[:])
                            last.then_inc(turned, 1)
                    if at(0) is not None:
                        for g in range(1, GROUPS):
                            product_group(*at(0), g)
                staged(pe, slot, 0)



def project_channels(nc, io, scr, ps, sem, h_all):
    with ExitStack() as keep:
        sb = lambda n, s, dt=F32: keep.enter_context(nc.sbuf_tensor(n, s, dt))
        w = sb("b_w", [P, 3, KD, P])
        taps_in = sb("b_taps_in", [TAPS, QKV])
        taps = sb("b_taps", [P, 3 * HEADS, TAPS])
        eye = sb("b_eye", [P, P])
        raw = sb("b_raw", [P, 3, S + 4])
        act_x = sb("b_act", [P, 3, S])
        tok = sb("b_tok", [P, 3, NT, P])
        sq = sb("b_sq", [P, NT, P])
        ch = sb("b_ch", [P, S])
        ssum = sb("b_ssum", [P, NT])
        ms = sb("b_ms", [P, NT])
        rs = sb("b_rs", [P, NT])
        power = sb("b_power", [P, NT])

        consts, padded, taps_up, taps_out = sem("b_consts"), sem("b_padded"), sem("b_taps_up"), sem("b_taps_out")
        w_in = [sem(f"b_w_in{y}") for y in range(3)]
        product, emptied = sem("b_product"), sem("b_emptied")
        conved, silued = sem("b_conved"), sem("b_silued")
        turned, tok_out = sem("b_turned"), sem("b_tok_out")
        squared, summed, rooted, scaled = sem("b_squared"), sem("b_summed"), sem("b_rooted"), sem("b_scaled")
        back, ch_out = sem("b_back"), sem("b_ch_out")
        tok_stored, ch_stored = [sem(f"b_tok_stored{y}") for y in range(3)], sem("b_ch_stored")
        chain, passed = sem("b_conv_taps"), sem("b_passed")
        QT, KT_, VT = range(3)
        qb = lambda b: ps[:, 4 + b, :].rearrange("p (c t) -> p c t", c=4)

        def each(eng, slot):
            slot((QT, 0), None, None)
            slot((KT_, 0), (QT, 0), None)
            slot((VT, 0), (KT_, 0), (QT, 0))

            def head(h):
                slot((QT, h), (VT, h - 1), (KT_, h - 1))
                slot((KT_, h), (QT, h), (VT, h - 1))
                slot((VT, h), (KT_, h), (QT, h))

            last = HEADS - 1
            with eng.Fori(1, last) as h:
                head(h)
            head(last)
            slot(None, (VT, last), (KT_, last))

        num = lambda item: 3 * item[1] + item[0]

        with nc.Block() as block:

            @block.sync
            def _(sp):
                sp.dma_start(taps_in[:], io["dn_conv"][0]).then_inc(consts, 16)
                j = NAMES.index("eye")
                sp.dma_start(eye[:], io["tab"][:, j * P:(j + 1) * P]).then_inc(consts, 16)
                def load(y, column):
                    src = io["w_in"][0, :, y * DN:(y + 1) * DN].rearrange("(k p) n -> p k n", p=P)
                    sp.dma_start(w[:, y, :, :], src[:, :, bass.ds(column, P)]).then_inc(w_in[y], 16)

                def slot(cur, old, older):
                    if old is None:
                        return
                    y, h = old
                    n = num(old)
                    m = 2 * h + y
                    if cur is not None and not (isinstance(h, int) and h == HEADS - 1):
                        column = (h + 1) * P if isinstance(h, int) else sp.snap((h + 1) * P)
                        sp.wait_ge(product, done(n, 4, 4))
                        load(y, column)
                    if older is not None and older[0] != VT:
                        y2, h2 = older
                        m2 = 2 * h2 + y2
                        head2, ch_is_out = [v if isinstance(v, int) else sp.snap(v) for v in (h2, done(m2, 4, 4))]
                        sp.wait_ge(ch_out, ch_is_out)
                        sp.dma_start(scr["ch"][:, :, 1 - y2, bass.ds(head2, 1), :].rearrange("c p o d -> p c (o d)"),
                                     ch[:].rearrange("p (c d) -> p c d", c=NT)).then_inc(ch_stored, 16)
                    head, tok_is_out, tok_is_scaled = [
                        v if isinstance(v, int) else sp.snap(v) for v in (h, done(n, 4, 4), done(m))]
                    if y != QT:
                        sp.wait_ge(tok_out, tok_is_out)
                        sp.sem_inc(passed, 1)
                        if y == KT_:
                            sp.wait_ge(scaled, tok_is_scaled)
                        sp.sem_inc(passed, 1)
                        sp.dma_start(scr["kv"][:, :, y - 1, bass.ds(head, 1), :].rearrange("c p o d -> p c (o d)"),
                                     tok[:, y]).then_inc(tok_stored[y], 16)
                for s in (tok_stored[KT_], tok_stored[VT], ch_stored):
                    sp.sem_inc(s, 16)
                for y in range(3):
                    load(y, 0)
                each(sp, slot)
                for y in (KT_, VT):
                    sp.wait_ge(tok_stored[y], landed(HEADS))
                sp.wait_ge(ch_stored, landed(2 * HEADS))

            @block.gpsimd
            def _(pool):
                pool.memset(power[:], -0.5)
                pool.memset(raw[:, :, 0:2], 0.0)
                pool.memset(raw[:, :, S + 2:S + 4], 0.0).then_inc(padded, 1)
                pool.wait_ge(padded, 1)
                for s in (squared, scaled):
                    pool.sem_inc(s, 2)
                pool.sem_inc(rooted, 2)

                def slot(cur, old, older):
                    if old is None:
                        return
                    y, h = old
                    n = num(old)
                    m = 2 * h + y
                    pool.wait_ge(tok_out, done(n, 4, 4))
                    if y != VT:
                        pool.wait_ge(summed, done(m - 1, 2, 2))
                        pool.tensor_tensor(sq[:], tok[:, y], tok[:, y], ALU.mult).then_inc(squared, 1)
                        pool.wait_ge(summed, done(m, 2, 2))
                        pool.wait_ge(scaled, done(m - 1))
                        pool.tensor_tensor(rs[:], ms[:], power[:], ALU.pow).then_inc(rooted, 1)
                        pool.wait_ge(rooted, done(m))
                        pool.tensor_tensor(tok[:, y], tok[:, y], rs[:].unsqueeze(2).to_broadcast([P, NT, P]),
                                           ALU.mult).then_inc(scaled, 1)
                        pool.wait_ge(scaled, done(m))
                each(pool, slot)

            @block.scalar
            def _(act):
                act.sem_inc(silued, 2)
                act.sem_inc(emptied, 8)
                act.sem_inc(tok_out, 8)
                act.wait_ge(padded, 1)

                def slot(cur, old, older):
                    if cur is not None:
                        y, h = cur
                        n = num(cur)
                        for q in range(4):
                            act.wait_ge(product, done(n, q + 1, 4))
                            if q == 0:
                                act.wait_ge(conved, done(n - 2))
                            act.copy(raw[:, y, 2 + q * 512:2 + (q + 1) * 512], ps[:, q, :]).then_inc(emptied, 1)
                    if old is not None:
                        y, h = old
                        n = num(old)
                        m = 2 * h + y
                        for q in range(4):
                            act.wait_ge(turned, done(n, q + 1, 4))
                            if q == 0 and y != VT:
                                act.wait_ge(back, done(m - 2, 4, 4))
                            if q == 0 and y != QT:
                                act.wait_ge(tok_stored[y], landed(h))
                            act.copy(tok[:, y, 4 * q:4 * q + 4, :], qb(q)).then_inc(tok_out, 1)
                    if cur is not None:
                        y, h = cur
                        n = num(cur)
                        act.wait_ge(conved, done(n))
                        act.activation(act_x[:, y], act_x[:, y], ACT.Silu).then_inc(silued, 1)
                each(act, slot)

            @block.vector
            def _(dve):
                dve.sem_inc(conved, 2)
                dve.sem_inc(summed, 4)
                dve.sem_inc(ch_out, 8)
                dve.wait_ge(taps_up, 1)
                dve.tensor_copy(taps[:], ps[:, 0, 0:3 * HEADS * 8].rearrange("p (b j) -> p b j", j=8)[:, :, 0:TAPS]).then_inc(taps_out, 1)
                dve.wait_ge(taps_out, 1)

                def slot(cur, old, older):
                    if older is not None and older[0] != VT:
                        y, h = older
                        m = 2 * h + y
                        dve.wait_ge(ch_stored, landed(m))
                        for q in range(4):
                            dve.wait_ge(back, done(m, q + 1, 4))
                            dve.tensor_copy(ch[:, q * 512:(q + 1) * 512], ps[:, 4 + q, :]).then_inc(ch_out, 1)
                    if cur is not None:
                        y, h = cur
                        n = num(cur)
                        dve.wait_ge(emptied, done(n, 4, 4))
                        dve.wait_ge(turned, done(n - 2, 4, 4))
                        b = y * HEADS + h
                        at = (lambda j: taps[:, b:b + 1, j]) if isinstance(b, int) else (lambda j: taps[:, bass.ds(b, 1), j])
                        dve.tensor_scalar(act_x[:, y], raw[:, y, 0:S], at(0), None, ALU.mult).then_inc(chain, 1)
                        for j in range(1, TAPS):
                            dve.wait_ge(chain, (TAPS - 1) * n + j)
                            dve.scalar_tensor_tensor(act_x[:, y], raw[:, y, j:j + S], at(j), act_x[:, y],
                                                     ALU.mult, ALU.add).then_inc(chain if j < TAPS - 1 else conved, 1)
                    if old is not None:
                        y, h = old
                        n = num(old)
                        m = 2 * h + y
                        if y != VT:
                            dve.wait_ge(squared, done(m))
                            dve.wait_ge(rooted, done(m - 1))
                            dve.tensor_reduce(ssum[:], sq[:], AX.X, ALU.add).then_inc(summed, 1)
                            dve.wait_ge(summed, done(m, 1, 2))
                            by = DH if y == QT else 1.0
                            dve.tensor_scalar(ms[:], ssum[:], by, by * EPS, ALU.mult, ALU.add).then_inc(summed, 1)
                each(dve, slot)

            @block.tensor
            def _(pe):
                pe.sem_inc(product, 8)
                pe.sem_inc(turned, 8)
                pe.sem_inc(back, 8)
                pe.wait_ge(consts, 32)
                for b in range(3 * HEADS):
                    last = pe.transpose(ps[:, 0, 8 * b:8 * b + TAPS], taps_in[:, b * P:(b + 1) * P], eye[0:TAPS, 0:TAPS])
                last.then_inc(taps_up, 1)
                pe.wait_ge(taps_out, 1)

                def slot(cur, old, older):
                    def quarter(q):
                        y, h = cur
                        n = num(cur)
                        pe.wait_ge(emptied, done(n - 1, q + 1, 4))
                        for k in range(KD):
                            last = pe.matmul(ps[:, q, :], w[:, y, k, :], h_all[:, k, q * 512:(q + 1) * 512],
                                             start=(k == 0), stop=(k == KD - 1))
                        last.then_inc(product, 1)

                    if cur is not None:
                        pe.wait_ge(w_in[cur[0]], 16 * (cur[1] + 1))
                        for q in range(3):
                            quarter(q)
                    if older is not None and older[0] != VT:
                        y, h = older
                        m = 2 * h + y
                        pe.wait_ge(tok_out, done(num(older), 4, 4))
                        pe.wait_ge(scaled, done(m))
                        for q in range(4):
                            for c in range(4):
                                last = pe.transpose(qb(q)[:, c, :], tok[:, y, 4 * q + c, :], eye[:])
                            last.then_inc(back, 1)
                    if cur is not None:
                        quarter(3)
                    if old is not None:
                        y, h = old
                        n = num(old)
                        m = 2 * h + y
                        pe.wait_ge(silued, done(n))
                        for q in range(4):
                            if y != QT:
                                pe.wait_ge(ch_out, done(m - 1, q + 1, 4))
                            for c in range(4):
                                t = 4 * q + c
                                last = pe.transpose(qb(q)[:, c, :], act_x[:, y, t * P:(t + 1) * P], eye[:])
                            last.then_inc(turned, 1)
                each(pe, slot)



def delta_net(nc, io, scr, ps, sem):
    with ExitStack() as keep:
        sb = lambda n, s, dt=F32: keep.enter_context(nc.sbuf_tensor(n, s, dt))
        DIR = ((0, "low", "up", "gt", "le", "lt"), (1, "up", "low", "lt", "ge", "gt"))
        names = ["eye", "le", "ge", "lt", "gt", "ones"] + [f"{d}{l}" for d in ("low", "up") for l in (1,) + LEVELS]
        tab_t, tab = load_tab(nc, keep, names, "d")
        ba = sb("d_ba", [P, NT, 16])
        dtb = sb("d_dtb", [P, 2 * HEADS])
        alog = sb("d_alog", [P, 2 * HEADS])
        decay_rate = sb("d_rate", [P, 2 * HEADS])
        beta = sb("d_beta", [P, NT, 2 * HEADS])
        g = sb("d_g", [P, NT, 2 * HEADS])
        e1 = sb("d_e1", [P, NT, 16])
        e2 = sb("d_e2", [P, NT, 2 * HEADS])
        eg, ekd, dn, nb, neg = [[sb(f"d_{x}{d}", [P, NT, HEADS]) for d in range(2)] for x in ("eg", "ekd", "dn", "nb", "neg")]
        ch = sb("d_ch", [P, 2, 2, 2, HEADS, DH])
        kv = sb("d_kv", [P, 2, 2, 2, HEADS, DH])
        o = sb("d_o", [P, 2, 2, HEADS, DH])
        four = lambda x: [sb(f"d_{x}{d}", [P, HEADS, P]) for d in range(2)]
        gm, E, E1, NBM, E3, NA, AT, X, R, VN, QS, KD_, ST = [four(x) for x in (
            "gm", "ee", "e_incl", "nb_mask", "e_beta", "na", "at", "x", "r", "vn", "qs", "kd", "state")]
        XT = [four(f"xt{p}_") for p in range(2)]
        pl = [[sb(f"d_p{d}_{l}", [P, HEADS, P]) for l in LEVELS] for d in range(2)]
        bank = lambda d, b: ps[:, 4 * d + b, :].rearrange("p (h t) -> p h t", h=HEADS)
        over = lambda m: m.unsqueeze(1).to_broadcast([P, HEADS, P])

        def side_of(a, l, side):
            half = 1 << (l - 1)
            if len(a.shape) == 3:
                return a.rearrange("p h (b s j) -> p h b s j", s=2, j=half)[:, :, :, side, :]
            return a.rearrange("p (b s j) -> p b s j", s=2, j=half)[:, :, side, :]

        tabs_in, gates_in, step_done, sums_up = sem("d_tabs_in"), sem("d_gates_in"), sem("d_gate_steps"), sem("d_sums_up")
        gate_exp, set_up = sem("d_gate_exp"), sem("d_set_up")
        passed, passed_sp, passed_pool = sem("d_passed"), sem("d_passed_sp"), sem("d_passed_pool")
        ch_in = [[sem(f"d_ch_in{d}{p}") for p in range(2)] for d in range(2)]
        o_stored = [[sem(f"d_o_stored{d}{p}") for p in range(2)] for d in range(2)]

        PE_STEPS = ["decay", "gram", "ks", "turn"] + [f"{x}{l}" for l in LEVELS for x in ("P", "X")] + ["vn", "o", "su"]
        ACT_STEPS = ["exp", "X1"] + [f"X{l}" for l in LEVELS[:-1]]
        POOL_STEPS = ["gm", "nb_mask", "eye", "incl", "kd"]
        DVE_STEPS = ["e3", "na", "xt1", "at", "r", "P2", "XT2", "P3", "XT3", "qs", "P4", "XT4", "P5", "XT5", "P6", "XT6",
                     "P7", "XT7", "vn", "o", "s"]
        pe_did, act_did, pool_did, dve_did = [[sem(f"d_{e}_did{d}") for d in range(2)] for e in ("pe", "act", "pool", "dve")]

        def at(steps, name, t):
            return len(steps) * (t + 2) + steps.index(name) + 1

        pe_at = lambda name, t: at(PE_STEPS, name, t)
        act_at = lambda name, t: at(ACT_STEPS, name, t)
        pool_at = lambda name, t: at(POOL_STEPS, name, t)
        dve_at = lambda name, t: at(DVE_STEPS, name, t)

        def each(eng, step):
            with eng.Fori(0, NT // 2) as i:
                for p in range(2):
                    t = 2 * i + p
                    step(i, p, t, (t, NT - 1 - t))

        with nc.Block() as block:

            @block.sync
            def _(sp):
                n = issue_tab(sp, io, tab_t, names, tabs_in)
                sp.dma_start(ba[:], scr["tok"][:, BA0:BA0 + 16].rearrange("(c p) w -> p c w", p=P)).then_inc(gates_in, 16)
                sp.dma_start(dtb[:], io["dn_dt_bias"].rearrange("a d h -> a (d h)").to_broadcast([P, 2 * HEADS])).then_inc(gates_in, 16)
                sp.dma_start(alog[:], io["dn_A_log"].rearrange("a d h -> a (d h)").to_broadcast([P, 2 * HEADS])).then_inc(gates_in, 16)

                def step(i, p, t, chunk):
                    for d in range(2):
                        c, turned, decayed, summed = [sp.snap(v) for v in (
                            chunk[d], pe_at("o", t - 2), pool_at("kd", t - 2), dve_at("r", t - 2))]
                        sp.wait_ge(pe_did[d], turned)
                        sp.wait_ge(pool_did[d], decayed)
                        sp.wait_ge(dve_did[d], summed)
                        sp.sem_inc(passed_sp, 1)
                        sp.dma_start(ch[:, d, p], scr["ch"][bass.ds(c, 1)].rearrange("o p a h n -> (o p) a h n")).then_inc(ch_in[d][p], 16)
                        sp.dma_start(kv[:, d, p], scr["kv"][bass.ds(c, 1)].rearrange("o p a h n -> (o p) a h n")).then_inc(ch_in[d][p], 16)
                each(sp, step)

            @block.gpsimd
            def _(pool):
                for d in range(2):
                    pool.sem_inc(pool_did[d], 2 * len(POOL_STEPS))
                pool.wait_ge(tabs_in, 16 * len(names))
                for d in range(2):
                    pool.memset(ST[d][:], 0.0).then_inc(set_up, 1)
                pool.wait_ge(step_done, 9)

                gates = lambda a, c: a[:, bass.ds(c, 1), :].rearrange("p o h -> p (o h)").unsqueeze(2).to_broadcast([P, HEADS, P])

                def step(i, p, t, chunk):
                    for d, low, up, gmask, cmask, smask in DIR:
                        c = chunk[d]
                        pool.wait_ge(pe_did[d], pe_at("decay", t - 1))
                        pool.sem_inc(passed_pool, 1)
                        pool.tensor_tensor(gm[d][:], over(tab[gmask]), g[:, bass.ds(c, 1), d * HEADS:(d + 1) * HEADS].rearrange(
                            "p o h -> p (o h)").unsqueeze(2).to_broadcast([P, HEADS, P]), ALU.mult).then_inc(pool_did[d], 1)
                    for d, low, up, gmask, cmask, smask in DIR:
                        pool.wait_ge(dve_did[d], dve_at("e3", t - 1))
                        pool.sem_inc(passed_pool, 1)
                        pool.tensor_tensor(NBM[d][:], over(tab[smask]), gates(nb[d], chunk[d]), ALU.mult).then_inc(pool_did[d], 1)
                    for d in range(2):
                        pool.wait_ge(pe_did[d], pe_at("vn", t - 2))
                        pool.sem_inc(passed_pool, 1)
                        pool.tensor_copy(XT[p][d][:], over(tab["eye"])).then_inc(pool_did[d], 1)
                    for d, low, up, gmask, cmask, smask in DIR:
                        pool.wait_ge(act_did[d], act_at("exp", t))
                        pool.wait_ge(dve_did[d], dve_at("at", t - 1))
                        pool.tensor_tensor(E1[d][:], E[d][:], over(tab[cmask]), ALU.mult).then_inc(pool_did[d], 1)
                    for d in range(2):
                        pool.wait_ge(ch_in[d][p], 32 * (i + 1))
                        pool.wait_ge(pe_did[d], pe_at("su", t - 1))
                        pool.tensor_tensor(KD_[d][:], kv[:, d, p, 0], gates(ekd[d], chunk[d]), ALU.mult).then_inc(pool_did[d], 1)
                each(pool, step)

            @block.scalar
            def _(act):
                for d in range(2):
                    act.sem_inc(act_did[d], 2 * len(ACT_STEPS))
                    for p in range(2):
                        act.sem_inc(o_stored[d][p], 16)
                act.wait_ge(gates_in, 48)
                act.wait_ge(tabs_in, 16 * len(names))
                act.activation(e1[:, :, 0:8], ba[:, :, 0:8], ACT.Exp, scale=-1.0)
                act.activation(decay_rate[:], alog[:], ACT.Exp).then_inc(gate_exp, 1)
                act.wait_ge(step_done, 2)
                act.activation(e1[:, :, 8:16], e2[:], ACT.Exp, scale=-1.0).then_inc(gate_exp, 1)
                act.wait_ge(gate_exp, 2)
                act.activation(e1[:, :, 8:16], e1[:, :, 8:16], ACT.Ln, bias=1.0).then_inc(gate_exp, 1)
                act.wait_ge(sums_up, 1)
                for d in range(2):
                    for n, dst in enumerate((eg, ekd, dn)):
                        act.activation(dst[d][:], ps[:, 0, (3 * d + n) * 64:(3 * d + n + 1) * 64].rearrange("p (c h) -> p c h", h=HEADS),
                                       ACT.Exp).then_inc(gate_exp, 1)

                for pb in pl[1]:
                    act.copy(pb[:], over(tab["eye"])).then_inc(set_up, 1)

                def step(i, p, t, chunk):
                    for d in range(2):
                        act.wait_ge(pe_did[d], pe_at("decay", t))
                        act.wait_ge(pool_did[d], pool_at("incl", t - 1))
                        act.wait_ge(dve_did[d], dve_at("e3", t - 1))
                        act.activation(E[d][:], bank(d, 2), ACT.Exp).then_inc(act_did[d], 1)
                    for d in range(2):
                        act.wait_ge(pe_did[d], pe_at("turn", t))
                        act.copy(X[d][:], bank(d, 0)).then_inc(act_did[d], 1)
                    for l in LEVELS[:-1]:
                        for d in range(2):
                            act.wait_ge(pe_did[d], pe_at(f"X{l}", t))
                            act.copy(side_of(X[d][:], l, d), side_of(bank(d, 0), l, d)).then_inc(act_did[d], 1)
                    for d in range(2):
                        act.wait_ge(dve_did[d], dve_at("o", t))
                        act.dma_start(scr["o"][d, bass.ds(chunk[d] * P, P), :], o[:, d, p].rearrange("p h n -> p (h n)")).then_inc(o_stored[d][p], 16)
                each(act, step)
                for d in range(2):
                    for p in range(2):
                        act.wait_ge(o_stored[d][p], landed(NT // 2))

            @block.vector
            def _(dve):
                for d in range(2):
                    dve.sem_inc(dve_did[d], 2 * len(DVE_STEPS))
                dve.wait_ge(gates_in, 48)
                dve.wait_ge(tabs_in, 16 * len(names))
                a_in = ba[:, :, 8:16]
                across = lambda a: a.unsqueeze(1).to_broadcast([P, NT, 2 * HEADS])
                dve.tensor_tensor(g[:], a_in, across(dtb[:]), ALU.add).then_inc(step_done, 1)
                dve.wait_ge(step_done, 1)
                dve.scalar_tensor_tensor(e2[:], g[:], -1.0, g[:], ALU.mult, ALU.max).then_inc(step_done, 1)
                dve.wait_ge(step_done, 2)
                dve.tensor_scalar(g[:], g[:], 0.0, None, ALU.max).then_inc(step_done, 1)
                dve.wait_ge(gate_exp, 1)
                dve.tensor_scalar(beta[:], e1[:, :, 0:8], 1.0, None, ALU.add).then_inc(step_done, 1)
                dve.wait_ge(step_done, 4)
                dve.reciprocal(beta[:], beta[:]).then_inc(step_done, 1)
                dve.wait_ge(gate_exp, 3)
                dve.tensor_tensor(g[:], g[:], e1[:, :, 8:16], ALU.add).then_inc(step_done, 1)
                dve.wait_ge(step_done, 6)
                dve.scalar_tensor_tensor(g[:], g[:], -1.0, across(decay_rate[:]), ALU.mult, ALU.mult).then_inc(step_done, 1)
                for pb in pl[0]:
                    dve.tensor_copy(pb[:], over(tab["eye"])).then_inc(set_up, 1)
                for d in range(2):
                    dve.tensor_scalar(nb[d][:], beta[:, :, d * HEADS:(d + 1) * HEADS], -1.0, None, ALU.mult).then_inc(step_done, 1)
                dve.wait_ge(gate_exp, 9)
                dve.wait_ge(set_up, 2 * (1 + len(LEVELS)))
                for d in range(2):
                    dve.tensor_scalar(neg[d][:], eg[d][:], -1.0, None, ALU.mult).then_inc(step_done, 1)
                dve.wait_ge(step_done, 11)
                gates = lambda a: a.rearrange("p o h -> p (o h)").unsqueeze(2).to_broadcast([P, HEADS, P])

                def step(i, p, t, chunk):
                    for d, low, up, gmask, cmask, smask in DIR:
                        dve.wait_ge(act_did[d], act_at("exp", t))
                        dve.wait_ge(pool_did[d], pool_at("nb_mask", t))
                        dve.tensor_tensor(E3[d][:], E[d][:], NBM[d][:], ALU.mult).then_inc(dve_did[d], 1)
                        dve.wait_ge(pe_did[d], pe_at("gram", t))
                        dve.wait_ge(dve_did[d], dve_at("e3", t))
                        dve.tensor_tensor(NA[d][:], bank(d, 0), E3[d][:], ALU.mult).then_inc(dve_did[d], 1)
                        dve.wait_ge(dve_did[d], dve_at("na", t))
                        dve.wait_ge(pool_did[d], pool_at("eye", t))
                        dve.sem_inc(passed, 1)
                        dve.copy_predicated(XT[p][d][:], over(tab[up + "1"].bitcast(I32)), NA[d][:]).then_inc(dve_did[d], 1)
                    for d in range(2):
                        dve.wait_ge(pe_did[d], pe_at("gram", t))
                        dve.wait_ge(pool_did[d], pool_at("incl", t))
                        dve.tensor_tensor(AT[d][:], bank(d, 1), E1[d][:], ALU.mult).then_inc(dve_did[d], 1)
                    for d in range(2):
                        c = chunk[d]
                        dve.wait_ge(pe_did[d], pe_at("ks", t))
                        dve.sem_inc(passed, 1)
                        for h in range(HEADS):
                            last = dve.scalar_tensor_tensor(R[d][:, h], bank(d, 3)[:, h], neg[d][:, bass.ds(c, 1), h], kv[:, d, p, 1, h],
                                                            ALU.mult, ALU.add)
                        last.then_inc(dve_did[d], 1)
                    for n, l in enumerate(LEVELS):
                        for d, low, up, gmask, cmask, smask in DIR:
                            mask = side_of(tab[f"{low}{l}"].bitcast(I32), l, d)
                            dve.wait_ge(pe_did[d], pe_at(f"P{l}", t))
                            dve.sem_inc(passed, 1)
                            dve.copy_predicated(side_of(pl[d][n][:], l, d), mask.unsqueeze(1).to_broadcast([P, HEADS] + list(mask.shape[1:])),
                                                side_of(bank(d, 0), l, d)).then_inc(dve_did[d], 1)
                        for d in range(2):
                            dve.wait_ge(pe_did[d], pe_at(f"X{l}", t))
                            dve.tensor_copy(side_of(XT[p][d][:], l, 1 - d), side_of(bank(d, 1), l, 1 - d)).then_inc(dve_did[d], 1)
                        if l == 3:
                            for d in range(2):
                                dve.tensor_tensor(QS[d][:], bank(d, 2), gates(eg[d][:, bass.ds(chunk[d], 1), :]), ALU.mult).then_inc(dve_did[d], 1)
                    for d in range(2):
                        c = chunk[d]
                        dve.wait_ge(pe_did[d], pe_at("vn", t))
                        dve.tensor_tensor(VN[d][:], bank(d, 1), gates(beta[:, bass.ds(c, 1), d * HEADS:(d + 1) * HEADS]),
                                          ALU.mult).then_inc(dve_did[d], 1)
                    for d in range(2):
                        c = chunk[d]
                        dve.wait_ge(pe_did[d], pe_at("o", t))
                        dve.wait_ge(dve_did[d], dve_at("qs", t))
                        dve.wait_ge(o_stored[d][p], landed(i))
                        dve.tensor_tensor(o[:, d, p], QS[d][:], bank(d, 2), ALU.add).then_inc(dve_did[d], 1)
                        dve.wait_ge(pe_did[d], pe_at("su", t))
                        for h in range(HEADS):
                            last = dve.scalar_tensor_tensor(ST[d][:, h], ST[d][:, h], dn[d][:, bass.ds(c, 1), h], bank(d, 3)[:, h],
                                                            ALU.mult, ALU.add)
                        last.then_inc(dve_did[d], 1)
                each(dve, step)

            @block.tensor
            def _(pe):
                for d in range(2):
                    pe.sem_inc(pe_did[d], 2 * len(PE_STEPS))
                pe.wait_ge(tabs_in, 16 * len(names))
                pe.wait_ge(step_done, 9)
                for d, low, up, gmask, cmask, smask in DIR:
                    gd = g[:, :, d * HEADS:(d + 1) * HEADS]
                    for n, mask in enumerate((cmask, gmask, "ones")):
                        last = pe.matmul(ps[:, 0, (3 * d + n) * 64:(3 * d + n + 1) * 64], tab[mask], gd, start=True, stop=True)
                last.then_inc(sums_up, 1)
                pe.wait_ge(gate_exp, 9)
                pe.wait_ge(set_up, 2 * (1 + len(LEVELS)))

                def step(i, p, t, chunk):
                    mm = lambda out, a, b: pe.matmul(out, a, b, start=True, stop=True)
                    for d, low, up, gmask, cmask, smask in DIR:
                        pe.wait_ge(dve_did[d], dve_at("o", t - 1))
                        pe.wait_ge(pool_did[d], pool_at("gm", t))
                        for h in range(HEADS):
                            last = mm(bank(d, 2)[:, h], gm[d][:, h], tab[cmask])
                        last.then_inc(pe_did[d], 1)
                    for d in range(2):
                        pe.wait_ge(ch_in[d][p], 32 * (i + 1))
                        pe.wait_ge(dve_did[d], dve_at("vn", t - 1))
                        for h in range(HEADS):
                            mm(bank(d, 0)[:, h], ch[:, d, p, 0, h], ch[:, d, p, 0, h])
                            last = mm(bank(d, 1)[:, h], ch[:, d, p, 0, h], ch[:, d, p, 1, h])
                        last.then_inc(pe_did[d], 1)
                    for d in range(2):
                        pe.wait_ge(dve_did[d], dve_at("s", t - 1))
                        pe.wait_ge(act_did[d], act_at("exp", t))
                        for h in range(HEADS):
                            mm(bank(d, 3)[:, h], ch[:, d, p, 0, h], ST[d][:, h])
                            last = mm(bank(d, 2)[:, h], ch[:, d, p, 1, h], ST[d][:, h])
                        last.then_inc(pe_did[d], 1)
                    for d in range(2):
                        pe.wait_ge(dve_did[d], dve_at("xt1", t))
                        for h in range(HEADS):
                            last = pe.transpose(bank(d, 0)[:, h], XT[p][d][:, h], tab["eye"])
                        last.then_inc(pe_did[d], 1)
                    for n, l in enumerate(LEVELS):
                        for d in range(2):
                            pe.wait_ge(act_did[d], act_at(f"X{l - 1}", t))
                            for h in range(HEADS):
                                last = mm(bank(d, 0)[:, h], NA[d][:, h], X[d][:, h])
                            last.then_inc(pe_did[d], 1)
                        for d in range(2):
                            pe.wait_ge(dve_did[d], dve_at(f"P{l}", t))
                            for h in range(HEADS):
                                if l < LEVELS[-1]:
                                    mm(bank(d, 0)[:, h], XT[p][d][:, h], pl[d][n][:, h])
                                last = mm(bank(d, 1)[:, h], pl[d][n][:, h], XT[p][d][:, h])
                            last.then_inc(pe_did[d], 1)
                    for d in range(2):
                        pe.wait_ge(dve_did[d], dve_at("XT7", t))
                        for h in range(HEADS):
                            last = mm(bank(d, 1)[:, h], XT[p][d][:, h], R[d][:, h])
                        last.then_inc(pe_did[d], 1)
                    for d in range(2):
                        pe.wait_ge(dve_did[d], dve_at("vn", t))
                        for h in range(HEADS):
                            last = mm(bank(d, 2)[:, h], AT[d][:, h], VN[d][:, h])
                        last.then_inc(pe_did[d], 1)
                        pe.wait_ge(pool_did[d], pool_at("kd", t))
                        for h in range(HEADS):
                            last = mm(bank(d, 3)[:, h], KD_[d][:, h], VN[d][:, h])
                        last.then_inc(pe_did[d], 1)
                each(pe, step)



def lagged(eng, slot):
    slot(0, 0, None)
    with eng.Fori(0, NT // 2 - 1) as i:
        slot(1, 2 * i + 1, 2 * i)
        slot(0, 2 * i + 2, 2 * i + 1)
    slot(1, NT - 1, NT - 2)
    slot(0, None, NT - 1)


def attention(nc, io, scr, ps, sem):
    with ExitStack() as keep:
        sb = lambda n, s, dt=F32: keep.enter_context(nc.sbuf_tensor(n, s, dt))
        HH = QH + KVH
        eye = sb("e_eye", [P, P])
        QB = 4
        qk = sb("e_qk", [P, QB, HH, AD])
        trig = sb("e_trig", [P, QB, 2, HALF])
        rot = sb("e_rot", [P, 4, HH, HALF])
        qkT = sb("e_qkT", [AD, HH, NT + 2, P])
        v = sb("e_v", [P, NT + 2, KVH * AD])
        qT = sb("e_qT", [AD, 2, QH, P])
        band = sb("e_band", [P, 2, 3 * P])
        sink = sb("e_sink", [P, QH])
        sc = sb("e_sc", [P, 2, QH, 3 * P])
        pr = sb("e_pr", [P, QH, 3 * P])
        pT = sb("e_pT", [P, QH, 3, P])
        m = sb("e_m", [P, QH])
        negm = sb("e_negm", [P, QH])
        ds = sb("e_ds", [P, QH])
        es = sb("e_es", [P, QH])
        sums = sb("e_sums", [P, QH])
        den = sb("e_den", [P, 2, QH])
        o = sb("e_o", [P, 2, QH, AD])

        consts, padded, passed = sem("e_consts"), sem("e_padded"), sem("e_passed")
        qk_in = [sem(f"e_qk_in{b}") for b in range(QB)]
        band_in, stored = [[sem(f"e_{x}{p}") for p in range(2)] for x in ("band_in", "stored")]
        multiplied, rotated, turned, all_out = sem("e_multiplied"), sem("e_rotated"), sem("e_turned"), sem("e_all_out")
        q_copied, scored, masked = sem("e_q_copied"), sem("e_scored"), sem("e_masked")
        maxed, sunk, exped, denned = sem("e_maxed"), sem("e_sunk"), sem("e_exped"), sem("e_denned")
        p_turned, pT_act, pT_dve, mixed, o_out = [sem("e_" + x) for x in ("p_turned", "pT_act", "pT_dve", "mixed", "o_out")]

        def each(eng, step):
            with eng.Fori(0, NT // 2) as i:
                for p in range(2):
                    step(i, p, 2 * i + p)

        def each_rotated(eng, prepare, start=0):
            with eng.Fori(start, NT // QB) as i:
                for b in range(QB):
                    prepare(i, b, QB * i + b)

        with nc.Block() as block:

            @block.sync
            def _(sp):
                j = NAMES.index("eye")
                sp.dma_start(eye[:], io["tab"][:, j * P:(j + 1) * P]).then_inc(consts, 16)
                sp.dma_start(sink[:], io["attn_sink"].to_broadcast([P, QH])).then_inc(consts, 16)
                sp.dma_start(v[:, 1:NT + 1, :], scr["tok"][:, V0:V0 + KVH * AD].rearrange("(c p) w -> p c w", p=P)).then_inc(consts, 16)

                def prepare(i, b, t):
                    if isinstance(t, int):
                        row = t * P
                    else:
                        row, free = sp.snap(t * P), sp.snap(done(t - QB))
                        sp.wait_ge(turned, free)
                    sp.dma_start(qk[:, b], scr["tok"][bass.ds(row, P), Q0:V0].rearrange("p (h d) -> p h d", d=AD)).then_inc(qk_in[b], 16)
                    sp.dma_start(trig[:, b], io["trig"][bass.ds(row, P), :].rearrange("p (a f) -> p a f", a=2)).then_inc(qk_in[b], 16)
                for b in range(QB):
                    prepare(0, b, b)
                each_rotated(sp, prepare, 1)

                def step(i, p, t):
                    row, free = sp.snap(t), sp.snap(done(t - 2, QH, QH))
                    sp.wait_ge(masked, free)
                    sp.dma_start(band[:, p], io["band"][bass.ds(row, 1)].rearrange("o p k -> (o p) k")).then_inc(band_in[p], 16)
                each(sp, step)

            @block.gpsimd
            def _(pool):
                pool.sem_inc(q_copied, 2)
                pool.memset(qkT[:, :, 0, :], 0.0)
                pool.memset(qkT[:, :, NT + 1, :], 0.0)
                pool.memset(v[:, 0, :], 0.0)
                pool.memset(v[:, NT + 1, :], 0.0).then_inc(padded, 1)
                pool.wait_ge(all_out, done(NT - 1))

                def step(i, p, t):
                    pool.wait_ge(scored, done(t - 2, QH, QH))
                    pool.tensor_copy(qT[:, p], qkT[:, 0:QH, bass.ds(t + 1, 1), :].rearrange("d h o t -> d h (o t)")).then_inc(q_copied, 1)
                each(pool, step)

            @block.scalar
            def _(act):
                for s, per in ((all_out, 1), (exped, QH + 1), (pT_act, 4)):
                    act.sem_inc(s, 2 * per)
                for p in range(2):
                    act.sem_inc(stored[p], 16)
                act.wait_ge(consts, 48)

                def prepare(i, b, t):
                    act.wait_ge(turned, done(t))
                    for n, (lo, hi) in enumerate(((0, 4), (4, 8), (8, HH))):
                        last = act.copy(qkT[:, lo:hi, bass.ds(t + 1, 1), :].rearrange("d h o t -> d h (o t)"),
                                        ps[0:AD, 4 * (b % 2) + n, 0:(hi - lo) * P].rearrange("d (h t) -> d h t", t=P))
                    last.then_inc(all_out, 1)
                each_rotated(act, prepare)

                def slot(p, t, old):
                    if old is not None:
                        for n, h in enumerate(range(0, QH, 2)):
                            act.wait_ge(p_turned, done(old, h + 1, QH))
                            act.wait_ge(mixed, done(old - 1))
                            act.copy(pT[:, h], ps[:, 4, 0:3 * P].rearrange("k (j q) -> k j q", j=3)).then_inc(pT_act, 1)
                    if t is not None:
                        act.wait_ge(sunk, done(t, 2, 2))
                        act.wait_ge(denned, done(t - 1, 2, 2))
                        act.activation(es[:], ds[:], ACT.Exp).then_inc(exped, 1)
                        act.wait_ge(p_turned, done(t - 1, QH, QH))
                        for h in range(QH):
                            act.activation(pr[:, h], sc[:, p, h], ACT.Exp, bias=negm[:, h:h + 1], accum_out=sums[:, h:h + 1]).then_inc(exped, 1)
                    if old is not None:
                        q = 1 - p
                        act.wait_ge(o_out, done(old))
                        act.dma_start(scr["attn"][bass.ds(old * P, P), :], o[:, q].rearrange("p h d -> p (h d)")).then_inc(stored[q], 16)
                lagged(act, slot)
                for p in range(2):
                    act.wait_ge(stored[p], landed(NT // 2))

            @block.vector
            def _(dve):
                for s, per in ((rotated, 2), (multiplied, 1), (masked, QH), (maxed, 2), (sunk, 2), (denned, 2), (pT_dve, 4), (o_out, 1)):
                    dve.sem_inc(s, 2 * per)
                dve.wait_ge(consts, 48)

                def prepare(i, b, t):
                    dve.wait_ge(qk_in[b], 32 * (i + 1))
                    lo, hi = qk[:, b, :, 0:HALF], qk[:, b, :, HALF:ROT]
                    cos = trig[:, b, 0, :].unsqueeze(1).to_broadcast([P, HH, HALF])
                    sin = trig[:, b, 1, :].unsqueeze(1).to_broadcast([P, HH, HALF])
                    dve.wait_ge(rotated, done(t - 1, 2, 2))
                    for n, (a, f) in enumerate(((lo, cos), (hi, sin), (hi, cos), (lo, sin))):
                        last = dve.tensor_tensor(rot[:, n], a, f, ALU.mult)
                    last.then_inc(multiplied, 1)
                    dve.wait_ge(multiplied, done(t))
                    dve.tensor_tensor(lo, rot[:, 0], rot[:, 1], ALU.subtract).then_inc(rotated, 1)
                    dve.tensor_tensor(hi, rot[:, 2], rot[:, 3], ALU.add).then_inc(rotated, 1)
                each_rotated(dve, prepare)

                def slot(p, t, old):
                    if t is not None:
                        for h in range(QH):
                            dve.wait_ge(scored, done(t, h + 1, QH))
                            if h == 0:
                                dve.wait_ge(band_in[p], uses(t, p) + 16)
                                dve.wait_ge(exped, done(t - 2, QH + 1, QH + 1))
                            dve.scalar_tensor_tensor(sc[:, p, h], ps[:, h % 4, 0:3 * P], AD ** -0.5, band[:, p], ALU.mult, ALU.add).then_inc(masked, 1)
                    if old is not None:
                        q = 1 - p
                        dve.wait_ge(exped, done(old, QH + 1, QH + 1))
                        dve.tensor_tensor(den[:, q], sums[:], es[:], ALU.add).then_inc(denned, 1)
                        dve.wait_ge(denned, done(old, 1, 2))
                        dve.reciprocal(den[:, q], den[:, q]).then_inc(denned, 1)
                        for h in range(1, QH, 2):
                            dve.wait_ge(p_turned, done(old, h + 1, QH))
                            dve.wait_ge(mixed, done(old - 1))
                            dve.tensor_copy(pT[:, h], ps[:, 5, 0:3 * P].rearrange("k (j q) -> k j q", j=3)).then_inc(pT_dve, 1)
                    if t is not None:
                        dve.wait_ge(masked, done(t, QH, QH))
                        dve.tensor_reduce(m[:], sc[:, p], AX.X, ALU.max).then_inc(maxed, 1)
                        dve.wait_ge(maxed, done(t, 1, 2))
                        dve.tensor_tensor(m[:], m[:], sink[:], ALU.max).then_inc(maxed, 1)
                        dve.wait_ge(maxed, done(t, 2, 2))
                        dve.tensor_scalar(negm[:], m[:], -1.0, None, ALU.mult).then_inc(sunk, 1)
                        dve.tensor_tensor(ds[:], sink[:], m[:], ALU.subtract).then_inc(sunk, 1)
                    if old is not None:
                        q = 1 - p
                        dve.wait_ge(mixed, done(old))
                        dve.wait_ge(denned, done(old, 2, 2))
                        dve.wait_ge(stored[q], 8 * (old - q) + 16)
                        dve.tensor_tensor(o[:, q], ps[:, 6, :].rearrange("p (h d) -> p h d", d=AD),
                                          den[:, q, :].unsqueeze(2).to_broadcast([P, QH, AD]), ALU.mult).then_inc(o_out, 1)
                lagged(dve, slot)

            @block.tensor
            def _(pe):
                for s, per in ((turned, 1), (scored, QH), (p_turned, QH), (mixed, 1)):
                    pe.sem_inc(s, 2 * per)
                pe.wait_ge(consts, 48)
                pe.wait_ge(padded, 1)

                def prepare(i, b, t):
                    pe.wait_ge(rotated, done(t, 2, 2))
                    pe.wait_ge(all_out, done(t - 2))
                    pe.sem_inc(passed, 1)
                    for h in range(HH):
                        last = pe.transpose(ps[0:AD, 4 * (b % 2) + h // 4, (h % 4) * P:(h % 4 + 1) * P], qk[:, b, h, :], eye[:])
                    last.then_inc(turned, 1)
                each_rotated(pe, prepare)
                pe.wait_ge(all_out, done(NT - 1))

                def slot(p, t, old):
                    if t is not None:
                        pe.wait_ge(q_copied, done(t))
                        for h in range(QH):
                            pe.wait_ge(masked, done(t, h - 3, QH))
                            pe.sem_inc(passed, 1)
                            kv = QH + h // (QH // KVH)
                            keys = qkT[:, kv, bass.ds(t, 3), :].rearrange("d j t -> d (j t)")
                            pe.matmul(ps[:, h % 4, 0:3 * P], qT[:, p, h, :], keys, start=True, stop=True).then_inc(scored, 1)
                    if old is not None:
                        for h in range(QH):
                            pe.wait_ge(exped, done(old, h + 2, QH + 1))
                            pe.wait_ge(pT_dve if h % 2 else pT_act, done(old, h // 2, 4))
                            for j in range(3):
                                last = pe.transpose(ps[:, 4 + h % 2, j * P:(j + 1) * P], pr[:, h, j * P:(j + 1) * P], eye[:])
                            last.then_inc(p_turned, 1)
                        pe.wait_ge(o_out, done(old - 1))
                        for h in range(QH):
                            pe.wait_ge(pT_dve if h % 2 else pT_act, done(old, h // 2 + 1, 4))
                            kv = h // (QH // KVH)
                            for j in range(3):
                                last = pe.matmul(ps[:, 6, h * AD:(h + 1) * AD], pT[:, h, j, :],
                                                 v[:, bass.ds(old + j, 1), kv * AD:(kv + 1) * AD].rearrange("k o d -> k (o d)"),
                                                 start=(j == 0), stop=(j == 2))
                        last.then_inc(mixed, 1)
                lagged(pe, slot)






def load_expert(sp, io, wgu, wd, expert, signals, free=(None, None)):
    up, down = signals
    if free[0] is not None:
        sp.wait_ge(*free[0])
    sp.dma_start(wgu[:], io["w_gate_up"][0, bass.ds(expert, 1)].rearrange("o (k p) n -> p (o k) n", p=P)).then_inc(up, 16)
    if free[1] is not None:
        sp.wait_ge(*free[1])
    sp.dma_start(wd[:], io["w_down"][0, bass.ds(expert, 1)].rearrange("o (j p) n -> p (o j) n", p=P)).then_inc(down, 16)


def mix_and_route(nc, io, scr, ps, sem, n_more, wgu, wd, early):
    with ExitStack() as keep:
        sb = lambda n, s, dt=F32: keep.enter_context(nc.sbuf_tensor(n, s, dt))
        names = ["eye", "lt", "ones", "le"]
        tab_t, tab = load_tab(nc, keep, names, "f")
        w = sb("f_w", [P, KD, D])
        wr = sb("f_wr", [P, KD, NG + NE])
        bias = sb("f_bias", [P, NG + NE])
        count = sb("f_count", [P, NG + NE + NR])
        token = sb("f_token", [P, NT + 1])
        nw = sb("f_nw", [P, HEADS, DH])
        lnf = sb("f_lnf", [P, D])
        power = sb("f_power", [P, HEADS])
        oo = sb("f_oo", [P, 2, 2, DN])
        za = sb("f_za", [P, 2, 2, DN])
        x = sb("f_x", [P, 2, D])
        mixin = sb("f_mixin", [P, HEADS, DH])
        junk = sb("f_junk", [P, D])
        ssq, ms, rstd = sb("f_ssq", [P, HEADS]), sb("f_ms", [P, HEADS]), sb("f_rstd", [P, HEADS])
        mT = sb("f_mT", [P, 2, KD, P])
        x1 = sb("f_x1", [P, 2, D])
        ss2, ms2, rstd2 = sb("f_ss2", [P, 1]), sb("f_ms2", [P, 1]), sb("f_rstd2", [P, 1])
        h2 = sb("f_h2", [P, 2, D])
        h2T = sb("f_h2T", [P, KD, P])
        lg = sb("f_lg", [P, NT, NG + NE])
        gexp, pick = sb("f_gexp", [P, NT, NG]), sb("f_pick", [P, NT, NG])
        em, score = sb("f_em", [P, NT, NE]), sb("f_score", [P, NT, NE])
        oh = sb("f_oh", [P, 3, NT, NE])
        before_tile = sb("f_before_tile", [P, NT + 1, NE])
        one = {n: sb("f_" + n, [P, NT]) for n in ("gmax", "gfirst", "gsum", "gap", "ratio", "spread")}
        pair = {n: sb("f_" + n, [P, 2, NT]) for n in ("top", "first", "gate", "place", "base")}
        total = sb("f_total", [P, NE])
        exceed, extra, extraT = sb("f_exceed", [P, NE, NR]), sb("f_extra", [P, NE]), sb("f_extraT", [NE, P])
        csum, before, items = sb("f_csum", [P, NE]), sb("f_before", [P, NE]), sb("f_items", [P, 2], I32)
        col = sb("f_col", [P, 5])
        slot_id = sb("f_slot", [P, 2, NT], I32)
        rec = sb("f_rec", [P, 2, NT, 4], I32)

        consts, tabs_in, router_in = sem("f_consts"), sem("f_tabs_in"), sem("f_router_in")
        w_in = [sem(f"f_w_in{half}") for half in range(2)]
        loaded, stored_x, stored_h = [[sem(f"f_{n}{p}") for p in range(2)] for n in ("loaded", "x1_stored", "h2_stored")]
        weighted, osummed, osquared, omean, orooted, odone = [
            sem("f_" + n) for n in ("weighted", "osummed", "osquared", "omean", "orooted", "odone")]
        mturned, mT_out, product, added = [sem("f_" + n) for n in ("mturned", "mT_out", "product", "added")]
        squared, mean, rooted, normed = [sem("f_" + n) for n in ("squared", "mean", "rooted", "normed")]
        hturned, hT_act, hT_dve, logits, logged = [sem("f_" + n) for n in ("hturned", "hT_act", "hT_dve", "logits", "logged")]
        gexped, rexped, routed, counted, scattered = [sem("f_" + n) for n in ("gexped", "rexped", "routed", "counted", "scattered")]
        planned, extra_up, items_out, powered, passed = [
            sem("f_" + n) for n in ("planned", "extra_up", "items_out", "powered", "passed")]
        N8 = count[:, 0:NG].unsqueeze(1).to_broadcast([P, NT, NG])
        N64 = count[:, NG:NG + NE].unsqueeze(1).to_broadcast([P, NT, NE])
        turn = lambda b: ps[:, b, :].rearrange("p (k t) -> p k t", k=4)
        heads = lambda a: a.rearrange("p (h d) -> p h d", h=HEADS)
        LOADS = 16 * 5
        ROUTE = ["none_before", "best", "shift", "ties", "first", "group", "penalty", "masked", "top0", "equal0", "ties0", "first0",
                 "mask0", "drop0", "top1", "equal1", "ties1", "first1", "mask1", "gap", "both"] + [
                 f"counts{t}" for t in range(NT)] + [
                 "gsum", "spread", "gate0", "gate1", "base", "token", "dest0", "dest1", "gates", "spare",
                 "mine0", "place0", "mine1", "place1", "slots", "total"]

        def route_at(name):
            return ROUTE.index(name) + 1

        each = staged

        with nc.Block() as block:

            @block.sync
            def _(sp):
                for h in range(HEADS):
                    sp.dma_start(nw[:, h, :], io["dn_norm"].to_broadcast([P, DH])).then_inc(consts, 16)

                def load(t, p, row):
                    for d in range(2):
                        sp.dma_start(oo[:, p, d], scr["o"][d, bass.ds(row, P), :]).then_inc(loaded[p], 16)
                    sp.dma_start(za[:, p, 0], scr["tok"][bass.ds(row, P), Z0:Z0 + DN]).then_inc(loaded[p], 16)
                    sp.dma_start(za[:, p, 1], scr["attn"][bass.ds(row, P), :]).then_inc(loaded[p], 16)
                    sp.dma_start(x[:, p], io["x"][0, bass.ds(row, P), :]).then_inc(loaded[p], 16)

                load(0, 0, 0)
                issue_tab(sp, io, tab_t, names, tabs_in)
                for half in range(2):
                    cols = slice(half * 512, (half + 1) * 512)
                    sp.dma_start(w[:, :, cols], io["w_out"][0, :, cols].rearrange("(k p) n -> p k n", p=P)).then_inc(w_in[half], 16)
                load(1, 1, P)
                sp.dma_start(lnf[:], io["ln_ffn"].to_broadcast([P, D])).then_inc(router_in, 16)
                sp.dma_start(wr[:, :, 0:NG], io["w_group"][0].rearrange("(k p) n -> p k n", p=P)).then_inc(router_in, 16)
                sp.dma_start(wr[:, :, NG:], io["w_expert"][0].rearrange("(k p) n -> p k n", p=P)).then_inc(router_in, 16)
                sp.dma_start(bias[:, 0:NG], io["b_group"].to_broadcast([P, NG])).then_inc(router_in, 16)
                sp.dma_start(bias[:, NG:], io["b_expert"].to_broadcast([P, NE])).then_inc(router_in, 16)
                sp.dma_start(token[:], io["token"]).then_inc(router_in, 16)
                sp.dma_start(count[:], io["count"]).then_inc(router_in, 16)

                with sp.Fori(1, NT // 2) as i:
                    for p in range(2):
                        t = 2 * i + p
                        row, free = sp.snap(t * P), sp.snap(done(t - 2, 2, 2))
                        sp.wait_ge(mturned, free)
                        sp.wait_ge(added, free)
                        load(t, p, row)

                for b in range(EARLY):
                    load_expert(sp, io, wgu[b], wd[b], b, early[b])
                sp.wait_ge(planned, 13)
                sp.dma_start(scr["items"], items[:]).then_inc(items_out, 16)
                sp.wait_ge(items_out, 16)

            ROUTER = 16 * 7

            @block.gpsimd
            def _(pool):
                for s in (weighted, orooted, rooted):
                    pool.sem_inc(s, 2)
                pool.memset(power[:], -0.5).then_inc(powered, 1)
                pool.wait_ge(powered, 1)
                pool.wait_ge(consts, 16 * HEADS)

                def slot(at):
                    if at(1) is not None:
                        t, p = at(1)
                        pool.wait_ge(loaded[p], 5 * uses(t, p) + LOADS)
                        pool.tensor_tensor(za[:, p, 0], za[:, p, 0], nw[:].rearrange("p h d -> p (h d)"), ALU.mult).then_inc(weighted, 1)
                        pool.wait_ge(omean, done(t))
                        pool.wait_ge(odone, done(t - 1, 2, 2))
                        pool.tensor_tensor(rstd[:], ms[:], power[:], ALU.pow).then_inc(orooted, 1)
                    if at(0) is not None:
                        t, p = at(0)
                        pool.wait_ge(mean, done(t))
                        pool.wait_ge(normed, done(t - 1))
                        pool.tensor_tensor(rstd2[:], ms2[:], power[:, 0:1], ALU.pow).then_inc(rooted, 1)
                each(pool, slot)

                pool.wait_ge(routed, route_at("slots"))
                for t in range(NT):
                    for c in range(2):
                        pool.indirect_dma_start(scr["list"][:, :], bass.IndirectOffsetOnAxis(slot_id[:, c, t:t + 1], 0), rec[:, c, t, :], None,
                                                bounds_check=LISTS - 1, oob_is_err=False).then_inc(scattered, 16)
                pool.wait_ge(scattered, 16 * 2 * NT)

            @block.scalar
            def _(act):
                for s, per in ((osquared, 1), (mT_out, 2), (squared, 1), (hT_act, 1)):
                    act.sem_inc(s, 2 * per)
                for p in range(2):
                    act.sem_inc(stored_x[p], 16)
                    act.sem_inc(stored_h[p], 16)

                def slot(at):
                    if at(1) is not None:
                        t, p = at(1)
                        act.wait_ge(osummed, done(t))
                        act.wait_ge(squared, done(t - 2))
                        act.wait_ge(omean, done(t - 1))
                        for h in range(HEADS):
                            last = act.activation(junk[:, h * DH:(h + 1) * DH], oo[:, p, 0, h * DH:(h + 1) * DH], ACT.Square,
                                                  accum_out=ssq[:, h:h + 1])
                        last.then_inc(osquared, 1)
                        for b in range(2):
                            act.wait_ge(mturned, done(t, b + 1, 2))
                            act.wait_ge(product, done(t - 2, 2, 2))
                            act.copy(mT[:, p, 4 * b:4 * b + 4], turn(b)).then_inc(mT_out, 1)
                    if at(-1) is not None:
                        t, p = at(-1)
                        act.wait_ge(hturned, done(t, 1, 2))
                        act.wait_ge(logits, done(t - 1))
                        act.copy(h2T[:, 0:4], turn(4)).then_inc(hT_act, 1)
                    if at(0) is not None:
                        t, p = at(0)
                        act.wait_ge(added, done(t, 2, 2))
                        act.wait_ge(mean, done(t - 1))
                        if at(1) is not None:
                            act.wait_ge(osquared, done(t + 1))
                        act.activation(junk[:], x1[:, p], ACT.Square, accum_out=ss2[:]).then_inc(squared, 1)
                        act.dma_start(scr["x1"][bass.ds(t * P, P), :], x1[:, p]).then_inc(stored_x[p], 16)
                        act.wait_ge(normed, done(t))
                        act.dma_start(scr["h2"][bass.ds(t * P, P), :], h2[:, p]).then_inc(stored_h[p], 16)
                each(act, slot)
                act.wait_ge(routed, route_at("shift"))
                act.activation(gexp[:], pick[:], ACT.Exp).then_inc(gexped, 1)
                act.wait_ge(routed, route_at("gap"))
                act.activation(one["ratio"][:], one["gap"][:], ACT.Exp).then_inc(rexped, 1)
                for p in range(2):
                    act.wait_ge(stored_x[p], landed(NT // 2))
                    act.wait_ge(stored_h[p], landed(NT // 2))

            @block.vector
            def _(dve):
                for s, per in ((osummed, 1), (omean, 1), (odone, 2), (added, 2), (mean, 1), (normed, 1), (hT_dve, 1), (logged, 1)):
                    dve.sem_inc(s, 2 * per)

                def slot(at):
                    if at(1) is not None:
                        t, p = at(1)
                        dve.wait_ge(loaded[p], 5 * uses(t, p) + LOADS)
                        dve.tensor_tensor(oo[:, p, 0], oo[:, p, 0], oo[:, p, 1], ALU.add).then_inc(osummed, 1)
                        dve.wait_ge(osummed, done(t))
                        dve.wait_ge(weighted, done(t))
                        dve.wait_ge(mturned, done(t - 1, 1, 2))
                        dve.tensor_tensor(mixin[:], heads(oo[:, p, 0]), heads(za[:, p, 0]), ALU.mult).then_inc(odone, 1)
                        dve.wait_ge(osquared, done(t))
                        dve.wait_ge(orooted, done(t - 1))
                        dve.tensor_scalar(ms[:], ssq[:], 1.0 / DH, EPS, ALU.mult, ALU.add).then_inc(omean, 1)
                        dve.wait_ge(orooted, done(t))
                        dve.wait_ge(odone, done(t, 1, 2))
                        dve.tensor_tensor(mixin[:], mixin[:], rstd[:].unsqueeze(2).to_broadcast([P, HEADS, DH]), ALU.mult).then_inc(odone, 1)
                    if at(-1) is not None:
                        t, p = at(-1)
                        dve.wait_ge(hturned, done(t, 2, 2))
                        dve.wait_ge(logits, done(t - 1))
                        dve.tensor_copy(h2T[:, 4:8], turn(5)).then_inc(hT_dve, 1)
                    if at(0) is not None:
                        t, p = at(0)
                        dve.wait_ge(stored_x[p], uses(t, p) + 16)
                        for b in range(2):
                            dve.wait_ge(product, done(t, b + 1, 2))
                            dve.tensor_tensor(x1[:, p, b * 512:(b + 1) * 512], ps[:, 2 + b, :], x[:, p, b * 512:(b + 1) * 512], ALU.add).then_inc(added, 1)
                    if at(-1) is not None:
                        t, p = at(-1)
                        dve.wait_ge(logits, done(t))
                        dve.sem_inc(passed, 1)
                        dve.tensor_tensor(lg[:, bass.ds(t, 1), :].rearrange("p o n -> p (o n)"), ps[:, 6 + p, 0:NG + NE], bias[:], ALU.add).then_inc(logged, 1)
                    if at(0) is not None:
                        t, p = at(0)
                        dve.wait_ge(squared, done(t))
                        dve.wait_ge(rooted, done(t - 1))
                        dve.tensor_scalar(ms2[:], ss2[:], 1.0 / D, EPS, ALU.mult, ALU.add).then_inc(mean, 1)
                        dve.wait_ge(rooted, done(t))
                        dve.wait_ge(added, done(t, 2, 2))
                        dve.wait_ge(stored_h[p], uses(t, p) + 16)
                        dve.wait_ge(hturned, done(t - 2, 2, 2))
                        if isinstance(t, int) and t == 0:
                            dve.wait_ge(router_in, ROUTER)
                        dve.scalar_tensor_tensor(h2[:, p], x1[:, p], rstd2[:], lnf[:], ALU.mult, ALU.mult).then_inc(normed, 1)
                each(dve, slot)

                def then(name, ins):
                    ins.then_inc(routed, 1)
                    dve.wait_ge(routed, route_at(name))

                gl, el = lg[:, :, 0:NG], lg[:, :, NG:]
                top, first, gate, place = [pair[n] for n in ("top", "first", "gate", "place")]
                over_g = lambda a: a.unsqueeze(2).to_broadcast([P, NT, NG])
                over_e = lambda a: a.unsqueeze(2).to_broadcast([P, NT, NE])
                then("none_before", dve.memset(before_tile[:, 0], 0.0))
                dve.wait_ge(logged, done(NT - 1))
                then("best", dve.tensor_reduce(one["gmax"][:], gl, AX.X, ALU.max))
                then("shift", dve.tensor_tensor(pick[:], gl, over_g(one["gmax"][:]), ALU.subtract))
                dve.wait_ge(gexped, 1)
                then("ties", dve.scalar_tensor_tensor(pick[:], pick[:], 0.0, N8, ALU.is_ge, ALU.mult))
                then("first", dve.tensor_reduce(one["gfirst"][:], pick[:], AX.X, ALU.max))
                then("group", dve.tensor_tensor(pick[:], N8, over_g(one["gfirst"][:]), ALU.is_equal))
                then("penalty", dve.tensor_scalar(pick[:], pick[:], -1.0, BIG, ALU.add, ALU.mult))
                then("masked", dve.tensor_tensor(em[:].rearrange("p t (g e) -> p (t g) e", g=NG),
                                                 el.rearrange("p t (g e) -> p t g e", g=NG),
                                                 pick[:].unsqueeze(3).to_broadcast([P, NT, NG, NE // NG]), ALU.add))
                for c in range(2):
                    then(f"top{c}", dve.tensor_reduce(top[:, c], em[:], AX.X, ALU.max))
                    then(f"equal{c}", dve.tensor_tensor(score[:], em[:], over_e(top[:, c]), ALU.is_ge))
                    then(f"ties{c}", dve.tensor_tensor(score[:], score[:], N64, ALU.mult))
                    then(f"first{c}", dve.tensor_reduce(first[:, c], score[:], AX.X, ALU.max))
                    then(f"mask{c}", dve.tensor_tensor(oh[:, c], N64, over_e(first[:, c]), ALU.is_equal))
                    if c == 0:
                        then("drop0", dve.scalar_tensor_tensor(em[:], oh[:, 0], -BIG, em[:], ALU.mult, ALU.add))
                then("gap", dve.tensor_tensor(one["gap"][:], top[:, 1], top[:, 0], ALU.subtract))
                then("both", dve.tensor_tensor(oh[:, 2], oh[:, 0], oh[:, 1], ALU.add))
                for t in range(NT):
                    then(f"counts{t}", dve.tensor_tensor(before_tile[:, t + 1], before_tile[:, t], oh[:, 2, t], ALU.add))
                then("gsum", dve.tensor_reduce(one["gsum"][:], gexp[:], AX.X, ALU.add))
                dve.wait_ge(rexped, 1)
                then("spread", dve.scalar_tensor_tensor(one["spread"][:], one["ratio"][:], 1.0, one["gsum"][:], ALU.add, ALU.mult))
                then("gate0", dve.reciprocal(gate[:, 0], one["spread"][:]))
                then("gate1", dve.tensor_tensor(gate[:, 1], gate[:, 0], one["ratio"][:], ALU.mult))
                then("base", dve.tensor_scalar(pair["base"][:], first[:], float(-CAP), float(LISTS), ALU.mult, ALU.add))
                then("token", dve.tensor_scalar(rec[:, :, :, 0], token[:, 0:NT].unsqueeze(1).to_broadcast([P, 2, NT]), 0.0, None, ALU.add))
                then("dest0", dve.tensor_scalar(rec[:, 0, :, 1], token[:, 0:NT], 0.0, None, ALU.add))
                then("dest1", dve.tensor_scalar(rec[:, 1, :, 1], token[:, 0:NT], float(S), None, ALU.add))
                then("gates", dve.tensor_copy(rec[:].bitcast(F32)[:, :, :, 2], gate[:]))
                then("spare", dve.tensor_scalar(rec[:, :, :, 3], gate[:], 0.0, None, ALU.mult))
                dve.wait_ge(counted, 1)
                for c in range(2):
                    then(f"mine{c}", dve.tensor_tensor(score[:].rearrange("p t e -> p (t e)"), oh[:, c].rearrange("p t e -> p (t e)"),
                                                       ps[:, 0:2, :].rearrange("p b n -> p (b n)"), ALU.mult))
                    then(f"place{c}", dve.tensor_reduce(place[:, c], score[:], AX.X, ALU.add))
                then("slots", dve.tensor_tensor(slot_id[:], pair["base"][:], place[:], ALU.add))
                then("total", dve.tensor_copy(total[:], ps[:, 2, 0:NE]))

                def plan(n, ins):
                    ins.then_inc(planned, 1)
                    dve.wait_ge(planned, n)

                plan(1, dve.tensor_tensor(exceed[:], total[:].unsqueeze(2).to_broadcast([P, NE, NR]),
                                          count[:, NG + NE:].unsqueeze(1).to_broadcast([P, NE, NR]), ALU.is_gt))
                plan(2, dve.tensor_reduce(extra[:], exceed[:], AX.X, ALU.add))
                dve.wait_ge(extra_up, 1)
                plan(3, dve.tensor_copy(extraT[:], ps[0:NE, 3, 0:P]))
                dve.wait_ge(extra_up, 2)
                plan(4, dve.tensor_copy(csum[:], ps[:, 4, 0:NE]))
                k = token[:, NT:NT + 1]
                plan(5, dve.tensor_scalar(before[:], csum[:], k, None, ALU.is_le))
                plan(6, dve.tensor_reduce(col[:, 0:1], before[:], AX.X, ALU.add))
                plan(7, dve.tensor_tensor(csum[:], before[:], extra[:], ALU.mult))
                plan(8, dve.tensor_reduce(col[:, 1:2], csum[:], AX.X, ALU.add))
                plan(9, dve.tensor_tensor(col[:, 2:3], k, col[:, 1:2], ALU.subtract))
                plan(10, dve.tensor_scalar(col[:, 3:4], col[:, 2:3], float(TILE), float(TILE), ALU.mult, ALU.add))
                plan(11, dve.scalar_tensor_tensor(col[:, 4:5], col[:, 0:1], float(CAP), col[:, 3:4], ALU.mult, ALU.add))
                plan(12, dve.tensor_scalar(items[:, 0:1], col[:, 0:1], float(NE - 1), None, ALU.min))
                plan(13, dve.tensor_scalar(items[:, 1:2], col[:, 4:5], float(LISTS), None, ALU.min))
                plan(14, dve.tensor_copy(n_more[:], ps[0:1, 4, NE - 1:NE]))

            @block.tensor
            def _(pe):
                for s, per in ((mturned, 2), (product, 2), (hturned, 2), (logits, 1)):
                    pe.sem_inc(s, 2 * per)
                pe.wait_ge(tabs_in, 16 * len(names))

                def product_half(t, p, b):
                    pe.wait_ge(added, done(t - 1, b + 1, 2))
                    if isinstance(t, int) and t == 0:
                        pe.wait_ge(w_in[b], 16)
                    for k in range(KD):
                        last = pe.matmul(ps[:, 2 + b, :], mT[:, p, k], w[:, k, b * 512:(b + 1) * 512], start=(k == 0), stop=(k == KD - 1))
                    last.then_inc(product, 1)

                def slot(at):
                    if at(0) is not None:
                        t, p = at(0)
                        pe.wait_ge(mT_out, done(t, 2, 2))
                        product_half(t, p, 0)
                    if at(1) is not None:
                        t, p = at(1)
                        pe.wait_ge(odone, done(t, 2, 2))
                        pe.wait_ge(mT_out, done(t - 1, 2, 2))
                        for b in range(2):
                            for k in range(4):
                                src = mixin[:, k] if b == 0 else za[:, p, 1, k * P:(k + 1) * P]
                                last = pe.transpose(turn(b)[:, k], src, tab["eye"])
                            last.then_inc(mturned, 1)
                    if at(-1) is not None:
                        t, p = at(-1)
                        pe.wait_ge(normed, done(t))
                        for b, out_ in ((0, hT_act), (1, hT_dve)):
                            pe.wait_ge(out_, done(t - 1))
                            for k in range(4):
                                last = pe.transpose(turn(4 + b)[:, k], h2[:, p, (4 * b + k) * P:(4 * b + k + 1) * P], tab["eye"])
                            last.then_inc(hturned, 1)
                    if at(0) is not None:
                        product_half(*at(0), 1)
                    if at(-1) is not None:
                        t, p = at(-1)
                        pe.wait_ge(hT_act, done(t))
                        pe.wait_ge(hT_dve, done(t))
                        if isinstance(t, int) and t == 0:
                            pe.wait_ge(router_in, ROUTER)
                        pe.wait_ge(logged, done(t - 2))
                        for k in range(KD):
                            last = pe.matmul(ps[:, 6 + p, 0:NG + NE], h2T[:, k], wr[:, k], start=(k == 0), stop=(k == KD - 1))
                        last.then_inc(logits, 1)
                each(pe, slot)
                pe.wait_ge(routed, route_at(f"counts{NT - 1}"))
                for half in range(2):
                    of = slice(half * NT // 2, (half + 1) * NT // 2)
                    pe.matmul(ps[:, half, :], tab["lt"], oh[:, 2, of], start=True, stop=False)
                    pe.matmul(ps[:, half, :], tab["ones"], before_tile[:, of], start=False, stop=True)
                pe.matmul(ps[:, 2, 0:NE], tab["ones"], before_tile[:, NT], start=True, stop=True).then_inc(counted, 1)
                pe.wait_ge(planned, 2)
                pe.transpose(ps[0:NE, 3, 0:P], extra[:], tab["eye"]).then_inc(extra_up, 1)
                pe.wait_ge(planned, 3)
                pe.matmul(ps[:, 4, 0:NE], extraT[:], tab["le"][0:NE, 0:NE], start=True, stop=True).then_inc(extra_up, 1)



def experts(nc, io, scr, ps, sem, n_more, wgu, wd, early):
    with ExitStack() as keep:
        sb = lambda n, s, dt=F32: keep.enter_context(nc.sbuf_tensor(n, s, dt))
        BUF = 4
        FT = FF // P
        eye = sb("g_eye", [P, P])
        XB = 4
        RB = 8
        wgu = wgu + [sb(f"g_wgu{b}", [P, KD, 2 * FF]) for b in range(EARLY, BUF)]
        wd = wd + [sb(f"g_wd{b}", [P, FT, D]) for b in range(EARLY, BUF)]
        lists = sb("g_lists", [P, NE, 4], I32)
        rec = [sb(f"g_rec{b}", [P, 4], I32) for b in range(RB)]
        xg = [sb(f"g_xg{b}", [P, D]) for b in range(XB)]
        xT = [sb(f"g_xT{b}", [P, KD, TILE]) for b in range(2)]
        sig = sb("g_sig", [P, FT, TILE])
        hid = [sb(f"g_hid{b}", [P, FT, TILE]) for b in range(2)]
        y = [sb(f"g_y{b}", [P, D]) for b in range(2)]
        items = sb("g_items", [1, P, 2], I32)

        consts, lists_in, items_in = sem("g_consts"), sem("g_lists_in"), sem("g_items_in")
        turn = lambda b: ps[:, b, 0:4 * TILE].rearrange("p (k t) -> p k t", k=4)
        up = lambda b: ps[:, 2 + b, 0:4 * TILE].rearrange("p (f t) -> p f t", f=4)
        down = lambda b, n: ps[:, 4 + 2 * b + n, :]

        class Signals:

            def __init__(self, pre):
                s = lambda n: sem(f"g_{pre}_{n}")
                self.gu_in, self.d_in = [s(f"gu_in{b}") for b in range(BUF)], [s(f"d_in{b}") for b in range(BUF)]
                self.listed, self.gathered = s("listed"), [s(f"gathered{b}") for b in range(XB)]
                self.scattered, self.freed = s("scattered"), s("freed")
                self.turned, self.xT_act, self.xT_dve = s("turned"), s("xT_act"), s("xT_dve")
                self.upped, self.sig_act, self.hidden = s("upped"), s("sig_act"), s("hidden")
                self.passed = s("passed")
                self.downed, self.y_act, self.y_dve = s("downed"), s("y_act"), s("y_dve")

        first, more = Signals("first"), Signals("more")
        for b in range(EARLY):
            first.gu_in[b], first.d_in[b] = early[b]


        def weights(sp, s, b, expert, free):
            load_expert(sp, io, wgu[b], wd[b], expert, (s.gu_in[b], s.d_in[b]),
                        ((s.upped, free), (s.downed, free)) if free is not None else (None, None))

        def gather(pool, s, b, rb, t, behind):
            if not isinstance(t, int) or t >= behind:
                pool.wait_ge(s.turned, done(t - behind, 2, 2))
                pool.sem_inc(s.passed, 1)
            pool.indirect_dma_start(xg[b][:], None, scr["h2"][:, :], bass.IndirectOffsetOnAxis(rec[rb][:, 0:1], 0),
                                    bounds_check=S - 1, oob_is_err=False).then_inc(s.gathered[b], 16)

        def landed_scatter(pool, s, t):
            pool.wait_ge(s.scattered, 16 * (t + 1))
            pool.sem_inc(s.freed, 1)

        def scatter(pool, s, rb, b2, t):
            pool.wait_ge(s.y_act, done(t))
            pool.wait_ge(s.y_dve, done(t))
            pool.sem_inc(s.passed, 1)
            pool.indirect_dma_start(scr["y"][:, :], bass.IndirectOffsetOnAxis(rec[rb][:, 1:2], 0), y[b2][:], None,
                                    bounds_check=2 * S - 1, oob_is_err=False).then_inc(s.scattered, 16)

        def act_turn(act, s, b2, t):
            act.wait_ge(s.turned, done(t, 1, 2))
            act.wait_ge(s.upped, done(t - 2))
            act.copy(xT[b2][:, 0:4], turn(0)).then_inc(s.xT_act, 1)

        def act_up(act, s, b2, t):
            act.wait_ge(s.upped, done(t))
            act.wait_ge(s.hidden, done(t - 1))
            act.activation(sig[:], up(b2)[:, 0:FT], ACT.Silu).then_inc(s.sig_act, 1)

        def act_down(act, s, rb, b2, t):
            act.wait_ge(s.downed, done(t))
            act.wait_ge(s.freed, done(t - 2))
            act.mul(y[b2][:, 0:512], down(b2, 0), rec[rb][:].bitcast(F32)[:, 2:3]).then_inc(s.y_act, 1)

        def dve_turn(dve, s, b2, t):
            dve.wait_ge(s.turned, done(t, 2, 2))
            dve.wait_ge(s.upped, done(t - 2))
            dve.tensor_copy(xT[b2][:, 4:8], turn(1)).then_inc(s.xT_dve, 1)

        def dve_up(dve, s, b2, t):
            dve.wait_ge(s.sig_act, done(t))
            dve.wait_ge(s.downed, done(t - 2))
            dve.tensor_tensor(hid[b2][:], up(b2)[:, FT:2 * FT], sig[:], ALU.mult).then_inc(s.hidden, 1)

        def dve_down(dve, s, rb, b2, t):
            dve.wait_ge(s.downed, done(t))
            dve.wait_ge(s.freed, done(t - 2))
            dve.tensor_scalar(y[b2][:, 512:], down(b2, 1), rec[rb][:].bitcast(F32)[:, 2:3], None, ALU.mult).then_inc(s.y_dve, 1)

        def pe_turn(pe, s, b, t, r):
            pe.wait_ge(s.gathered[b], 16 * (r + 1))
            for half, emptied in ((0, s.xT_act), (1, s.xT_dve)):
                pe.wait_ge(emptied, done(t - 1))
                for k in range(4):
                    kk = 4 * half + k
                    last = pe.transpose(turn(half)[:, k], xg[b][0:TILE, kk * P:(kk + 1) * P], eye[0:TILE, 0:TILE])
                last.then_inc(s.turned, 1)

        def pe_up(pe, s, b4, b2, t, r4):
            pe.wait_ge(s.xT_act, done(t))
            pe.wait_ge(s.xT_dve, done(t))
            pe.wait_ge(s.hidden, done(t - 2))
            pe.wait_ge(s.gu_in[b4], 16 * (r4 + 1))
            for f in range(2 * FT):
                for k in range(KD):
                    last = pe.matmul(up(b2)[:, f], wgu[b4][:, k, f * P:(f + 1) * P], xT[b2][:, k], start=(k == 0), stop=(k == KD - 1))
            last.then_inc(s.upped, 1)

        def pe_down(pe, s, b4, b2, t, r4):
            pe.wait_ge(s.hidden, done(t))
            pe.wait_ge(s.y_act, done(t - 2))
            pe.wait_ge(s.y_dve, done(t - 2))
            pe.wait_ge(s.d_in[b4], 16 * (r4 + 1))
            for n in range(2):
                for j in range(FT):
                    last = pe.matmul(down(b2, n), hid[b2][:, j], wd[b4][:, j, n * 512:(n + 1) * 512], start=(j == 0), stop=(j == FT - 1))
            last.then_inc(s.downed, 1)

        def each(eng, slot):
            for c in range(-3, 2):
                slot(lambda n, c=c: tile(c + n))
            with eng.Fori(0, NE // RB - 1) as j:
                for q in range(2, 2 + RB):
                    slot(lambda n: (RB * j + q + n, (q + n) % RB, (q + n) % 4, (q + n) % 2, 2 * j + (q + n) // 4))
            for c in range(NE - RB + 2, NE + 1):
                slot(lambda n, c=c: tile(c + n))

        def tile(t):
            return (t, t % RB, t % 4, t % 2, t // 4) if 0 <= t < NE else None

        def again(eng, body):
            n = eng.value_load(n_more[0:1, 0:1], min_val=0, max_val=MORE)
            with eng.If(n > 0):
                body()

        with nc.Block() as block:

            @block.sync
            def _(sp):
                j = NAMES.index("eye")
                sp.dma_start(eye[:], io["tab"][:, j * P:(j + 1) * P]).then_inc(consts, 16)
                every = scr["list"][0:LISTS, :].rearrange("(e r) c -> r e c", r=CAP)[0:P]
                sp.dma_start(lists[:, 0:RB], every[:, 0:RB]).then_inc(consts, 16)
                sp.dma_start(items[:], scr["items"].unsqueeze(0)).then_inc(items_in, 16)
                sp.wait_ge(first.gathered[2], 16)
                sp.dma_start(lists[:, RB:], every[:, RB:]).then_inc(lists_in, 16)
                for b in range(EARLY, BUF):
                    weights(sp, first, b, b, None)
                with sp.Fori(1, NE // BUF) as j:
                    for b in range(BUF):
                        e, free = sp.snap(BUF * j + b), sp.snap(done(BUF * j + b - BUF))
                        weights(sp, first, b, e, free)

                def body():
                    sp.wait_ge(first.downed, done(NE - 1))
                    sp.wait_ge(items_in, 16)
                    with sp.Fori(0, MORE) as k:
                        e = sp.value_load(items[0:1, bass.ds(k, 1), 0], min_val=0, max_val=NE - 1)
                        free = sp.snap(done(k - 1))
                        weights(sp, more, 0, e, free)
                again(sp, body)

            @block.gpsimd
            def _(pool):
                for s in (first, more):
                    pool.sem_inc(s.freed, 2)
                pool.wait_ge(consts, 32)
                pool.wait_ge(items_in, 16)

                for b in range(XB):
                    pool.memset(xg[b][:], 0.0).then_inc(first.listed, 1)

                def slot(at):
                    if at(3) is not None:
                        t, rb, b, b2, r = at(3)
                        if isinstance(t, int) and t == 4:
                            pool.wait_ge(lists_in, 16)
                        pool.sem_inc(first.passed, 1)
                        pool.tensor_copy(rec[rb][:], lists[:, bass.ds(t, 1), :].rearrange("p o c -> p (o c)")).then_inc(first.listed, 1)
                        pool.wait_ge(first.listed, XB + 1 + t)
                        gather(pool, first, b, rb, t, XB)
                    if at(-2) is not None:
                        landed_scatter(pool, first, at(-2)[0])
                    if at(-1) is not None:
                        t, rb, b, b2, r = at(-1)
                        scatter(pool, first, rb, b2, t)
                each(pool, slot)
                landed_scatter(pool, first, NE - 1)

                def body():
                    pool.wait_ge(items_in, 16)
                    with pool.Fori(0, MORE) as k:
                        row = pool.value_load(items[0:1, bass.ds(k, 1), 1], min_val=0, max_val=LISTS)
                        pool.dma_start(rec[0][:], scr["list"][bass.ds(row, P), :]).then_inc(more.listed, 16)
                        pool.wait_ge(more.listed, 16 * (k + 1))
                        gather(pool, more, 0, 0, k, 1)
                        scatter(pool, more, 0, 0, k)
                        landed_scatter(pool, more, k)
                again(pool, body)

            @block.scalar
            def _(act):
                for s in (first, more):
                    for q in (s.xT_act, s.sig_act, s.y_act):
                        act.sem_inc(q, 2)

                def slot(at):
                    if at(0) is not None:
                        act_up(act, first, at(0)[3], at(0)[0])
                    if at(1) is not None:
                        act_turn(act, first, at(1)[3], at(1)[0])
                    if at(-1) is not None:
                        t, rb, b, b2, r = at(-1)
                        act_down(act, first, rb, b2, t)
                each(act, slot)

                def body():
                    with act.Fori(0, MORE) as k:
                        act_turn(act, more, 0, k)
                        act_up(act, more, 0, k)
                        act_down(act, more, 0, 0, k)
                again(act, body)

            @block.vector
            def _(dve):
                for s in (first, more):
                    for q, per in ((s.xT_dve, 1), (s.hidden, 1), (s.y_dve, 1)):
                        dve.sem_inc(q, 2 * per)

                def slot(at):
                    if at(0) is not None:
                        dve_up(dve, first, at(0)[3], at(0)[0])
                    if at(1) is not None:
                        dve_turn(dve, first, at(1)[3], at(1)[0])
                    if at(-1) is not None:
                        t, rb, b, b2, r = at(-1)
                        dve_down(dve, first, rb, b2, t)
                each(dve, slot)

                def body():
                    with dve.Fori(0, MORE) as k:
                        dve_turn(dve, more, 0, k)
                        dve_up(dve, more, 0, k)
                        dve_down(dve, more, 0, 0, k)
                again(dve, body)

            @block.tensor
            def _(pe):
                for s in (first, more):
                    for q, per in ((s.turned, 2), (s.upped, 1), (s.downed, 1)):
                        pe.sem_inc(q, 2 * per)
                pe.wait_ge(consts, 32)

                def slot(at):
                    if at(0) is not None:
                        t, rb, b, b2, r = at(0)
                        pe_up(pe, first, b, b2, t, r)
                    if at(1) is not None:
                        t, rb, b, b2, r = at(1)
                        pe_turn(pe, first, b, t, r)
                    if at(-1) is not None:
                        t, rb, b, b2, r = at(-1)
                        pe_down(pe, first, b, b2, t, r)
                each(pe, slot)

                def body():
                    with pe.Fori(0, MORE) as k:
                        pe_turn(pe, more, 0, k, k)
                        pe_up(pe, more, 0, 0, k, k)
                        pe_down(pe, more, 0, 0, k, k)
                again(pe, body)



def finish(nc, io, scr, ps, sem, out):
    with ExitStack() as keep:
        sb = lambda n, s, dt=F32: keep.enter_context(nc.sbuf_tensor(n, s, dt))
        ln = sb("h_ln", [P, D])
        x = sb("h_x", [P, 2, 3, D])
        s1 = sb("h_sum", [P, 2, D])
        sq = sb("h_sq", [P, D])
        power = sb("h_power", [P, 1])
        ss, ms, rstd = sb("h_ss", [P, 1]), sb("h_ms", [P, 1]), sb("h_rstd", [P, 1])
        o = sb("h_o", [P, 2, D])
        consts, powered = sem("h_consts"), sem("h_powered")
        loaded, stored = [[sem(f"h_{n}{p}") for p in range(2)] for n in ("loaded", "stored")]
        summed, squared, mean, rooted, normed, scaled = [sem("h_" + n) for n in ("summed", "squared", "mean", "rooted", "normed", "scaled")]

        def each(eng, step):
            with eng.Fori(0, NT // 2) as i:
                for p in range(2):
                    step(i, p, 2 * i + p)

        with nc.Block() as block:

            @block.sync
            def _(sp):
                sp.dma_start(ln[:], io["ln_final"].unsqueeze(0).to_broadcast([P, D])).then_inc(consts, 16)

                def step(i, p, t):
                    row, row1, free = sp.snap(t * P), sp.snap(t * P + S), sp.snap(done(t - 2, 2, 2))
                    sp.wait_ge(summed, free)
                    sp.dma_start(x[:, p, 0], scr["x1"][bass.ds(row, P), :]).then_inc(loaded[p], 16)
                    sp.dma_start(x[:, p, 1], scr["y"][bass.ds(row, P), :]).then_inc(loaded[p], 16)
                    sp.dma_start(x[:, p, 2], scr["y"][bass.ds(row1, P), :]).then_inc(loaded[p], 16)
                each(sp, step)

            @block.gpsimd
            def _(pool):
                pool.sem_inc(rooted, 2)
                pool.sem_inc(scaled, 2)
                pool.memset(power[:], -0.5).then_inc(powered, 1)
                pool.wait_ge(powered, 1)
                pool.wait_ge(consts, 16)

                def step(i, p, t):
                    pool.wait_ge(mean, done(t))
                    pool.wait_ge(normed, done(t - 1))
                    pool.tensor_tensor(rstd[:], ms[:], power[:], ALU.pow).then_inc(rooted, 1)
                    pool.wait_ge(normed, done(t))
                    pool.wait_ge(stored[p], landed(i))
                    pool.tensor_tensor(o[:, p], s1[:, p], ln[:], ALU.mult).then_inc(scaled, 1)
                each(pool, step)

            @block.scalar
            def _(act):
                act.sem_inc(squared, 2)
                for p in range(2):
                    act.sem_inc(stored[p], 16)

                def step(i, p, t):
                    act.wait_ge(summed, done(t, 2, 2))
                    act.wait_ge(mean, done(t - 1))
                    act.wait_ge(squared, done(t - 1))
                    act.activation(sq[:], s1[:, p], ACT.Square, accum_out=ss[:]).then_inc(squared, 1)
                    act.wait_ge(scaled, done(t))
                    act.dma_start(out[0, bass.ds(t * P, P), :], o[:, p]).then_inc(stored[p], 16)
                each(act, step)
                for p in range(2):
                    act.wait_ge(stored[p], landed(NT // 2))

            @block.vector
            def _(dve):
                for s, per in ((summed, 2), (mean, 1), (normed, 1)):
                    dve.sem_inc(s, 2 * per)

                def step(i, p, t):
                    dve.wait_ge(loaded[p], 48 * (i + 1))
                    dve.wait_ge(scaled, done(t - 2))
                    dve.tensor_tensor(s1[:, p], x[:, p, 1], x[:, p, 2], ALU.add).then_inc(summed, 1)
                    dve.wait_ge(summed, done(t, 1, 2))
                    dve.tensor_tensor(s1[:, p], s1[:, p], x[:, p, 0], ALU.add).then_inc(summed, 1)
                    dve.wait_ge(squared, done(t))
                    dve.wait_ge(rooted, done(t - 1))
                    dve.tensor_scalar(ms[:], ss[:], 1.0 / D, EPS, ALU.mult, ALU.add).then_inc(mean, 1)
                    dve.wait_ge(rooted, done(t))
                    dve.tensor_scalar(s1[:, p], s1[:, p], rstd[:], None, ALU.mult).then_inc(normed, 1)
                each(dve, step)


INPUTS = ["x", "ln_mix", "w_in", "dn_conv", "dn_A_log", "dn_dt_bias", "dn_norm", "attn_sink", "w_out", "ln_ffn", "w_group", "b_group",
          "w_expert", "b_expert", "w_gate_up", "w_down", "ln_final"]


def kernel(**inputs):
    import concourse.bacc as bacc
    from concourse.bass_utils import run_bass_kernel_spmd

    nc = bacc.Bacc("TRN2", target_bir_lowering=False, num_devices=1)
    arrays = {"in_" + n: np.ascontiguousarray(inputs[n]) for n in INPUTS}
    arrays.update({"in_" + n: a for n, a in TABLES.items()})
    io = {n[3:]: nc.dram_tensor(n, a.shape, mybir.dt.from_np(a.dtype), kind="ExternalInput").ap() for n, a in arrays.items()}
    out = nc.dram_tensor("out", (1, S, D), F32, kind="ExternalOutput").ap()
    program(nc, io, out)
    r = run_bass_kernel_spmd(nc, [arrays], core_ids=[0])
    return r.results[0]["out"]
```

```python
from contextlib import ExitStack

import numpy as np

import concourse.bass as bass
from concourse import mybir

F32 = mybir.dt.float32
F32R = mybir.dt.float32r
I32 = mybir.dt.int32
ALU = mybir.AluOpType
ACT = mybir.ActivationFunctionType
AX = mybir.AxisListType

P = 128
S = 2048
D = 1024
KD = D // P
NT = S // P
EPS = 1e-6

HEADS = 4
DH = 128
DN = HEADS * DH
TAPS = 5
QH = 8
KVH = 2
AD = 64
ROT = AD // 4
HALF = ROT // 2
THETA = 500000.0
WINDOW = 128

QKV = 3 * DN
TOKW = DN + 16 + QH * AD + 2 * KVH * AD
Z0, BA0, Q0 = 0, DN, DN + 16
K0 = Q0 + QH * AD
V0 = K0 + KVH * AD
GROUPS = 3
GW = TOKW // GROUPS

NG = 8
NE = 64
FF = 256
CAP = S
LISTS = NE * CAP
NOWHERE = 1 << 20
BIG = 1.0e30
LEVELS = (2, 3, 4, 5, 6, 7)
TILE = P
MORE = 2 * S // TILE - 1
NR = (S - 1) // TILE


def done(t, k=1, per=1):
    return per * (t + 2) + k


def landed(uses):
    return 16 * (uses + 1)


def uses(t, p):
    return 8 * (t - p)


def staged(eng, slot, behind=1):
    there = lambda t: (t, t % 2) if 0 <= t < NT else None
    start = max(behind, 1)
    pairs = (NT - 1 - start) // 2
    for c in range(-1, start):
        slot(lambda n: there(c + n))
    with eng.Fori(0, pairs) as i:
        for q in (start, start + 1):
            slot(lambda n: (2 * i + q + n, (q + n) % 2))
    for c in range(start + 2 * pairs, NT + behind):
        slot(lambda n: there(c + n))



def tables():
    r = np.arange(P)
    row, col = r[:, None], r[None, :]
    square = {
        "eye": row == col, "le": row <= col, "ge": row >= col, "lt": row < col, "gt": row > col,
        "ones": row >= 0 * col,
    }
    for level in (1,) + LEVELS:
        half = 1 << (level - 1)
        same = row // (2 * half) == col // (2 * half)
        low = same & (row // half % 2 == 1) & (col // half % 2 == 0)
        square[f"low{level}"] = low
        square[f"up{level}"] = low.T
    names = list(square)
    tab = np.concatenate([np.broadcast_to(square[n], (P, P)).astype(np.float32) for n in names], 1)
    freq = np.float32(THETA) ** (-np.arange(0, ROT, 2, dtype=np.float32) / ROT)
    ang = np.arange(S, dtype=np.float32)[:, None] * freq[None, :].astype(np.float32)
    trig = np.concatenate([np.cos(ang), np.sin(ang)], 1).astype(np.float32)
    kpos = np.arange(3 * P)[None, :] - P
    qpos = r[:, None]
    band = np.zeros((NT, P, 3 * P), np.float32)
    for n in range(NT):
        bad = (abs(qpos - kpos) > WINDOW) | (kpos + n * P < 0) | (kpos + n * P >= S)
        band[n] = np.where(bad, -BIG, 0.0)
    count = np.concatenate([np.arange(NG, 0, -1), np.arange(NE, 0, -1),
                            np.arange(1, NR + 1) * TILE]).astype(np.float32)
    count = np.broadcast_to(count[None], (P, count.size)).copy()
    token = (np.arange(NT)[None, :] * P + r[:, None]).astype(np.float32)
    token = np.concatenate([token, r[:, None].astype(np.float32)], 1)
    return names, {"tab": tab, "trig": trig, "band": band, "count": count, "token": token}


NAMES, TABLES = tables()


def program(nc, io, out):
    top = ExitStack()
    with top:
        named = []

        def sem(name):
            named.append(nc.alloc_semaphore(name=name))
            return named[-1]

        def recycle():
            nc.clear_and_free_semaphores(named)
            named.clear()
            nc.all_engine_barrier()

        dram = lambda name, shape, dt=F32: nc.dram_tensor(name, shape, dt).ap()
        scr = {
            "tok": dram("s_tok", (S, TOKW)),
            "ch": dram("s_ch", (NT, P, 2, HEADS, DH)),
            "kv": dram("s_kv", (NT, P, 2, HEADS, DH)),
            "o": dram("s_o", (2, S, DN)),
            "attn": dram("s_attn", (S, QH * AD)),
            "x1": dram("s_x1", (S, D)),
            "h2": dram("s_h2", (S, D)),
            "list": dram("s_list", (LISTS + P, 4), I32),
            "items": dram("s_items", (P, 2), I32),
            "y": dram("s_y", (2 * S, D)),
        }
        ps = top.enter_context(nc.psum_tensor("ps", [P, 8, 512], F32))
        with ExitStack() as keep:
            h_all = keep.enter_context(nc.sbuf_tensor("h_all", [P, KD, S], F32))
            project_tokens(nc, io, scr, ps, sem, h_all)
            project_channels(nc, io, scr, ps, sem, h_all)
        delta_net(nc, io, scr, ps, sem)
        recycle()
        attention(nc, io, scr, ps, sem)
        with ExitStack() as keep:
            n_more = keep.enter_context(nc.sbuf_tensor("n_more", [1, 1], I32))
            mix_and_route(nc, io, scr, ps, sem, n_more)
            experts(nc, io, scr, ps, sem, n_more)
        finish(nc, io, scr, ps, sem, out)




def load_tab(nc, keep, names, prefix):
    t = keep.enter_context(nc.sbuf_tensor(prefix + "_tab", [P, len(names), P], F32))
    return t, {n: t[:, i, :] for i, n in enumerate(names)}


def issue_tab(eng, io, t, names, semaphore):
    for i, n in enumerate(names):
        j = NAMES.index(n)
        eng.dma_start(t[:, i, :], io["tab"][:, j * P:(j + 1) * P]).then_inc(semaphore, 16)
    return 16 * len(names)



def project_tokens(nc, io, scr, ps, sem, h_all):
    with ExitStack() as keep:
        sb = lambda n, s, dt=F32: keep.enter_context(nc.sbuf_tensor(n, s, dt))
        w_lead, w_rest = sb("a_w_lead", [P, KD, TOKW], F32R), sb("a_w_rest", [P, KD, TOKW], F32R)
        w_raw = h_all[:, :, S - TOKW:]
        ln = sb("a_ln", [P, KD])
        eye = sb("a_eye", [P, P])
        x = sb("a_x", [P, 2, D])
        ss = sb("a_ss", [P, 2, 1])
        ms = sb("a_ms", [P, 2, 1])
        rstd = sb("a_rstd", [P, 2, 1])
        xn = sb("a_xn", [P, 2, D])
        hT_lead, hT_rest = sb("a_hT_lead", [P, 2, KD, P], F32R), sb("a_hT_rest", [P, 2, KD, P], F32R)
        o = sb("a_o", [P, 2, TOKW])
        fill = sb("a_fill", [P, P + 1, 2, 4], I32)
        power = sb("a_power", [P, 1])

        consts, w_in = sem("a_consts"), [sem(f"a_w_in{g}") for g in range(GROUPS)]
        x_in = [sem("a_x_in0"), sem("a_x_in1")]
        squared, mean, rooted, normed = sem("a_squared"), sem("a_mean"), sem("a_rooted"), sem("a_normed")
        turned, h_act, h_dve, led, rest = [sem("a_" + n) for n in ("turned", "h_act", "h_dve", "led", "rest")]
        w_led, w_split, passed = sem("a_w_led"), sem("a_w_split"), sem("a_passed")
        product, out_act, out_dve = sem("a_product"), sem("a_out_act"), sem("a_out_dve")
        stored = [sem("a_stored0"), sem("a_stored1")]
        blank, filled = sem("a_blank"), sem("a_filled")
        turn = [ps[:, b, :].rearrange("p (k t) -> p k t", k=4) for b in (0, 1)]

        def each(eng, step, start=0):
            with eng.Fori(start, NT // 2) as i:
                for p in range(2):
                    step(i, p, 2 * i + p)

        with nc.Block() as block:

            @block.sync
            def _(sp):
                sp.dma_start(ln[:], io["ln_mix"][0].rearrange("(k p) -> p k", p=P), allow_slow_non_contiguous=True).then_inc(consts, 16)
                j = NAMES.index("eye")
                sp.dma_start(eye[:], io["tab"][:, j * P:(j + 1) * P]).then_inc(consts, 16)

                def step(i, p, t):
                    row = t * P if isinstance(t, int) else sp.snap(t * P)
                    sp.wait_ge(squared, done(t - 2))
                    sp.wait_ge(normed, done(t - 2))
                    sp.dma_start(x[:, p, :], io["x"][0, bass.ds(row, P), :]).then_inc(x_in[p], 16)
                for t in range(2):
                    step(0, t, t)
                for g in range(GROUPS):
                    src = io["w_in"][0, :, QKV + g * GW:QKV + (g + 1) * GW].rearrange("(k p) n -> p k n", p=P)
                    sp.dma_start(w_raw[:, :, g * GW:(g + 1) * GW], src).then_inc(w_in[g], 16)
                sp.wait_ge(blank, 2)
                rows = LISTS // (NT // 2)

                def empty(i):
                    sp.dma_start(scr["list"][bass.ds(i * rows, rows), :].rearrange("(p r) c -> p r c", p=P),
                                 fill[:, 0:P, 0, :]).then_inc(filled, 16)

                empty(0)
                sp.dma_start(scr["list"][LISTS:, :], fill[:, P, 0, :]).then_inc(filled, 16)
                with sp.Fori(1, NT // 2) as i:
                    for p in range(2):
                        step(i, p, 2 * i + p)
                    empty(i)
                sp.wait_ge(filled, 16 * 9)

            @block.gpsimd
            def _(pool):
                pool.memset(power[:], -0.5)
                pool.memset(fill[:], 0).then_inc(blank, 1)
                pool.wait_ge(blank, 1)
                pool.memset(fill[:, :, :, 0:2], NOWHERE).then_inc(blank, 1)
                pool.wait_ge(blank, 2)
                pool.sem_inc(rooted, 2)

                def step(i, p, t):
                    pool.wait_ge(mean, done(t))
                    pool.wait_ge(normed, done(t - 2))
                    pool.tensor_tensor(rstd[:, p, :], ms[:, p, :], power[:], ALU.pow).then_inc(rooted, 1)
                each(pool, step)

            @block.scalar
            def _(act):
                for s in (squared, h_act, led):
                    act.sem_inc(s, 2)
                act.sem_inc(out_act, 4)
                for p in range(2):
                    act.sem_inc(stored[p], 16)
                act.wait_ge(consts, 16 * 2)

                def slot(at):
                    if at(1) is not None:
                        t, p = at(1)
                        act.wait_ge(x_in[p], uses(t, p) + 16)
                        act.wait_ge(squared, done(t - 1))
                        act.wait_ge(mean, done(t - 2))
                        act.wait_ge(turned, done(t - 2, 2, 2))
                        act.activation(xn[:, p, :], x[:, p, :], ACT.Square, accum_out=ss[:, p, :]).then_inc(squared, 1)
                        act.wait_ge(turned, done(t, 1, 2))
                        for k in range(4):
                            last = act.mul(h_all[:, k, bass.ds(t * P, P)], turn[0][:, k, :], ln[:, k:k + 1])
                        last.then_inc(h_act, 1)
                        act.wait_ge(h_act, done(t))
                        act.wait_ge(h_dve, done(t))
                        act.wait_ge(product, done(t - 2, 3, 3))
                        act.sem_inc(passed, 1)
                        act.copy(hT_lead[:, p], h_all[:, :, bass.ds(t * P, P)]).then_inc(led, 1)
                    if at(0) is None:
                        for g in range(GROUPS):
                            of = slice(g * GW, (g + 1) * GW)
                            act.wait_ge(w_in[g], 16)
                            act.copy(w_lead[:, :, of], w_raw[:, :, of]).then_inc(w_led, 1)
                        act.wait_ge(w_split, GROUPS)
                        return
                    t, p = at(0)
                    act.wait_ge(stored[p], uses(t, p) + 16)
                    act.wait_ge(product, done(t, 1, 3))
                    act.activation(o[:, p, 0:GW], ps[:, 2 + 3 * p, 0:GW], ACT.Silu).then_inc(out_act, 1)
                    act.wait_ge(product, done(t, 2, 3))
                    act.activation(o[:, p, GW:DN], ps[:, 3 + 3 * p, 0:DN - GW], ACT.Silu)
                    act.copy(o[:, p, DN:2 * GW], ps[:, 3 + 3 * p, DN - GW:GW]).then_inc(out_act, 1)
                    act.wait_ge(out_act, done(t, 2, 2))
                    act.wait_ge(out_dve, done(t))
                    act.dma_start(scr["tok"][bass.ds(t * P, P), :], o[:, p, :]).then_inc(stored[p], 16)
                staged(act, slot, 0)
                for p in range(2):
                    act.wait_ge(stored[p], landed(NT // 2))

            @block.vector
            def _(dve):
                for s in (mean, normed, h_dve, rest, out_dve):
                    dve.sem_inc(s, 2)
                dve.wait_ge(consts, 16 * 2)

                def slot(at):
                    if at(1) is not None:
                        t, p = at(1)
                        dve.wait_ge(squared, done(t))
                        dve.wait_ge(rooted, done(t - 2))
                        dve.tensor_scalar(ms[:, p, :], ss[:, p, :], 1.0 / D, EPS, ALU.mult, ALU.add).then_inc(mean, 1)
                        dve.wait_ge(x_in[p], uses(t, p) + 16)
                        dve.wait_ge(rooted, done(t))
                        dve.wait_ge(turned, done(t - 2, 2, 2))
                        dve.tensor_scalar(xn[:, p, :], x[:, p, :], rstd[:, p, :], None, ALU.mult).then_inc(normed, 1)
                        dve.wait_ge(turned, done(t, 2, 2))
                        for k in range(4):
                            last = dve.tensor_scalar(h_all[:, 4 + k, bass.ds(t * P, P)], turn[1][:, k, :], ln[:, 4 + k:5 + k], None, ALU.mult)
                        last.then_inc(h_dve, 1)
                        dve.wait_ge(led, done(t))
                        dve.wait_ge(product, done(t - 2, 3, 3))
                        dve.tensor_tensor(hT_rest[:, p], h_all[:, :, bass.ds(t * P, P)], hT_lead[:, p].bitcast(F32), ALU.subtract).then_inc(rest, 1)
                    if at(0) is None:
                        for g in range(GROUPS):
                            of = slice(g * GW, (g + 1) * GW)
                            dve.wait_ge(w_led, g + 1)
                            dve.tensor_tensor(w_rest[:, :, of], w_raw[:, :, of], w_lead[:, :, of].bitcast(F32), ALU.subtract).then_inc(w_split, 1)
                    if at(0) is not None:
                        t, p = at(0)
                        dve.wait_ge(stored[p], uses(t, p) + 16)
                        dve.wait_ge(product, done(t, 3, 3))
                        dve.tensor_copy(o[:, p, 2 * GW:], ps[:, 2 + 3 * p + 2, 0:GW]).then_inc(out_dve, 1)
                staged(dve, slot, 0)

            @block.tensor
            def _(pe):
                pe.sem_inc(turned, 4)
                pe.sem_inc(product, 6)
                pe.wait_ge(consts, 16 * 2)

                def product_group(t, p, g):
                    if isinstance(t, int) and t == 0:
                        pe.wait_ge(w_split, g + 1)
                    of = slice(g * GW, (g + 1) * GW)
                    for k in range(KD):
                        pe.matmul(ps[:, 2 + 3 * p + g, 0:GW], hT_lead[:, p, k, :], w_lead[:, k, of], start=(k == 0), stop=False)
                        pe.matmul(ps[:, 2 + 3 * p + g, 0:GW], hT_lead[:, p, k, :], w_rest[:, k, of], start=False, stop=False)
                        last = pe.matmul(ps[:, 2 + 3 * p + g, 0:GW], hT_rest[:, p, k, :], w_lead[:, k, of], start=False, stop=(k == KD - 1))
                    last.then_inc(product, 1)

                def slot(at):
                    if at(0) is not None:
                        t, p = at(0)
                        pe.wait_ge(led, done(t))
                        pe.wait_ge(rest, done(t))
                        pe.wait_ge(out_act, done(t - 2, 2, 2))
                        pe.wait_ge(out_dve, done(t - 2))
                        product_group(t, p, 0)
                    if at(1) is not None:
                        t, p = at(1)
                        pe.wait_ge(normed, done(t))
                        for half, evacuated in ((0, h_act), (1, h_dve)):
                            pe.wait_ge(evacuated, done(t - 1))
                            for k in range(4):
                                kk = 4 * half + k
                                last = pe.transpose(turn[half][:, k, :], xn[:, p, kk * P:(kk + 1) * P], eye[:])
                            last.then_inc(turned, 1)
                    if at(0) is not None:
                        for g in range(1, GROUPS):
                            product_group(*at(0), g)
                staged(pe, slot, 0)



def project_channels(nc, io, scr, ps, sem, h_all):
    with ExitStack() as keep:
        sb = lambda n, s, dt=F32: keep.enter_context(nc.sbuf_tensor(n, s, dt))
        w = sb("b_w", [P, 3, KD, P])
        taps_in = sb("b_taps_in", [TAPS, QKV])
        taps = sb("b_taps", [P, 3 * HEADS, TAPS])
        eye = sb("b_eye", [P, P])
        raw = sb("b_raw", [P, 3, S + 4])
        act_x = sb("b_act", [P, 3, S])
        tok = sb("b_tok", [P, 3, NT, P])
        sq = sb("b_sq", [P, NT, P])
        ch = sb("b_ch", [P, S])
        ssum = sb("b_ssum", [P, NT])
        ms = sb("b_ms", [P, NT])
        rs = sb("b_rs", [P, NT])
        power = sb("b_power", [P, NT])

        consts, padded, taps_up, taps_out = sem("b_consts"), sem("b_padded"), sem("b_taps_up"), sem("b_taps_out")
        w_in = [sem(f"b_w_in{y}") for y in range(3)]
        product, emptied = sem("b_product"), sem("b_emptied")
        conved, silued = sem("b_conved"), sem("b_silued")
        turned, tok_out = sem("b_turned"), sem("b_tok_out")
        squared, summed, rooted, scaled = sem("b_squared"), sem("b_summed"), sem("b_rooted"), sem("b_scaled")
        back, ch_out = sem("b_back"), sem("b_ch_out")
        tok_stored, ch_stored = [sem(f"b_tok_stored{y}") for y in range(3)], sem("b_ch_stored")
        chain, passed = sem("b_conv_taps"), sem("b_passed")
        QT, KT_, VT = range(3)
        qb = lambda b: ps[:, 4 + b, :].rearrange("p (c t) -> p c t", c=4)

        def each(eng, slot):
            slot((QT, 0), None, None)
            slot((KT_, 0), (QT, 0), None)
            slot((VT, 0), (KT_, 0), (QT, 0))

            def head(h):
                slot((QT, h), (VT, h - 1), (KT_, h - 1))
                slot((KT_, h), (QT, h), (VT, h - 1))
                slot((VT, h), (KT_, h), (QT, h))

            last = HEADS - 1
            with eng.Fori(1, last) as h:
                head(h)
            head(last)
            slot(None, (VT, last), (KT_, last))

        num = lambda item: 3 * item[1] + item[0]

        with nc.Block() as block:

            @block.sync
            def _(sp):
                sp.dma_start(taps_in[:], io["dn_conv"][0]).then_inc(consts, 16)
                j = NAMES.index("eye")
                sp.dma_start(eye[:], io["tab"][:, j * P:(j + 1) * P]).then_inc(consts, 16)
                def load(y, column):
                    src = io["w_in"][0, :, y * DN:(y + 1) * DN].rearrange("(k p) n -> p k n", p=P)
                    sp.dma_start(w[:, y, :, :], src[:, :, bass.ds(column, P)]).then_inc(w_in[y], 16)

                def slot(cur, old, older):
                    if old is None:
                        return
                    y, h = old
                    n = num(old)
                    m = 2 * h + y
                    if cur is not None and not (isinstance(h, int) and h == HEADS - 1):
                        column = (h + 1) * P if isinstance(h, int) else sp.snap((h + 1) * P)
                        sp.wait_ge(product, done(n, 4, 4))
                        load(y, column)
                    if older is not None and older[0] != VT:
                        y2, h2 = older
                        m2 = 2 * h2 + y2
                        head2, ch_is_out = [v if isinstance(v, int) else sp.snap(v) for v in (h2, done(m2, 4, 4))]
                        sp.wait_ge(ch_out, ch_is_out)
                        sp.dma_start(scr["ch"][:, :, 1 - y2, bass.ds(head2, 1), :].rearrange("c p o d -> p c (o d)"),
                                     ch[:].rearrange("p (c d) -> p c d", c=NT)).then_inc(ch_stored, 16)
                    head, tok_is_out, tok_is_scaled = [
                        v if isinstance(v, int) else sp.snap(v) for v in (h, done(n, 4, 4), done(m))]
                    if y != QT:
                        sp.wait_ge(tok_out, tok_is_out)
                        sp.sem_inc(passed, 1)
                        if y == KT_:
                            sp.wait_ge(scaled, tok_is_scaled)
                        sp.sem_inc(passed, 1)
                        sp.dma_start(scr["kv"][:, :, y - 1, bass.ds(head, 1), :].rearrange("c p o d -> p c (o d)"),
                                     tok[:, y]).then_inc(tok_stored[y], 16)
                for s in (tok_stored[KT_], tok_stored[VT], ch_stored):
                    sp.sem_inc(s, 16)
                for y in range(3):
                    load(y, 0)
                each(sp, slot)
                for y in (KT_, VT):
                    sp.wait_ge(tok_stored[y], landed(HEADS))
                sp.wait_ge(ch_stored, landed(2 * HEADS))

            @block.gpsimd
            def _(pool):
                pool.memset(power[:], -0.5)
                pool.memset(raw[:, :, 0:2], 0.0)
                pool.memset(raw[:, :, S + 2:S + 4], 0.0).then_inc(padded, 1)
                pool.wait_ge(padded, 1)
                for s in (squared, scaled):
                    pool.sem_inc(s, 2)
                pool.sem_inc(rooted, 2)

                def slot(cur, old, older):
                    if old is None:
                        return
                    y, h = old
                    n = num(old)
                    m = 2 * h + y
                    pool.wait_ge(tok_out, done(n, 4, 4))
                    if y != VT:
                        pool.wait_ge(summed, done(m - 1, 2, 2))
                        pool.tensor_tensor(sq[:], tok[:, y], tok[:, y], ALU.mult).then_inc(squared, 1)
                        pool.wait_ge(summed, done(m, 2, 2))
                        pool.wait_ge(scaled, done(m - 1))
                        pool.tensor_tensor(rs[:], ms[:], power[:], ALU.pow).then_inc(rooted, 1)
                        pool.wait_ge(rooted, done(m))
                        pool.tensor_tensor(tok[:, y], tok[:, y], rs[:].unsqueeze(2).to_broadcast([P, NT, P]),
                                           ALU.mult).then_inc(scaled, 1)
                        pool.wait_ge(scaled, done(m))
                each(pool, slot)

            @block.scalar
            def _(act):
                act.sem_inc(silued, 2)
                act.sem_inc(emptied, 8)
                act.sem_inc(tok_out, 8)
                act.wait_ge(padded, 1)

                def slot(cur, old, older):
                    if cur is not None:
                        y, h = cur
                        n = num(cur)
                        for q in range(4):
                            act.wait_ge(product, done(n, q + 1, 4))
                            if q == 0:
                                act.wait_ge(conved, done(n - 2))
                            act.copy(raw[:, y, 2 + q * 512:2 + (q + 1) * 512], ps[:, q, :]).then_inc(emptied, 1)
                    if old is not None:
                        y, h = old
                        n = num(old)
                        m = 2 * h + y
                        for q in range(4):
                            act.wait_ge(turned, done(n, q + 1, 4))
                            if q == 0 and y != VT:
                                act.wait_ge(back, done(m - 2, 4, 4))
                            if q == 0 and y != QT:
                                act.wait_ge(tok_stored[y], landed(h))
                            act.copy(tok[:, y, 4 * q:4 * q + 4, :], qb(q)).then_inc(tok_out, 1)
                    if cur is not None:
                        y, h = cur
                        n = num(cur)
                        act.wait_ge(conved, done(n))
                        act.activation(act_x[:, y], act_x[:, y], ACT.Silu).then_inc(silued, 1)
                each(act, slot)

            @block.vector
            def _(dve):
                dve.sem_inc(conved, 2)
                dve.sem_inc(summed, 4)
                dve.sem_inc(ch_out, 8)
                dve.wait_ge(taps_up, 1)
                dve.tensor_copy(taps[:], ps[:, 0, 0:3 * HEADS * 8].rearrange("p (b j) -> p b j", j=8)[:, :, 0:TAPS]).then_inc(taps_out, 1)
                dve.wait_ge(taps_out, 1)

                def slot(cur, old, older):
                    if older is not None and older[0] != VT:
                        y, h = older
                        m = 2 * h + y
                        dve.wait_ge(ch_stored, landed(m))
                        for q in range(4):
                            dve.wait_ge(back, done(m, q + 1, 4))
                            dve.tensor_copy(ch[:, q * 512:(q + 1) * 512], ps[:, 4 + q, :]).then_inc(ch_out, 1)
                    if cur is not None:
                        y, h = cur
                        n = num(cur)
                        dve.wait_ge(emptied, done(n, 4, 4))
                        dve.wait_ge(turned, done(n - 2, 4, 4))
                        b = y * HEADS + h
                        at = (lambda j: taps[:, b:b + 1, j]) if isinstance(b, int) else (lambda j: taps[:, bass.ds(b, 1), j])
                        dve.tensor_scalar(act_x[:, y], raw[:, y, 0:S], at(0), None, ALU.mult).then_inc(chain, 1)
                        for j in range(1, TAPS):
                            dve.wait_ge(chain, (TAPS - 1) * n + j)
                            dve.scalar_tensor_tensor(act_x[:, y], raw[:, y, j:j + S], at(j), act_x[:, y],
                                                     ALU.mult, ALU.add).then_inc(chain if j < TAPS - 1 else conved, 1)
                    if old is not None:
                        y, h = old
                        n = num(old)
                        m = 2 * h + y
                        if y != VT:
                            dve.wait_ge(squared, done(m))
                            dve.wait_ge(rooted, done(m - 1))
                            dve.tensor_reduce(ssum[:], sq[:], AX.X, ALU.add).then_inc(summed, 1)
                            dve.wait_ge(summed, done(m, 1, 2))
                            by = DH if y == QT else 1.0
                            dve.tensor_scalar(ms[:], ssum[:], by, by * EPS, ALU.mult, ALU.add).then_inc(summed, 1)
                each(dve, slot)

            @block.tensor
            def _(pe):
                pe.sem_inc(product, 8)
                pe.sem_inc(turned, 8)
                pe.sem_inc(back, 8)
                pe.wait_ge(consts, 32)
                for b in range(3 * HEADS):
                    last = pe.transpose(ps[:, 0, 8 * b:8 * b + TAPS], taps_in[:, b * P:(b + 1) * P], eye[0:TAPS, 0:TAPS])
                last.then_inc(taps_up, 1)
                pe.wait_ge(taps_out, 1)

                def slot(cur, old, older):
                    def quarter(q):
                        y, h = cur
                        n = num(cur)
                        pe.wait_ge(emptied, done(n - 1, q + 1, 4))
                        for k in range(KD):
                            last = pe.matmul(ps[:, q, :], w[:, y, k, :], h_all[:, k, q * 512:(q + 1) * 512],
                                             start=(k == 0), stop=(k == KD - 1))
                        last.then_inc(product, 1)

                    if cur is not None:
                        pe.wait_ge(w_in[cur[0]], 16 * (cur[1] + 1))
                        for q in range(3):
                            quarter(q)
                    if older is not None and older[0] != VT:
                        y, h = older
                        m = 2 * h + y
                        pe.wait_ge(tok_out, done(num(older), 4, 4))
                        pe.wait_ge(scaled, done(m))
                        for q in range(4):
                            for c in range(4):
                                last = pe.transpose(qb(q)[:, c, :], tok[:, y, 4 * q + c, :], eye[:])
                            last.then_inc(back, 1)
                    if cur is not None:
                        quarter(3)
                    if old is not None:
                        y, h = old
                        n = num(old)
                        m = 2 * h + y
                        pe.wait_ge(silued, done(n))
                        for q in range(4):
                            if y != QT:
                                pe.wait_ge(ch_out, done(m - 1, q + 1, 4))
                            for c in range(4):
                                t = 4 * q + c
                                last = pe.transpose(qb(q)[:, c, :], act_x[:, y, t * P:(t + 1) * P], eye[:])
                            last.then_inc(turned, 1)
                each(pe, slot)


def delta_net(nc, io, scr, ps, sem):
    with ExitStack() as keep:
        sb = lambda n, s, dt=F32: keep.enter_context(nc.sbuf_tensor(n, s, dt))
        DIR = ((0, "low", "up", "gt", "le", "lt"), (1, "up", "low", "lt", "ge", "gt"))
        tab_t, tab = load_tab(nc, keep, NAMES, "d")
        ba = sb("d_ba", [P, NT, 16])
        dtb = sb("d_dtb", [P, 2 * HEADS])
        alog = sb("d_alog", [P, 2 * HEADS])
        decay_rate = sb("d_rate", [P, 2 * HEADS])
        beta = sb("d_beta", [P, NT, 2 * HEADS])
        g = sb("d_g", [P, NT, 2 * HEADS])
        e1 = sb("d_e1", [P, NT, 16])
        e2 = sb("d_e2", [P, NT, 2 * HEADS])
        eg, ekd, dn, nb, neg = [[sb(f"d_{x}{d}", [P, NT, HEADS]) for d in range(2)] for x in ("eg", "ekd", "dn", "nb", "neg")]
        ch = sb("d_ch", [P, 2, 2, 2, HEADS, DH])
        kv = sb("d_kv", [P, 2, 2, 2, HEADS, DH])
        o = sb("d_o", [P, 2, 2, HEADS, DH])
        four = lambda x: [sb(f"d_{x}{d}", [P, HEADS, P]) for d in range(2)]
        gm, E, E1, NBM, E3, NA, AT, X, R, VN, QS, KD_, ST = [four(x) for x in (
            "gm", "ee", "e_incl", "nb_mask", "e_beta", "na", "at", "x", "r", "vn", "qs", "kd", "state")]
        XT = [four(f"xt{p}_") for p in range(2)]
        pl = [[sb(f"d_p{d}_{l}", [P, HEADS, P]) for l in LEVELS] for d in range(2)]
        bank = lambda d, b: ps[:, 4 * d + b, :].rearrange("p (h t) -> p h t", h=HEADS)
        over = lambda m: m.unsqueeze(1).to_broadcast([P, HEADS, P])

        def side_of(a, l, side):
            half = 1 << (l - 1)
            if len(a.shape) == 3:
                return a.rearrange("p h (b s j) -> p h b s j", s=2, j=half)[:, :, :, side, :]
            return a.rearrange("p (b s j) -> p b s j", s=2, j=half)[:, :, side, :]

        tabs_in, gates_in, step_done, sums_up = sem("d_tabs_in"), sem("d_gates_in"), sem("d_gate_steps"), sem("d_sums_up")
        gate_exp, set_up = sem("d_gate_exp"), sem("d_set_up")
        passed, passed_sp, passed_pool = sem("d_passed"), sem("d_passed_sp"), sem("d_passed_pool")
        ch_in = [[sem(f"d_ch_in{d}{p}") for p in range(2)] for d in range(2)]
        o_stored = [[sem(f"d_o_stored{d}{p}") for p in range(2)] for d in range(2)]

        PE_STEPS = ["decay", "gram", "ks", "turn"] + [f"{x}{l}" for l in LEVELS for x in ("P", "X")] + ["vn", "o", "su"]
        ACT_STEPS = ["exp", "X1"] + [f"X{l}" for l in LEVELS[:-1]]
        POOL_STEPS = ["gm", "nb_mask", "eye", "incl", "kd"]
        DVE_STEPS = ["e3", "na", "xt1", "at", "r", "P2", "XT2", "P3", "XT3", "qs", "P4", "XT4", "P5", "XT5", "P6", "XT6",
                     "P7", "XT7", "vn", "o", "s"]
        pe_did, act_did, pool_did, dve_did = [[sem(f"d_{e}_did{d}") for d in range(2)] for e in ("pe", "act", "pool", "dve")]

        def at(steps, name, t):
            return len(steps) * (t + 2) + steps.index(name) + 1

        pe_at = lambda name, t: at(PE_STEPS, name, t)
        act_at = lambda name, t: at(ACT_STEPS, name, t)
        pool_at = lambda name, t: at(POOL_STEPS, name, t)
        dve_at = lambda name, t: at(DVE_STEPS, name, t)

        def each(eng, step):
            with eng.Fori(0, NT // 2) as i:
                for p in range(2):
                    t = 2 * i + p
                    step(i, p, t, (t, NT - 1 - t))

        with nc.Block() as block:

            @block.sync
            def _(sp):
                sp.dma_start(ba[:], scr["tok"][:, BA0:BA0 + 16].rearrange("(c p) w -> p c w", p=P)).then_inc(gates_in, 16)
                sp.dma_start(dtb[:], io["dn_dt_bias"].rearrange("a d h -> a (d h)").to_broadcast([P, 2 * HEADS])).then_inc(gates_in, 16)
                sp.dma_start(alog[:], io["dn_A_log"].rearrange("a d h -> a (d h)").to_broadcast([P, 2 * HEADS])).then_inc(gates_in, 16)
                sp.dma_start(tab_t[:].rearrange("p n c -> p (n c)"), io["tab"]).then_inc(tabs_in, 16)

                def step(i, p, t, chunk):
                    for d in range(2):
                        c, turned, decayed, summed = [sp.snap(v) for v in (
                            chunk[d], pe_at("o", t - 2), pool_at("kd", t - 2), dve_at("r", t - 2))]
                        sp.wait_ge(pe_did[d], turned)
                        sp.wait_ge(pool_did[d], decayed)
                        sp.wait_ge(dve_did[d], summed)
                        sp.sem_inc(passed_sp, 1)
                        sp.dma_start(ch[:, d, p], scr["ch"][bass.ds(c, 1)].rearrange("o p a h n -> (o p) a h n")).then_inc(ch_in[d][p], 16)
                        sp.dma_start(kv[:, d, p], scr["kv"][bass.ds(c, 1)].rearrange("o p a h n -> (o p) a h n")).then_inc(ch_in[d][p], 16)
                each(sp, step)

            @block.gpsimd
            def _(pool):
                for d in range(2):
                    pool.sem_inc(pool_did[d], 2 * len(POOL_STEPS))
                pool.wait_ge(tabs_in, 16)
                for d in range(2):
                    pool.memset(ST[d][:], 0.0).then_inc(set_up, 1)
                pool.wait_ge(step_done, 9)

                gates = lambda a, c: a[:, bass.ds(c, 1), :].rearrange("p o h -> p (o h)").unsqueeze(2).to_broadcast([P, HEADS, P])

                def step(i, p, t, chunk):
                    for d, low, up, gmask, cmask, smask in DIR:
                        c = chunk[d]
                        pool.wait_ge(pe_did[d], pe_at("decay", t - 1))
                        pool.sem_inc(passed_pool, 1)
                        pool.tensor_tensor(gm[d][:], over(tab[gmask]), g[:, bass.ds(c, 1), d * HEADS:(d + 1) * HEADS].rearrange(
                            "p o h -> p (o h)").unsqueeze(2).to_broadcast([P, HEADS, P]), ALU.mult).then_inc(pool_did[d], 1)
                    for d, low, up, gmask, cmask, smask in DIR:
                        pool.wait_ge(dve_did[d], dve_at("e3", t - 1))
                        pool.sem_inc(passed_pool, 1)
                        pool.tensor_tensor(NBM[d][:], over(tab[smask]), gates(nb[d], chunk[d]), ALU.mult).then_inc(pool_did[d], 1)
                    for d in range(2):
                        pool.wait_ge(pe_did[d], pe_at("vn", t - 2))
                        pool.sem_inc(passed_pool, 1)
                        pool.tensor_copy(XT[p][d][:], over(tab["eye"])).then_inc(pool_did[d], 1)
                    for d, low, up, gmask, cmask, smask in DIR:
                        pool.wait_ge(act_did[d], act_at("exp", t))
                        pool.wait_ge(dve_did[d], dve_at("at", t - 1))
                        pool.tensor_tensor(E1[d][:], E[d][:], over(tab[cmask]), ALU.mult).then_inc(pool_did[d], 1)
                    for d in range(2):
                        pool.wait_ge(ch_in[d][p], 32 * (i + 1))
                        pool.wait_ge(pe_did[d], pe_at("su", t - 1))
                        pool.tensor_tensor(KD_[d][:], kv[:, d, p, 0], gates(ekd[d], chunk[d]), ALU.mult).then_inc(pool_did[d], 1)
                each(pool, step)

            @block.scalar
            def _(act):
                for d in range(2):
                    act.sem_inc(act_did[d], 2 * len(ACT_STEPS))
                    for p in range(2):
                        act.sem_inc(o_stored[d][p], 16)
                act.wait_ge(gates_in, 48)
                act.wait_ge(tabs_in, 16)
                act.activation(e1[:, :, 0:8], ba[:, :, 0:8], ACT.Exp, scale=-1.0)
                act.activation(decay_rate[:], alog[:], ACT.Exp).then_inc(gate_exp, 1)
                act.wait_ge(step_done, 2)
                act.activation(e1[:, :, 8:16], e2[:], ACT.Exp, scale=-1.0).then_inc(gate_exp, 1)
                act.wait_ge(gate_exp, 2)
                act.activation(e1[:, :, 8:16], e1[:, :, 8:16], ACT.Ln, bias=1.0).then_inc(gate_exp, 1)
                act.wait_ge(sums_up, 1)
                for d in range(2):
                    for n, dst in enumerate((eg, ekd, dn)):
                        act.activation(dst[d][:], ps[:, 0, (3 * d + n) * 64:(3 * d + n + 1) * 64].rearrange("p (c h) -> p c h", h=HEADS),
                                       ACT.Exp).then_inc(gate_exp, 1)

                for pb in pl[1]:
                    act.copy(pb[:], over(tab["eye"])).then_inc(set_up, 1)

                def step(i, p, t, chunk):
                    for d in range(2):
                        act.wait_ge(pe_did[d], pe_at("decay", t))
                        act.wait_ge(pool_did[d], pool_at("incl", t - 1))
                        act.wait_ge(dve_did[d], dve_at("e3", t - 1))
                        act.activation(E[d][:], bank(d, 2), ACT.Exp).then_inc(act_did[d], 1)
                    for d in range(2):
                        act.wait_ge(pe_did[d], pe_at("turn", t))
                        act.copy(X[d][:], bank(d, 0)).then_inc(act_did[d], 1)
                    for l in LEVELS[:-1]:
                        for d in range(2):
                            act.wait_ge(pe_did[d], pe_at(f"X{l}", t))
                            act.copy(side_of(X[d][:], l, d), side_of(bank(d, 0), l, d)).then_inc(act_did[d], 1)
                    for d in range(2):
                        act.wait_ge(dve_did[d], dve_at("o", t))
                        act.dma_start(scr["o"][d, bass.ds(chunk[d] * P, P), :], o[:, d, p].rearrange("p h n -> p (h n)")).then_inc(o_stored[d][p], 16)
                each(act, step)
                for d in range(2):
                    for p in range(2):
                        act.wait_ge(o_stored[d][p], landed(NT // 2))

            @block.vector
            def _(dve):
                for d in range(2):
                    dve.sem_inc(dve_did[d], 2 * len(DVE_STEPS))
                dve.wait_ge(gates_in, 48)
                dve.wait_ge(tabs_in, 16)
                a_in = ba[:, :, 8:16]
                across = lambda a: a.unsqueeze(1).to_broadcast([P, NT, 2 * HEADS])
                dve.tensor_tensor(g[:], a_in, across(dtb[:]), ALU.add).then_inc(step_done, 1)
                dve.wait_ge(step_done, 1)
                dve.scalar_tensor_tensor(e2[:], g[:], -1.0, g[:], ALU.mult, ALU.max).then_inc(step_done, 1)
                dve.wait_ge(step_done, 2)
                dve.tensor_scalar(g[:], g[:], 0.0, None, ALU.max).then_inc(step_done, 1)
                dve.wait_ge(gate_exp, 1)
                dve.tensor_scalar(beta[:], e1[:, :, 0:8], 1.0, None, ALU.add).then_inc(step_done, 1)
                dve.wait_ge(step_done, 4)
                dve.reciprocal(beta[:], beta[:]).then_inc(step_done, 1)
                dve.wait_ge(gate_exp, 3)
                dve.tensor_tensor(g[:], g[:], e1[:, :, 8:16], ALU.add).then_inc(step_done, 1)
                dve.wait_ge(step_done, 6)
                dve.scalar_tensor_tensor(g[:], g[:], -1.0, across(decay_rate[:]), ALU.mult, ALU.mult).then_inc(step_done, 1)
                for pb in pl[0]:
                    dve.tensor_copy(pb[:], over(tab["eye"])).then_inc(set_up, 1)
                for d in range(2):
                    dve.tensor_scalar(nb[d][:], beta[:, :, d * HEADS:(d + 1) * HEADS], -1.0, None, ALU.mult).then_inc(step_done, 1)
                dve.wait_ge(gate_exp, 9)
                dve.wait_ge(set_up, 2 * (1 + len(LEVELS)))
                for d in range(2):
                    dve.tensor_scalar(neg[d][:], eg[d][:], -1.0, None, ALU.mult).then_inc(step_done, 1)
                dve.wait_ge(step_done, 11)
                gates = lambda a: a.rearrange("p o h -> p (o h)").unsqueeze(2).to_broadcast([P, HEADS, P])

                def step(i, p, t, chunk):
                    for d, low, up, gmask, cmask, smask in DIR:
                        dve.wait_ge(act_did[d], act_at("exp", t))
                        dve.wait_ge(pool_did[d], pool_at("nb_mask", t))
                        dve.tensor_tensor(E3[d][:], E[d][:], NBM[d][:], ALU.mult).then_inc(dve_did[d], 1)
                        dve.wait_ge(pe_did[d], pe_at("gram", t))
                        dve.wait_ge(dve_did[d], dve_at("e3", t))
                        dve.tensor_tensor(NA[d][:], bank(d, 0), E3[d][:], ALU.mult).then_inc(dve_did[d], 1)
                        dve.wait_ge(dve_did[d], dve_at("na", t))
                        dve.wait_ge(pool_did[d], pool_at("eye", t))
                        dve.sem_inc(passed, 1)
                        dve.copy_predicated(XT[p][d][:], over(tab[up + "1"].bitcast(I32)), NA[d][:]).then_inc(dve_did[d], 1)
                    for d in range(2):
                        dve.wait_ge(pe_did[d], pe_at("gram", t))
                        dve.wait_ge(pool_did[d], pool_at("incl", t))
                        dve.tensor_tensor(AT[d][:], bank(d, 1), E1[d][:], ALU.mult).then_inc(dve_did[d], 1)
                    for d in range(2):
                        c = chunk[d]
                        dve.wait_ge(pe_did[d], pe_at("ks", t))
                        dve.sem_inc(passed, 1)
                        for h in range(HEADS):
                            last = dve.scalar_tensor_tensor(R[d][:, h], bank(d, 3)[:, h], neg[d][:, bass.ds(c, 1), h], kv[:, d, p, 1, h],
                                                            ALU.mult, ALU.add)
                        last.then_inc(dve_did[d], 1)
                    for n, l in enumerate(LEVELS):
                        for d, low, up, gmask, cmask, smask in DIR:
                            mask = side_of(tab[f"{low}{l}"].bitcast(I32), l, d)
                            dve.wait_ge(pe_did[d], pe_at(f"P{l}", t))
                            dve.sem_inc(passed, 1)
                            dve.copy_predicated(side_of(pl[d][n][:], l, d), mask.unsqueeze(1).to_broadcast([P, HEADS] + list(mask.shape[1:])),
                                                side_of(bank(d, 0), l, d)).then_inc(dve_did[d], 1)
                        for d in range(2):
                            dve.wait_ge(pe_did[d], pe_at(f"X{l}", t))
                            dve.tensor_copy(side_of(XT[p][d][:], l, 1 - d), side_of(bank(d, 1), l, 1 - d)).then_inc(dve_did[d], 1)
                        if l == 3:
                            for d in range(2):
                                dve.tensor_tensor(QS[d][:], bank(d, 2), gates(eg[d][:, bass.ds(chunk[d], 1), :]), ALU.mult).then_inc(dve_did[d], 1)
                    for d in range(2):
                        c = chunk[d]
                        dve.wait_ge(pe_did[d], pe_at("vn", t))
                        dve.tensor_tensor(VN[d][:], bank(d, 1), gates(beta[:, bass.ds(c, 1), d * HEADS:(d + 1) * HEADS]),
                                          ALU.mult).then_inc(dve_did[d], 1)
                    for d in range(2):
                        c = chunk[d]
                        dve.wait_ge(pe_did[d], pe_at("o", t))
                        dve.wait_ge(dve_did[d], dve_at("qs", t))
                        dve.wait_ge(o_stored[d][p], landed(i))
                        dve.tensor_tensor(o[:, d, p], QS[d][:], bank(d, 2), ALU.add).then_inc(dve_did[d], 1)
                        dve.wait_ge(pe_did[d], pe_at("su", t))
                        for h in range(HEADS):
                            last = dve.scalar_tensor_tensor(ST[d][:, h], ST[d][:, h], dn[d][:, bass.ds(c, 1), h], bank(d, 3)[:, h],
                                                            ALU.mult, ALU.add)
                        last.then_inc(dve_did[d], 1)
                each(dve, step)

            @block.tensor
            def _(pe):
                for d in range(2):
                    pe.sem_inc(pe_did[d], 2 * len(PE_STEPS))
                pe.wait_ge(tabs_in, 16)
                pe.wait_ge(step_done, 9)
                for d, low, up, gmask, cmask, smask in DIR:
                    gd = g[:, :, d * HEADS:(d + 1) * HEADS]
                    for n, mask in enumerate((cmask, gmask, "ones")):
                        last = pe.matmul(ps[:, 0, (3 * d + n) * 64:(3 * d + n + 1) * 64], tab[mask], gd, start=True, stop=True)
                last.then_inc(sums_up, 1)
                pe.wait_ge(gate_exp, 9)
                pe.wait_ge(set_up, 2 * (1 + len(LEVELS)))

                def step(i, p, t, chunk):
                    mm = lambda out, a, b: pe.matmul(out, a, b, start=True, stop=True)
                    for d, low, up, gmask, cmask, smask in DIR:
                        pe.wait_ge(dve_did[d], dve_at("o", t - 1))
                        pe.wait_ge(pool_did[d], pool_at("gm", t))
                        for h in range(HEADS):
                            last = mm(bank(d, 2)[:, h], gm[d][:, h], tab[cmask])
                        last.then_inc(pe_did[d], 1)
                    for d in range(2):
                        pe.wait_ge(ch_in[d][p], 32 * (i + 1))
                        pe.wait_ge(dve_did[d], dve_at("vn", t - 1))
                        for h in range(HEADS):
                            mm(bank(d, 0)[:, h], ch[:, d, p, 0, h], ch[:, d, p, 0, h])
                            last = mm(bank(d, 1)[:, h], ch[:, d, p, 0, h], ch[:, d, p, 1, h])
                        last.then_inc(pe_did[d], 1)
                    for d in range(2):
                        pe.wait_ge(dve_did[d], dve_at("s", t - 1))
                        pe.wait_ge(act_did[d], act_at("exp", t))
                        for h in range(HEADS):
                            mm(bank(d, 3)[:, h], ch[:, d, p, 0, h], ST[d][:, h])
                            last = mm(bank(d, 2)[:, h], ch[:, d, p, 1, h], ST[d][:, h])
                        last.then_inc(pe_did[d], 1)
                    for d in range(2):
                        pe.wait_ge(dve_did[d], dve_at("xt1", t))
                        for h in range(HEADS):
                            last = pe.transpose(bank(d, 0)[:, h], XT[p][d][:, h], tab["eye"])
                        last.then_inc(pe_did[d], 1)
                    for n, l in enumerate(LEVELS):
                        for d in range(2):
                            pe.wait_ge(act_did[d], act_at(f"X{l - 1}", t))
                            for h in range(HEADS):
                                last = mm(bank(d, 0)[:, h], NA[d][:, h], X[d][:, h])
                            last.then_inc(pe_did[d], 1)
                        for d in range(2):
                            pe.wait_ge(dve_did[d], dve_at(f"P{l}", t))
                            for h in range(HEADS):
                                if l < LEVELS[-1]:
                                    mm(bank(d, 0)[:, h], XT[p][d][:, h], pl[d][n][:, h])
                                last = mm(bank(d, 1)[:, h], pl[d][n][:, h], XT[p][d][:, h])
                            last.then_inc(pe_did[d], 1)
                    for d in range(2):
                        pe.wait_ge(dve_did[d], dve_at("XT7", t))
                        for h in range(HEADS):
                            last = mm(bank(d, 1)[:, h], XT[p][d][:, h], R[d][:, h])
                        last.then_inc(pe_did[d], 1)
                    for d in range(2):
                        pe.wait_ge(dve_did[d], dve_at("vn", t))
                        for h in range(HEADS):
                            last = mm(bank(d, 2)[:, h], AT[d][:, h], VN[d][:, h])
                        last.then_inc(pe_did[d], 1)
                        pe.wait_ge(pool_did[d], pool_at("kd", t))
                        for h in range(HEADS):
                            last = mm(bank(d, 3)[:, h], KD_[d][:, h], VN[d][:, h])
                        last.then_inc(pe_did[d], 1)
                each(pe, step)



def lagged(eng, slot):
    slot(0, 0, None)
    with eng.Fori(0, NT // 2 - 1) as i:
        slot(1, 2 * i + 1, 2 * i)
        slot(0, 2 * i + 2, 2 * i + 1)
    slot(1, NT - 1, NT - 2)
    slot(0, None, NT - 1)


def attention(nc, io, scr, ps, sem):
    with ExitStack() as keep:
        sb = lambda n, s, dt=F32: keep.enter_context(nc.sbuf_tensor(n, s, dt))
        HH = QH + KVH
        eye = sb("e_eye", [P, P])
        QB = 4
        qk = sb("e_qk", [P, QB, HH, AD])
        trig = sb("e_trig", [P, QB, 2, HALF])
        rot = sb("e_rot", [P, 4, HH, HALF])
        qkT = sb("e_qkT", [AD, HH, NT + 2, P])
        v = sb("e_v", [P, NT + 2, KVH * AD])
        qT = sb("e_qT", [AD, 2, QH, P])
        band = sb("e_band", [P, 2, 3 * P])
        sink = sb("e_sink", [P, QH])
        sc = sb("e_sc", [P, 2, QH, 3 * P])
        pr = sb("e_pr", [P, QH, 3 * P])
        pT = sb("e_pT", [P, QH, 3, P])
        m = sb("e_m", [P, QH])
        negm = sb("e_negm", [P, QH])
        ds = sb("e_ds", [P, QH])
        es = sb("e_es", [P, QH])
        sums = sb("e_sums", [P, QH])
        den = sb("e_den", [P, 2, QH])
        o = sb("e_o", [P, 2, QH, AD])

        consts, padded, passed = sem("e_consts"), sem("e_padded"), sem("e_passed")
        qk_in = [sem(f"e_qk_in{b}") for b in range(QB)]
        band_in, stored = [[sem(f"e_{x}{p}") for p in range(2)] for x in ("band_in", "stored")]
        multiplied, rotated, turned, all_out = sem("e_multiplied"), sem("e_rotated"), sem("e_turned"), sem("e_all_out")
        q_copied, scored, masked = sem("e_q_copied"), sem("e_scored"), sem("e_masked")
        maxed, sunk, exped, denned = sem("e_maxed"), sem("e_sunk"), sem("e_exped"), sem("e_denned")
        p_turned, pT_act, pT_dve, mixed, o_out = [sem("e_" + x) for x in ("p_turned", "pT_act", "pT_dve", "mixed", "o_out")]

        turned_to = lambda h: (4, 5, 7)[h % 3]

        def each(eng, step):
            with eng.Fori(0, NT // 2) as i:
                for p in range(2):
                    step(i, p, 2 * i + p)

        def each_rotated(eng, prepare, start=0):
            with eng.Fori(start, NT // QB) as i:
                for b in range(QB):
                    prepare(i, b, QB * i + b)

        with nc.Block() as block:

            @block.sync
            def _(sp):
                j = NAMES.index("eye")
                sp.dma_start(eye[:], io["tab"][:, j * P:(j + 1) * P]).then_inc(consts, 16)
                sp.dma_start(sink[:], io["attn_sink"].to_broadcast([P, QH])).then_inc(consts, 16)
                sp.dma_start(v[:, 1:NT + 1, :], scr["tok"][:, V0:V0 + KVH * AD].rearrange("(c p) w -> p c w", p=P)).then_inc(consts, 16)

                def prepare(i, b, t):
                    if isinstance(t, int):
                        row = t * P
                    else:
                        row, free = sp.snap(t * P), sp.snap(done(t - QB))
                        sp.wait_ge(turned, free)
                    sp.dma_start(qk[:, b], scr["tok"][bass.ds(row, P), Q0:V0].rearrange("p (h d) -> p h d", d=AD)).then_inc(qk_in[b], 16)
                    sp.dma_start(trig[:, b], io["trig"][bass.ds(row, P), :].rearrange("p (a f) -> p a f", a=2)).then_inc(qk_in[b], 16)
                for b in range(QB):
                    prepare(0, b, b)
                each_rotated(sp, prepare, 1)

                def step(i, p, t):
                    row, free = sp.snap(t), sp.snap(done(t - 2, QH, QH))
                    sp.wait_ge(masked, free)
                    sp.dma_start(band[:, p], io["band"][bass.ds(row, 1)].rearrange("o p k -> (o p) k")).then_inc(band_in[p], 16)
                each(sp, step)

            @block.gpsimd
            def _(pool):
                pool.sem_inc(q_copied, 2)
                pool.memset(qkT[:, :, 0, :], 0.0)
                pool.memset(qkT[:, :, NT + 1, :], 0.0)
                pool.memset(v[:, 0, :], 0.0)
                pool.memset(v[:, NT + 1, :], 0.0).then_inc(padded, 1)
                pool.wait_ge(all_out, done(NT - 1))

                def step(i, p, t):
                    pool.wait_ge(scored, done(t - 2, QH, QH))
                    pool.tensor_copy(qT[:, p], qkT[:, 0:QH, bass.ds(t + 1, 1), :].rearrange("d h o t -> d h (o t)")).then_inc(q_copied, 1)
                each(pool, step)

            @block.scalar
            def _(act):
                for s, per in ((all_out, 1), (exped, QH + 1), (pT_act, 4)):
                    act.sem_inc(s, 2 * per)
                for p in range(2):
                    act.sem_inc(stored[p], 16)
                act.wait_ge(consts, 48)

                def prepare(i, b, t):
                    act.wait_ge(turned, done(t))
                    for n, (lo, hi) in enumerate(((0, 4), (4, 8), (8, HH))):
                        last = act.copy(qkT[:, lo:hi, bass.ds(t + 1, 1), :].rearrange("d h o t -> d h (o t)"),
                                        ps[0:AD, 4 * (b % 2) + n, 0:(hi - lo) * P].rearrange("d (h t) -> d h t", t=P))
                    last.then_inc(all_out, 1)
                each_rotated(act, prepare)

                def slot(p, t, old):
                    if old is not None:
                        for n, h in enumerate(range(0, QH, 2)):
                            act.wait_ge(p_turned, done(old, h + 1, QH))
                            act.wait_ge(mixed, done(old - 1))
                            act.copy(pT[:, h], ps[:, turned_to(h), 0:3 * P].rearrange("k (j q) -> k j q", j=3)).then_inc(pT_act, 1)
                    if t is not None:
                        act.wait_ge(sunk, done(t, 2, 2))
                        act.wait_ge(denned, done(t - 1, 2, 2))
                        act.activation(es[:], ds[:], ACT.Exp).then_inc(exped, 1)
                        act.wait_ge(p_turned, done(t - 1, QH, QH))
                        for h in range(QH):
                            act.activation(pr[:, h], sc[:, p, h], ACT.Exp, bias=negm[:, h:h + 1], accum_out=sums[:, h:h + 1]).then_inc(exped, 1)
                    if old is not None:
                        q = 1 - p
                        act.wait_ge(o_out, done(old))
                        act.dma_start(scr["attn"][bass.ds(old * P, P), :], o[:, q].rearrange("p h d -> p (h d)")).then_inc(stored[q], 16)
                lagged(act, slot)
                for p in range(2):
                    act.wait_ge(stored[p], landed(NT // 2))

            @block.vector
            def _(dve):
                for s, per in ((rotated, 2), (multiplied, 1), (masked, QH), (maxed, 2), (sunk, 2), (denned, 2), (pT_dve, 4), (o_out, 1)):
                    dve.sem_inc(s, 2 * per)
                dve.wait_ge(consts, 48)

                def prepare(i, b, t):
                    dve.wait_ge(qk_in[b], 32 * (i + 1))
                    lo, hi = qk[:, b, :, 0:HALF], qk[:, b, :, HALF:ROT]
                    cos = trig[:, b, 0, :].unsqueeze(1).to_broadcast([P, HH, HALF])
                    sin = trig[:, b, 1, :].unsqueeze(1).to_broadcast([P, HH, HALF])
                    dve.wait_ge(rotated, done(t - 1, 2, 2))
                    for n, (a, f) in enumerate(((lo, cos), (hi, sin), (hi, cos), (lo, sin))):
                        last = dve.tensor_tensor(rot[:, n], a, f, ALU.mult)
                    last.then_inc(multiplied, 1)
                    dve.wait_ge(multiplied, done(t))
                    dve.tensor_tensor(lo, rot[:, 0], rot[:, 1], ALU.subtract).then_inc(rotated, 1)
                    dve.tensor_tensor(hi, rot[:, 2], rot[:, 3], ALU.add).then_inc(rotated, 1)
                each_rotated(dve, prepare)

                def slot(p, t, old):
                    if t is not None:
                        for h in range(QH):
                            dve.wait_ge(scored, done(t, h + 1, QH))
                            if h == 0:
                                dve.wait_ge(band_in[p], uses(t, p) + 16)
                                dve.wait_ge(exped, done(t - 2, QH + 1, QH + 1))
                            dve.scalar_tensor_tensor(sc[:, p, h], ps[:, h % 4, 0:3 * P], AD ** -0.5, band[:, p], ALU.mult, ALU.add).then_inc(masked, 1)
                    if old is not None:
                        q = 1 - p
                        dve.wait_ge(exped, done(old, QH + 1, QH + 1))
                        dve.tensor_tensor(den[:, q], sums[:], es[:], ALU.add).then_inc(denned, 1)
                        dve.wait_ge(denned, done(old, 1, 2))
                        dve.reciprocal(den[:, q], den[:, q]).then_inc(denned, 1)
                        for h in range(1, QH, 2):
                            dve.wait_ge(p_turned, done(old, h + 1, QH))
                            dve.wait_ge(mixed, done(old - 1))
                            dve.tensor_copy(pT[:, h], ps[:, turned_to(h), 0:3 * P].rearrange("k (j q) -> k j q", j=3)).then_inc(pT_dve, 1)
                    if t is not None:
                        dve.wait_ge(masked, done(t, QH, QH))
                        dve.tensor_reduce(m[:], sc[:, p], AX.X, ALU.max).then_inc(maxed, 1)
                        dve.wait_ge(maxed, done(t, 1, 2))
                        dve.tensor_tensor(m[:], m[:], sink[:], ALU.max).then_inc(maxed, 1)
                        dve.wait_ge(maxed, done(t, 2, 2))
                        dve.tensor_scalar(negm[:], m[:], -1.0, None, ALU.mult).then_inc(sunk, 1)
                        dve.tensor_tensor(ds[:], sink[:], m[:], ALU.subtract).then_inc(sunk, 1)
                    if old is not None:
                        q = 1 - p
                        dve.wait_ge(mixed, done(old))
                        dve.wait_ge(denned, done(old, 2, 2))
                        dve.wait_ge(stored[q], 8 * (old - q) + 16)
                        dve.tensor_tensor(o[:, q], ps[:, 6, :].rearrange("p (h d) -> p h d", d=AD),
                                          den[:, q, :].unsqueeze(2).to_broadcast([P, QH, AD]), ALU.mult).then_inc(o_out, 1)
                lagged(dve, slot)

            @block.tensor
            def _(pe):
                for s, per in ((turned, 1), (scored, QH), (p_turned, QH), (mixed, 1)):
                    pe.sem_inc(s, 2 * per)
                pe.wait_ge(consts, 48)
                pe.wait_ge(padded, 1)

                def prepare(i, b, t):
                    pe.wait_ge(rotated, done(t, 2, 2))
                    pe.wait_ge(all_out, done(t - 2))
                    pe.sem_inc(passed, 1)
                    for h in range(HH):
                        last = pe.transpose(ps[0:AD, 4 * (b % 2) + h // 4, (h % 4) * P:(h % 4 + 1) * P], qk[:, b, h, :], eye[:])
                    last.then_inc(turned, 1)
                each_rotated(pe, prepare)
                pe.wait_ge(all_out, done(NT - 1))

                def slot(p, t, old):
                    if t is not None:
                        pe.wait_ge(q_copied, done(t))
                        for h in range(QH):
                            pe.wait_ge(masked, done(t, h - 3, QH))
                            pe.sem_inc(passed, 1)
                            kv = QH + h // (QH // KVH)
                            keys = qkT[:, kv, bass.ds(t, 3), :].rearrange("d j t -> d (j t)")
                            pe.matmul(ps[:, h % 4, 0:3 * P], qT[:, p, h, :], keys, start=True, stop=True).then_inc(scored, 1)
                    if old is not None:
                        for h in range(QH):
                            pe.wait_ge(exped, done(old, h + 2, QH + 1))
                            if h >= 3:
                                pe.wait_ge(pT_act if h % 2 else pT_dve, done(old, (h - 1) // 2, 4))
                            for j in range(3):
                                last = pe.transpose(ps[:, turned_to(h), j * P:(j + 1) * P], pr[:, h, j * P:(j + 1) * P], eye[:])
                            last.then_inc(p_turned, 1)
                        pe.wait_ge(o_out, done(old - 1))
                        for h in range(QH):
                            pe.wait_ge(pT_dve if h % 2 else pT_act, done(old, h // 2 + 1, 4))
                            kv = h // (QH // KVH)
                            for j in range(3):
                                last = pe.matmul(ps[:, 6, h * AD:(h + 1) * AD], pT[:, h, j, :],
                                                 v[:, bass.ds(old + j, 1), kv * AD:(kv + 1) * AD].rearrange("k o d -> k (o d)"),
                                                 start=(j == 0), stop=(j == 2))
                        last.then_inc(mixed, 1)
                lagged(pe, slot)




def mix_and_route(nc, io, scr, ps, sem, n_more):
    with ExitStack() as keep:
        sb = lambda n, s, dt=F32: keep.enter_context(nc.sbuf_tensor(n, s, dt))
        names = ["eye", "lt", "ones", "le"]
        tab_t, tab = load_tab(nc, keep, names, "f")
        w_lead, w_rest = sb("f_w_lead", [P, KD, D], F32R), sb("f_w_rest", [P, KD, D], F32R)
        wr = sb("f_wr", [P, KD, NG + NE])
        bias = sb("f_bias", [P, NG + NE])
        count = sb("f_count", [P, NG + NE + NR])
        token = sb("f_token", [P, NT + 1])
        nw = sb("f_nw", [P, HEADS, DH])
        lnf = sb("f_lnf", [P, D])
        power = sb("f_power", [P, HEADS])
        oo = sb("f_oo", [P, 2, 2, DN])
        za = sb("f_za", [P, 2, 2, DN])
        x = sb("f_x", [P, 2, D])
        mixin = sb("f_mixin", [P, 2, HEADS, DH])
        junk, junk_o = sb("f_junk", [P, D]), sb("f_junk_o", [P, DN])
        ssq, ms, rstd = sb("f_ssq", [P, HEADS]), sb("f_ms", [P, HEADS]), sb("f_rstd", [P, HEADS])
        mT_lead, mT_rest = sb("f_mT_lead", [P, 2, KD, P], F32R), sb("f_mT_rest", [P, 2, KD, P], F32R)
        x1 = sb("f_x1", [P, 2, D])
        ss2, ms2, rstd2 = sb("f_ss2", [P, 1]), sb("f_ms2", [P, 1]), sb("f_rstd2", [P, 1])
        h2 = sb("f_h2", [P, 2, D])
        h2T = sb("f_h2T", [P, KD, P])
        lg = sb("f_lg", [P, NT, NG + NE])
        gexp, pick = sb("f_gexp", [P, NT, NG]), sb("f_pick", [P, NT, NG])
        em, score = sb("f_em", [P, NT, NE]), sb("f_score", [P, NT, NE])
        oh = sb("f_oh", [P, 3, NT, NE])
        before_tile = sb("f_before_tile", [P, NT + 1, NE])
        one = {n: sb("f_" + n, [P, NT]) for n in ("gmax", "gfirst", "gsum", "gap", "ratio", "spread")}
        pair = {n: sb("f_" + n, [P, 2, NT]) for n in ("top", "first", "gate", "place", "base")}
        total = sb("f_total", [P, NE])
        exceed, extra, extraT = sb("f_exceed", [P, NE, NR]), sb("f_extra", [P, NE]), sb("f_extraT", [NE, P])
        csum, before, items = sb("f_csum", [P, NE]), sb("f_before", [P, NE]), sb("f_items", [P, 2], I32)
        col = sb("f_col", [P, 5])
        slot_id = sb("f_slot", [P, 2, NT], I32)
        rec = sb("f_rec", [P, 2, NT, 4], I32)

        consts, tabs_in, router_in = sem("f_consts"), sem("f_tabs_in"), sem("f_router_in")
        QUARTERS, QW = 4, D // 4
        as_quarter = lambda a: a.rearrange("p (k n) -> p k n", k=KD)
        room = [as_quarter(x1[:].rearrange("p b d -> p (b d)")), as_quarter(h2[:].rearrange("p b d -> p (b d)")),
                as_quarter(oh[:, 0:2].rearrange("p c t e -> p (c t e)"))]
        w_in = [sem(f"f_w_in{q}") for q in range(QUARTERS)]
        w_led, w_split, mT_split = sem("f_w_led"), sem("f_w_split"), sem("f_mT_split")
        loaded, x_in, stored_x, stored_h = [[sem(f"f_{n}{p}") for p in range(2)] for n in ("loaded", "x_in", "x1_stored", "h2_stored")]
        weighted, osummed, osquared, omean, orooted, odone = [
            sem("f_" + n) for n in ("weighted", "osummed", "osquared", "omean", "orooted", "odone")]
        mturned, mT_out, product, added = [sem("f_" + n) for n in ("mturned", "mT_out", "product", "added")]
        squared, mean, rooted, normed = [sem("f_" + n) for n in ("squared", "mean", "rooted", "normed")]
        hturned, hT_act, hT_dve, logits, logged = [sem("f_" + n) for n in ("hturned", "hT_act", "hT_dve", "logits", "logged")]
        gexped, rexped, routed, counted, scattered = [sem("f_" + n) for n in ("gexped", "rexped", "routed", "counted", "scattered")]
        planned, extra_up, items_out, powered, passed = [
            sem("f_" + n) for n in ("planned", "extra_up", "items_out", "powered", "passed")]
        turn = lambda b: ps[:, b, :].rearrange("p (k t) -> p k t", k=4)
        heads = lambda a: a.rearrange("p (h d) -> p h d", h=HEADS)
        LOADS = 16 * 4
        CHOOSE = ["best", "shift", "ties", "first", "group", "penalty", "masked", "top0", "equal0", "ties0", "first0", "mask0",
                  "drop0", "top1", "equal1", "ties1", "first1", "mask1", "gap", "both"] + [f"count{n}" for n in range(NT // 2)]
        RECORD = ["gsum", "spread", "gate0", "gate1", "base", "token", "dest0", "dest1", "gates", "spare",
                  "mine0", "place0", "mine1", "place1", "slots"]
        ROUTE = ["none_before"] + [(half, n) for half in range(2) for n in CHOOSE + RECORD] + ["total"]
        halves = [slice(half * NT // 2, (half + 1) * NT // 2) for half in range(2)]

        def route_at(*name):
            return ROUTE.index(name if len(name) > 1 else name[0]) + 1

        def is_last(at):
            return at(-1) is not None and isinstance(at(-1)[0], int) and at(-1)[0] == NT - 1

        each = lambda eng, slot: staged(eng, slot, 2)

        with nc.Block() as block:

            @block.sync
            def _(sp):
                for h in range(HEADS):
                    sp.dma_start(nw[:, h, :], io["dn_norm"].to_broadcast([P, DH])).then_inc(consts, 16)

                def load(p, row):
                    for d in range(2):
                        sp.dma_start(oo[:, p, d], scr["o"][d, bass.ds(row, P), :]).then_inc(loaded[p], 16)
                    sp.dma_start(za[:, p, 0], scr["tok"][bass.ds(row, P), Z0:Z0 + DN]).then_inc(loaded[p], 16)
                    sp.dma_start(za[:, p, 1], scr["attn"][bass.ds(row, P), :]).then_inc(loaded[p], 16)

                def load_x(p, row):
                    sp.dma_start(x[:, p], io["x"][0, bass.ds(row, P), :]).then_inc(x_in[p], 16)

                load(0, 0)
                issue_tab(sp, io, tab_t, names, tabs_in)

                def load_quarter(q):
                    cols = slice(q * QW, (q + 1) * QW)
                    sp.dma_start(room[q % 3], io["w_out"][0, :, cols].rearrange("(k p) n -> p k n", p=P)).then_inc(w_in[q], 16)

                for q in range(3):
                    load_quarter(q)
                load_x(0, 0)
                load(1, P)
                sp.dma_start(lnf[:], io["ln_ffn"].to_broadcast([P, D])).then_inc(router_in, 16)
                sp.dma_start(wr[:, :, 0:NG], io["w_group"][0].rearrange("(k p) n -> p k n", p=P)).then_inc(router_in, 16)
                sp.dma_start(wr[:, :, NG:], io["w_expert"][0].rearrange("(k p) n -> p k n", p=P)).then_inc(router_in, 16)
                sp.dma_start(bias[:, 0:NG], io["b_group"].to_broadcast([P, NG])).then_inc(router_in, 16)
                sp.dma_start(bias[:, NG:], io["b_expert"].to_broadcast([P, NE])).then_inc(router_in, 16)
                sp.dma_start(token[:], io["token"]).then_inc(router_in, 16)
                sp.dma_start(count[:], io["count"]).then_inc(router_in, 16)
                sp.wait_ge(w_split, 1)
                load_quarter(3)
                load_x(1, P)

                with sp.Fori(1, NT // 2) as i:
                    for p in range(2):
                        t = 2 * i + p
                        row, free = sp.snap(t * P), sp.snap(done(t - 2, 2, 2))
                        sp.wait_ge(mturned, free)
                        load(p, row)
                        sp.wait_ge(added, free)
                        load_x(p, row)

                sp.wait_ge(planned, 13)
                sp.dma_start(scr["items"], items[:]).then_inc(items_out, 16)
                sp.wait_ge(items_out, 16)

            ROUTER = 16 * 7

            @block.gpsimd
            def _(pool):
                for s in (weighted, orooted, rooted):
                    pool.sem_inc(s, 2)
                pool.memset(power[:], -0.5).then_inc(powered, 1)
                pool.wait_ge(powered, 1)
                pool.wait_ge(consts, 16 * HEADS)

                def scatter(half):
                    pool.wait_ge(routed, route_at(half, "slots"))
                    for t in range(halves[half].start, halves[half].stop):
                        for c in range(2):
                            pool.indirect_dma_start(scr["list"][:, :], bass.IndirectOffsetOnAxis(slot_id[:, c, t:t + 1], 0), rec[:, c, t, :], None,
                                                    bounds_check=LISTS - 1, oob_is_err=False).then_inc(scattered, 16)

                def slot(at):
                    if at(1) is not None:
                        t, p = at(1)
                        pool.wait_ge(loaded[p], 4 * uses(t, p) + LOADS)
                        pool.tensor_tensor(za[:, p, 0], za[:, p, 0], nw[:].rearrange("p h d -> p (h d)"), ALU.mult).then_inc(weighted, 1)
                        pool.wait_ge(omean, done(t))
                        pool.wait_ge(odone, done(t - 1, 2, 2))
                        pool.tensor_tensor(rstd[:], ms[:], power[:], ALU.pow).then_inc(orooted, 1)
                    if at(-1) is not None:
                        t, p = at(-1)
                        pool.wait_ge(mean, done(t))
                        pool.wait_ge(normed, done(t - 1))
                        pool.tensor_tensor(rstd2[:], ms2[:], power[:, 0:1], ALU.pow).then_inc(rooted, 1)
                    if is_last(at):
                        scatter(0)
                each(pool, slot)

                scatter(1)
                pool.wait_ge(scattered, 16 * 2 * NT)

            @block.scalar
            def _(act):
                for s, per in ((osquared, 1), (mT_out, 2), (squared, 1), (hT_act, 1)):
                    act.sem_inc(s, 2 * per)
                for p in range(2):
                    act.sem_inc(stored_x[p], 16)
                    act.sem_inc(stored_h[p], 16)

                def exp_groups(half):
                    act.wait_ge(routed, route_at(half, "shift"))
                    act.activation(gexp[:, halves[half]], pick[:, halves[half]], ACT.Exp).then_inc(gexped, 1)

                def exp_gap(half):
                    act.wait_ge(routed, route_at(half, "gap"))
                    act.activation(one["ratio"][:, halves[half]], one["gap"][:, halves[half]], ACT.Exp).then_inc(rexped, 1)

                def slot(at):
                    if at(1) is not None:
                        t, p = at(1)
                        act.wait_ge(osummed, done(t))
                        act.wait_ge(osquared, done(t - 1))
                        act.wait_ge(omean, done(t - 1))
                        for h in range(HEADS):
                            last = act.activation(junk_o[:, h * DH:(h + 1) * DH], oo[:, p, 0, h * DH:(h + 1) * DH], ACT.Square,
                                                  accum_out=ssq[:, h:h + 1])
                        last.then_inc(osquared, 1)
                    if at(0) is not None:
                        t, p = at(0)
                        for b in range(2):
                            act.wait_ge(mturned, done(t, b + 1, 2))
                            act.wait_ge(product, done(t - 2, 2, 2))
                            act.copy(mT_lead[:, p, 4 * b:4 * b + 4], turn(b)).then_inc(mT_out, 1)
                    if at(0) is None and at(1) is not None:
                        for q in range(QUARTERS):
                            act.wait_ge(w_in[q], 16)
                            act.copy(w_lead[:, :, q * QW:(q + 1) * QW], room[q % 3]).then_inc(w_led, 1)
                    if is_last(at):
                        exp_groups(0)
                    if at(-2) is not None:
                        t, p = at(-2)
                        act.wait_ge(hturned, done(t, 1, 2))
                        act.wait_ge(logits, done(t - 1))
                        act.copy(h2T[:, 0:4], turn(4)).then_inc(hT_act, 1)
                    if is_last(at):
                        exp_gap(0)
                    if at(-1) is not None:
                        t, p = at(-1)
                        act.wait_ge(added, done(t, 2, 2))
                        act.wait_ge(mean, done(t - 1))
                        act.wait_ge(squared, done(t - 1))
                        act.activation(junk[:], x1[:, p], ACT.Square, accum_out=ss2[:]).then_inc(squared, 1)
                        act.dma_start(scr["x1"][bass.ds(t * P, P), :], x1[:, p]).then_inc(stored_x[p], 16)
                        act.wait_ge(normed, done(t))
                        act.dma_start(scr["h2"][bass.ds(t * P, P), :], h2[:, p]).then_inc(stored_h[p], 16)
                each(act, slot)
                exp_groups(1)
                exp_gap(1)
                for p in range(2):
                    act.wait_ge(stored_x[p], landed(NT // 2))
                    act.wait_ge(stored_h[p], landed(NT // 2))

            @block.vector
            def _(dve):
                for s, per in ((osummed, 1), (omean, 1), (odone, 2), (mT_split, 2), (added, 2), (mean, 1), (normed, 1), (hT_dve, 1), (logged, 1)):
                    dve.sem_inc(s, 2 * per)

                def then(name, ins):
                    ins.then_inc(routed, 1)
                    dve.wait_ge(routed, route_at(*name) if isinstance(name, tuple) else route_at(name))

                HT = NT // 2

                def choose(half):
                    part = lambda a: a[:, halves[half]]
                    over = lambda a, n: part(a).unsqueeze(2).to_broadcast([P, HT, n])
                    N8 = count[:, 0:NG].unsqueeze(1).to_broadcast([P, HT, NG])
                    N64 = count[:, NG:NG + NE].unsqueeze(1).to_broadcast([P, HT, NE])
                    step = lambda n, ins: then((half, n), ins)
                    pk, em_, sc, logit = part(pick), part(em), part(score), part(lg)
                    dve.wait_ge(logged, done(halves[half].stop - 1))
                    step("best", dve.tensor_reduce(part(one["gmax"]), logit[:, :, 0:NG], AX.X, ALU.max))
                    step("shift", dve.tensor_tensor(pk, logit[:, :, 0:NG], over(one["gmax"], NG), ALU.subtract))
                    dve.wait_ge(gexped, half + 1)
                    step("ties", dve.scalar_tensor_tensor(pk, pk, 0.0, N8, ALU.is_ge, ALU.mult))
                    step("first", dve.tensor_reduce(part(one["gfirst"]), pk, AX.X, ALU.max))
                    step("group", dve.tensor_tensor(pk, N8, over(one["gfirst"], NG), ALU.is_equal))
                    step("penalty", dve.tensor_scalar(pk, pk, -1.0, BIG, ALU.add, ALU.mult))
                    step("masked", dve.tensor_tensor(em_.rearrange("p t (g e) -> p (t g) e", g=NG),
                                                     logit[:, :, NG:].rearrange("p t (g e) -> p t g e", g=NG),
                                                     pk.unsqueeze(3).to_broadcast([P, HT, NG, NE // NG]), ALU.add))
                    for c in range(2):
                        step(f"top{c}", dve.tensor_reduce(part(top[:, c]), em_, AX.X, ALU.max))
                        step(f"equal{c}", dve.tensor_tensor(sc, em_, over(top[:, c], NE), ALU.is_ge))
                        step(f"ties{c}", dve.tensor_tensor(sc, sc, N64, ALU.mult))
                        step(f"first{c}", dve.tensor_reduce(part(first[:, c]), sc, AX.X, ALU.max))
                        step(f"mask{c}", dve.tensor_tensor(part(oh[:, c]), N64, over(first[:, c], NE), ALU.is_equal))
                        if c == 0:
                            step("drop0", dve.scalar_tensor_tensor(em_, part(oh[:, 0]), -BIG, em_, ALU.mult, ALU.add))
                    step("gap", dve.tensor_tensor(part(one["gap"]), part(top[:, 1]), part(top[:, 0]), ALU.subtract))
                    step("both", dve.tensor_tensor(part(oh[:, 2]), part(oh[:, 0]), part(oh[:, 1]), ALU.add))
                    for n in range(HT):
                        t = halves[half].start + n
                        step(f"count{n}", dve.tensor_tensor(before_tile[:, t + 1], before_tile[:, t], oh[:, 2, t], ALU.add))

                def record(half):
                    step = lambda n, ins: then((half, n), ins)
                    part = lambda a: a[:, halves[half]]
                    mine = lambda a: a[:, :, halves[half]]
                    tok, sc = part(token), part(score)
                    step("gsum", dve.tensor_reduce(part(one["gsum"]), part(gexp), AX.X, ALU.add))
                    dve.wait_ge(rexped, half + 1)
                    step("spread", dve.scalar_tensor_tensor(part(one["spread"]), part(one["ratio"]), 1.0, part(one["gsum"]), ALU.add, ALU.mult))
                    step("gate0", dve.reciprocal(part(gate[:, 0]), part(one["spread"])))
                    step("gate1", dve.tensor_tensor(part(gate[:, 1]), part(gate[:, 0]), part(one["ratio"]), ALU.mult))
                    step("base", dve.tensor_scalar(mine(pair["base"]), mine(first), float(-CAP), float(LISTS), ALU.mult, ALU.add))
                    step("token", dve.tensor_scalar(mine(rec)[:, :, :, 0], tok.unsqueeze(1).to_broadcast([P, 2, HT]), 0.0, None, ALU.add))
                    step("dest0", dve.tensor_scalar(mine(rec)[:, 0, :, 1], tok, 0.0, None, ALU.add))
                    step("dest1", dve.tensor_scalar(mine(rec)[:, 1, :, 1], tok, float(S), None, ALU.add))
                    step("gates", dve.tensor_copy(mine(rec[:].bitcast(F32))[:, :, :, 2], mine(gate)))
                    step("spare", dve.tensor_scalar(mine(rec)[:, :, :, 3], mine(gate), 0.0, None, ALU.mult))
                    dve.wait_ge(counted, half + 1)
                    for c in range(2):
                        step(f"mine{c}", dve.tensor_tensor(sc.rearrange("p t e -> p (t e)"), part(oh[:, c]).rearrange("p t e -> p (t e)"),
                                                           ps[:, half, :], ALU.mult))
                        step(f"place{c}", dve.tensor_reduce(part(place[:, c]), sc, AX.X, ALU.add))
                    step("slots", dve.tensor_tensor(mine(slot_id), mine(pair["base"]), mine(place), ALU.add))

                top, first, gate, place = [pair[n] for n in ("top", "first", "gate", "place")]
                then("none_before", dve.memset(before_tile[:, 0], 0.0))

                def slot(at):
                    if at(1) is not None:
                        t, p = at(1)
                        dve.wait_ge(loaded[p], 4 * uses(t, p) + LOADS)
                        dve.tensor_tensor(oo[:, p, 0], oo[:, p, 0], oo[:, p, 1], ALU.add).then_inc(osummed, 1)
                        dve.wait_ge(osummed, done(t))
                        dve.wait_ge(weighted, done(t))
                        dve.wait_ge(mturned, done(t - 2, 1, 2))
                        dve.tensor_tensor(mixin[:, p], heads(oo[:, p, 0]), heads(za[:, p, 0]), ALU.mult).then_inc(odone, 1)
                        dve.wait_ge(osquared, done(t))
                        dve.wait_ge(orooted, done(t - 1))
                        dve.tensor_scalar(ms[:], ssq[:], 1.0 / DH, EPS, ALU.mult, ALU.add).then_inc(omean, 1)
                        dve.wait_ge(orooted, done(t))
                        dve.wait_ge(odone, done(t, 1, 2))
                        dve.tensor_tensor(mixin[:, p], mixin[:, p], rstd[:].unsqueeze(2).to_broadcast([P, HEADS, DH]), ALU.mult).then_inc(odone, 1)
                    if at(0) is not None:
                        t, p = at(0)
                        for b in range(2):
                            dve.wait_ge(mT_out, done(t, b + 1, 2))
                            dve.wait_ge(product, done(t - 2, 2, 2))
                            dve.tensor_tensor(mT_rest[:, p, 4 * b:4 * b + 4], turn(b), mT_lead[:, p, 4 * b:4 * b + 4].bitcast(F32),
                                              ALU.subtract).then_inc(mT_split, 1)
                    if at(0) is None and at(1) is not None:
                        for q in range(QUARTERS):
                            cols = slice(q * QW, (q + 1) * QW)
                            dve.wait_ge(w_led, q + 1)
                            dve.tensor_tensor(w_rest[:, :, cols], room[q % 3], w_lead[:, :, cols].bitcast(F32),
                                              ALU.subtract).then_inc(w_split, 1)
                    if is_last(at):
                        choose(0)
                    if at(-2) is not None:
                        t, p = at(-2)
                        dve.wait_ge(hturned, done(t, 2, 2))
                        dve.wait_ge(logits, done(t - 1))
                        dve.tensor_copy(h2T[:, 4:8], turn(5)).then_inc(hT_dve, 1)
                    if at(-1) is not None:
                        t, p = at(-1)
                        dve.wait_ge(x_in[p], uses(t, p) + 16)
                        dve.wait_ge(stored_x[p], uses(t, p) + 16)
                        for b in range(2):
                            dve.wait_ge(product, done(t, b + 1, 2))
                            dve.tensor_tensor(x1[:, p, b * 512:(b + 1) * 512], ps[:, 2 + b, :], x[:, p, b * 512:(b + 1) * 512], ALU.add).then_inc(added, 1)
                    if at(-2) is not None:
                        t, p = at(-2)
                        dve.wait_ge(logits, done(t))
                        dve.sem_inc(passed, 1)
                        dve.tensor_tensor(lg[:, bass.ds(t, 1), :].rearrange("p o n -> p (o n)"), ps[:, 6 + p, 0:NG + NE], bias[:], ALU.add).then_inc(logged, 1)
                    if at(-1) is not None:
                        t, p = at(-1)
                        dve.wait_ge(squared, done(t))
                        dve.wait_ge(rooted, done(t - 1))
                        dve.tensor_scalar(ms2[:], ss2[:], 1.0 / D, EPS, ALU.mult, ALU.add).then_inc(mean, 1)
                        dve.wait_ge(rooted, done(t))
                        dve.wait_ge(added, done(t, 2, 2))
                        dve.wait_ge(stored_h[p], uses(t, p) + 16)
                        dve.wait_ge(hturned, done(t - 2, 2, 2))
                        if isinstance(t, int) and t == 0:
                            dve.wait_ge(router_in, ROUTER)
                        dve.scalar_tensor_tensor(h2[:, p], x1[:, p], rstd2[:], lnf[:], ALU.mult, ALU.mult).then_inc(normed, 1)
                    if is_last(at):
                        record(0)
                each(dve, slot)

                choose(1)
                record(1)
                then("total", dve.tensor_copy(total[:], ps[:, 2, 0:NE]))

                def plan(n, ins):
                    ins.then_inc(planned, 1)
                    dve.wait_ge(planned, n)

                plan(1, dve.tensor_tensor(exceed[:], total[:].unsqueeze(2).to_broadcast([P, NE, NR]),
                                          count[:, NG + NE:].unsqueeze(1).to_broadcast([P, NE, NR]), ALU.is_gt))
                plan(2, dve.tensor_reduce(extra[:], exceed[:], AX.X, ALU.add))
                dve.wait_ge(extra_up, 1)
                plan(3, dve.tensor_copy(extraT[:], ps[0:NE, 3, 0:P]))
                dve.wait_ge(extra_up, 2)
                plan(4, dve.tensor_copy(csum[:], ps[:, 4, 0:NE]))
                k = token[:, NT:NT + 1]
                plan(5, dve.tensor_scalar(before[:], csum[:], k, None, ALU.is_le))
                plan(6, dve.tensor_reduce(col[:, 0:1], before[:], AX.X, ALU.add))
                plan(7, dve.tensor_tensor(csum[:], before[:], extra[:], ALU.mult))
                plan(8, dve.tensor_reduce(col[:, 1:2], csum[:], AX.X, ALU.add))
                plan(9, dve.tensor_tensor(col[:, 2:3], k, col[:, 1:2], ALU.subtract))
                plan(10, dve.tensor_scalar(col[:, 3:4], col[:, 2:3], float(TILE), float(TILE), ALU.mult, ALU.add))
                plan(11, dve.scalar_tensor_tensor(col[:, 4:5], col[:, 0:1], float(CAP), col[:, 3:4], ALU.mult, ALU.add))
                plan(12, dve.tensor_scalar(items[:, 0:1], col[:, 0:1], float(NE - 1), None, ALU.min))
                plan(13, dve.tensor_scalar(items[:, 1:2], col[:, 4:5], float(LISTS), None, ALU.min))
                plan(14, dve.tensor_copy(n_more[:], ps[0:1, 4, NE - 1:NE]))

            @block.tensor
            def _(pe):
                for s, per in ((mturned, 2), (product, 2), (hturned, 2), (logits, 1)):
                    pe.sem_inc(s, 2 * per)
                pe.wait_ge(tabs_in, 16 * len(names))

                def count_before(half):
                    pe.wait_ge(routed, route_at(half, f"count{NT // 2 - 1}"))
                    pe.matmul(ps[:, half, :], tab["lt"], oh[:, 2, halves[half]], start=True, stop=False)
                    last = pe.matmul(ps[:, half, :], tab["ones"], before_tile[:, halves[half]], start=False, stop=True)
                    if half == 1:
                        last = pe.matmul(ps[:, 2, 0:NE], tab["ones"], before_tile[:, NT], start=True, stop=True)
                    last.then_inc(counted, 1)

                def product_half(t, p, b):
                    pe.wait_ge(added, done(t - 1, b + 1, 2))
                    if isinstance(t, int) and t == 0:
                        pe.wait_ge(w_split, (b + 1) * QUARTERS // 2)
                    cols = slice(b * 512, (b + 1) * 512)
                    for k in range(KD):
                        pe.matmul(ps[:, 2 + b, :], mT_lead[:, p, k], w_lead[:, k, cols], start=(k == 0), stop=False)
                        pe.matmul(ps[:, 2 + b, :], mT_lead[:, p, k], w_rest[:, k, cols], start=False, stop=False)
                        last = pe.matmul(ps[:, 2 + b, :], mT_rest[:, p, k], w_lead[:, k, cols], start=False, stop=(k == KD - 1))
                    last.then_inc(product, 1)

                def slot(at):
                    if at(-1) is not None:
                        t, p = at(-1)
                        pe.wait_ge(mT_split, done(t, 2, 2))
                        product_half(t, p, 0)
                    if at(0) is not None:
                        t, p = at(0)
                        pe.wait_ge(odone, done(t, 2, 2))
                        pe.wait_ge(mT_split, done(t - 1, 2, 2))
                        for b in range(2):
                            for k in range(4):
                                src = mixin[:, p, k] if b == 0 else za[:, p, 1, k * P:(k + 1) * P]
                                last = pe.transpose(turn(b)[:, k], src, tab["eye"])
                            last.then_inc(mturned, 1)
                    if at(-2) is not None:
                        t, p = at(-2)
                        pe.wait_ge(normed, done(t))
                        for b, out_ in ((0, hT_act), (1, hT_dve)):
                            pe.wait_ge(out_, done(t - 1))
                            for k in range(4):
                                last = pe.transpose(turn(4 + b)[:, k], h2[:, p, (4 * b + k) * P:(4 * b + k + 1) * P], tab["eye"])
                            last.then_inc(hturned, 1)
                    if at(-1) is not None:
                        product_half(*at(-1), 1)
                        if isinstance(at(-1)[0], int) and at(-1)[0] == 0:
                            pe.wait_ge(router_in, ROUTER)
                    if at(-2) is not None:
                        t, p = at(-2)
                        pe.wait_ge(hT_act, done(t))
                        pe.wait_ge(hT_dve, done(t))
                        pe.wait_ge(logged, done(t - 2))
                        for k in range(KD):
                            last = pe.matmul(ps[:, 6 + p, 0:NG + NE], h2T[:, k], wr[:, k], start=(k == 0), stop=(k == KD - 1))
                        last.then_inc(logits, 1)
                    if is_last(at):
                        count_before(0)
                each(pe, slot)
                count_before(1)
                pe.wait_ge(planned, 2)
                pe.transpose(ps[0:NE, 3, 0:P], extra[:], tab["eye"]).then_inc(extra_up, 1)
                pe.wait_ge(planned, 3)
                pe.matmul(ps[:, 4, 0:NE], extraT[:], tab["le"][0:NE, 0:NE], start=True, stop=True).then_inc(extra_up, 1)



def experts(nc, io, scr, ps, sem, n_more):
    with ExitStack() as keep:
        sb = lambda n, s, dt=F32: keep.enter_context(nc.sbuf_tensor(n, s, dt))
        BUF = 4
        FT = FF // P
        eye = sb("g_eye", [P, P])
        XB = 4
        RB = 8
        wgu = [sb(f"g_wgu{b}", [P, KD, 2 * FF]) for b in range(BUF)]
        wd = [sb(f"g_wd{b}", [P, FT, D]) for b in range(BUF)]
        lists = sb("g_lists", [P, NE, 4], I32)
        rec = [sb(f"g_rec{b}", [P, 4], I32) for b in range(RB)]
        xg = [sb(f"g_xg{b}", [P, D]) for b in range(XB)]
        xT = [sb(f"g_xT{b}", [P, KD, TILE]) for b in range(2)]
        sig = sb("g_sig", [P, FT, TILE])
        hid = [sb(f"g_hid{b}", [P, FT, TILE]) for b in range(2)]
        y = [sb(f"g_y{b}", [P, D]) for b in range(2)]
        items = sb("g_items", [1, P, 2], I32)

        consts, lists_in, items_in = sem("g_consts"), sem("g_lists_in"), sem("g_items_in")
        turn = lambda b: ps[:, b, 0:4 * TILE].rearrange("p (k t) -> p k t", k=4)
        up = lambda b: ps[:, 2 + b, 0:4 * TILE].rearrange("p (f t) -> p f t", f=4)
        down = lambda b, n: ps[:, 4 + 2 * b + n, :]

        class Signals:

            def __init__(self, pre):
                s = lambda n: sem(f"g_{pre}_{n}")
                self.gu_in, self.d_in = [s(f"gu_in{b}") for b in range(BUF)], [s(f"d_in{b}") for b in range(BUF)]
                self.listed, self.gathered = s("listed"), [s(f"gathered{b}") for b in range(XB)]
                self.scattered, self.freed = s("scattered"), s("freed")
                self.turned, self.xT_act, self.xT_dve = s("turned"), s("xT_act"), s("xT_dve")
                self.upped, self.sig_act, self.hidden = s("upped"), s("sig_act"), s("hidden")
                self.passed = s("passed")
                self.downed, self.y_act, self.y_dve = s("downed"), s("y_act"), s("y_dve")

        first, more = Signals("first"), Signals("more")


        def weights(sp, s, b, expert, free):
            if free is not None:
                sp.wait_ge(s.upped, free)
            sp.dma_start(wgu[b][:], io["w_gate_up"][0, bass.ds(expert, 1)].rearrange("o (k p) n -> p (o k) n", p=P)).then_inc(s.gu_in[b], 16)
            if free is not None:
                sp.wait_ge(s.downed, free)
            sp.dma_start(wd[b][:], io["w_down"][0, bass.ds(expert, 1)].rearrange("o (j p) n -> p (o j) n", p=P)).then_inc(s.d_in[b], 16)

        def gather(pool, s, b, rb, t, behind):
            if not isinstance(t, int) or t >= behind:
                pool.wait_ge(s.turned, done(t - behind, 2, 2))
                pool.sem_inc(s.passed, 1)
            pool.indirect_dma_start(xg[b][:], None, scr["h2"][:, :], bass.IndirectOffsetOnAxis(rec[rb][:, 0:1], 0),
                                    bounds_check=S - 1, oob_is_err=False).then_inc(s.gathered[b], 16)

        def landed_scatter(pool, s, t):
            pool.wait_ge(s.scattered, 16 * (t + 1))
            pool.sem_inc(s.freed, 1)

        def scatter(pool, s, rb, b2, t):
            pool.wait_ge(s.y_act, done(t))
            pool.wait_ge(s.y_dve, done(t))
            pool.sem_inc(s.passed, 1)
            pool.indirect_dma_start(scr["y"][:, :], bass.IndirectOffsetOnAxis(rec[rb][:, 1:2], 0), y[b2][:], None,
                                    bounds_check=2 * S - 1, oob_is_err=False).then_inc(s.scattered, 16)

        def act_turn(act, s, b2, t):
            act.wait_ge(s.turned, done(t, 1, 2))
            act.wait_ge(s.upped, done(t - 2))
            act.copy(xT[b2][:, 0:4], turn(0)).then_inc(s.xT_act, 1)

        def act_up(act, s, b2, t):
            act.wait_ge(s.upped, done(t))
            act.wait_ge(s.hidden, done(t - 1))
            act.activation(sig[:], up(b2)[:, 0:FT], ACT.Silu).then_inc(s.sig_act, 1)

        def act_down(act, s, rb, b2, t):
            act.wait_ge(s.downed, done(t))
            act.wait_ge(s.freed, done(t - 2))
            act.mul(y[b2][:, 0:512], down(b2, 0), rec[rb][:].bitcast(F32)[:, 2:3]).then_inc(s.y_act, 1)

        def dve_turn(dve, s, b2, t):
            dve.wait_ge(s.turned, done(t, 2, 2))
            dve.wait_ge(s.upped, done(t - 2))
            dve.tensor_copy(xT[b2][:, 4:8], turn(1)).then_inc(s.xT_dve, 1)

        def dve_up(dve, s, b2, t):
            dve.wait_ge(s.sig_act, done(t))
            dve.wait_ge(s.downed, done(t - 2))
            dve.tensor_tensor(hid[b2][:], up(b2)[:, FT:2 * FT], sig[:], ALU.mult).then_inc(s.hidden, 1)

        def dve_down(dve, s, rb, b2, t):
            dve.wait_ge(s.downed, done(t))
            dve.wait_ge(s.freed, done(t - 2))
            dve.tensor_scalar(y[b2][:, 512:], down(b2, 1), rec[rb][:].bitcast(F32)[:, 2:3], None, ALU.mult).then_inc(s.y_dve, 1)

        def pe_turn(pe, s, b, t, r):
            pe.wait_ge(s.gathered[b], 16 * (r + 1))
            for half, emptied in ((0, s.xT_act), (1, s.xT_dve)):
                pe.wait_ge(emptied, done(t - 1))
                for k in range(4):
                    kk = 4 * half + k
                    last = pe.transpose(turn(half)[:, k], xg[b][0:TILE, kk * P:(kk + 1) * P], eye[0:TILE, 0:TILE])
                last.then_inc(s.turned, 1)

        def pe_up(pe, s, b4, b2, t, r4):
            pe.wait_ge(s.xT_act, done(t))
            pe.wait_ge(s.xT_dve, done(t))
            pe.wait_ge(s.hidden, done(t - 2))
            pe.wait_ge(s.gu_in[b4], 16 * (r4 + 1))
            for f in range(2 * FT):
                for k in range(KD):
                    last = pe.matmul(up(b2)[:, f], wgu[b4][:, k, f * P:(f + 1) * P], xT[b2][:, k], start=(k == 0), stop=(k == KD - 1))
            last.then_inc(s.upped, 1)

        def pe_down(pe, s, b4, b2, t, r4):
            pe.wait_ge(s.hidden, done(t))
            pe.wait_ge(s.y_act, done(t - 2))
            pe.wait_ge(s.y_dve, done(t - 2))
            pe.wait_ge(s.d_in[b4], 16 * (r4 + 1))
            for n in range(2):
                for j in range(FT):
                    last = pe.matmul(down(b2, n), hid[b2][:, j], wd[b4][:, j, n * 512:(n + 1) * 512], start=(j == 0), stop=(j == FT - 1))
            last.then_inc(s.downed, 1)

        def each(eng, slot):
            for c in range(-3, 2):
                slot(lambda n, c=c: tile(c + n))
            with eng.Fori(0, NE // RB - 1) as j:
                for q in range(2, 2 + RB):
                    slot(lambda n: (RB * j + q + n, (q + n) % RB, (q + n) % 4, (q + n) % 2, 2 * j + (q + n) // 4))
            for c in range(NE - RB + 2, NE + 1):
                slot(lambda n, c=c: tile(c + n))

        def tile(t):
            return (t, t % RB, t % 4, t % 2, t // 4) if 0 <= t < NE else None

        def again(eng, body):
            n = eng.value_load(n_more[0:1, 0:1], min_val=0, max_val=MORE)
            with eng.If(n > 0):
                body()

        with nc.Block() as block:

            @block.sync
            def _(sp):
                j = NAMES.index("eye")
                sp.dma_start(eye[:], io["tab"][:, j * P:(j + 1) * P]).then_inc(consts, 16)
                every = scr["list"][0:LISTS, :].rearrange("(e r) c -> r e c", r=CAP)[0:P]
                sp.dma_start(lists[:, 0:RB], every[:, 0:RB]).then_inc(consts, 16)
                sp.dma_start(items[:], scr["items"].unsqueeze(0)).then_inc(items_in, 16)
                weights(sp, first, 0, 0, None)
                sp.wait_ge(first.gathered[2], 16)
                weights(sp, first, 1, 1, None)
                sp.dma_start(lists[:, RB:], every[:, RB:]).then_inc(lists_in, 16)
                for b in range(2, BUF):
                    weights(sp, first, b, b, None)
                with sp.Fori(1, NE // BUF) as j:
                    for b in range(BUF):
                        e, free = sp.snap(BUF * j + b), sp.snap(done(BUF * j + b - BUF))
                        weights(sp, first, b, e, free)

                def body():
                    sp.wait_ge(first.downed, done(NE - 1))
                    sp.wait_ge(items_in, 16)
                    with sp.Fori(0, MORE) as k:
                        e = sp.value_load(items[0:1, bass.ds(k, 1), 0], min_val=0, max_val=NE - 1)
                        free = sp.snap(done(k - 1))
                        weights(sp, more, 0, e, free)
                again(sp, body)

            @block.gpsimd
            def _(pool):
                for s in (first, more):
                    pool.sem_inc(s.freed, 2)
                pool.wait_ge(consts, 32)
                pool.wait_ge(items_in, 16)

                for b in range(XB):
                    pool.memset(xg[b][:], 0.0).then_inc(first.listed, 1)

                def slot(at):
                    if at(3) is not None:
                        t, rb, b, b2, r = at(3)
                        if isinstance(t, int) and t == 4:
                            pool.wait_ge(lists_in, 16)
                        pool.sem_inc(first.passed, 1)
                        pool.tensor_copy(rec[rb][:], lists[:, bass.ds(t, 1), :].rearrange("p o c -> p (o c)")).then_inc(first.listed, 1)
                        pool.wait_ge(first.listed, XB + 1 + t)
                        gather(pool, first, b, rb, t, XB)
                    if at(-2) is not None:
                        landed_scatter(pool, first, at(-2)[0])
                    if at(-1) is not None:
                        t, rb, b, b2, r = at(-1)
                        scatter(pool, first, rb, b2, t)
                each(pool, slot)
                landed_scatter(pool, first, NE - 1)

                def body():
                    pool.wait_ge(items_in, 16)
                    with pool.Fori(0, MORE) as k:
                        row = pool.value_load(items[0:1, bass.ds(k, 1), 1], min_val=0, max_val=LISTS)
                        pool.dma_start(rec[0][:], scr["list"][bass.ds(row, P), :]).then_inc(more.listed, 16)
                        pool.wait_ge(more.listed, 16 * (k + 1))
                        gather(pool, more, 0, 0, k, 1)
                        scatter(pool, more, 0, 0, k)
                        landed_scatter(pool, more, k)
                again(pool, body)

            @block.scalar
            def _(act):
                for s in (first, more):
                    for q in (s.xT_act, s.sig_act, s.y_act):
                        act.sem_inc(q, 2)

                def slot(at):
                    if at(0) is not None:
                        act_up(act, first, at(0)[3], at(0)[0])
                    if at(1) is not None:
                        act_turn(act, first, at(1)[3], at(1)[0])
                    if at(-1) is not None:
                        t, rb, b, b2, r = at(-1)
                        act_down(act, first, rb, b2, t)
                each(act, slot)

                def body():
                    with act.Fori(0, MORE) as k:
                        act_turn(act, more, 0, k)
                        act_up(act, more, 0, k)
                        act_down(act, more, 0, 0, k)
                again(act, body)

            @block.vector
            def _(dve):
                for s in (first, more):
                    for q, per in ((s.xT_dve, 1), (s.hidden, 1), (s.y_dve, 1)):
                        dve.sem_inc(q, 2 * per)

                def slot(at):
                    if at(0) is not None:
                        dve_up(dve, first, at(0)[3], at(0)[0])
                    if at(1) is not None:
                        dve_turn(dve, first, at(1)[3], at(1)[0])
                    if at(-1) is not None:
                        t, rb, b, b2, r = at(-1)
                        dve_down(dve, first, rb, b2, t)
                each(dve, slot)

                def body():
                    with dve.Fori(0, MORE) as k:
                        dve_turn(dve, more, 0, k)
                        dve_up(dve, more, 0, k)
                        dve_down(dve, more, 0, 0, k)
                again(dve, body)

            @block.tensor
            def _(pe):
                for s in (first, more):
                    for q, per in ((s.turned, 2), (s.upped, 1), (s.downed, 1)):
                        pe.sem_inc(q, 2 * per)
                pe.wait_ge(consts, 32)

                def slot(at):
                    if at(0) is not None:
                        t, rb, b, b2, r = at(0)
                        pe_up(pe, first, b, b2, t, r)
                    if at(1) is not None:
                        t, rb, b, b2, r = at(1)
                        pe_turn(pe, first, b, t, r)
                    if at(-1) is not None:
                        t, rb, b, b2, r = at(-1)
                        pe_down(pe, first, b, b2, t, r)
                each(pe, slot)

                def body():
                    with pe.Fori(0, MORE) as k:
                        pe_turn(pe, more, 0, k, k)
                        pe_up(pe, more, 0, 0, k, k)
                        pe_down(pe, more, 0, 0, k, k)
                again(pe, body)



def finish(nc, io, scr, ps, sem, out):
    with ExitStack() as keep:
        sb = lambda n, s, dt=F32: keep.enter_context(nc.sbuf_tensor(n, s, dt))
        ln = sb("h_ln", [P, D])
        x = sb("h_x", [P, 2, 3, D])
        s1 = sb("h_sum", [P, 2, D])
        sq = sb("h_sq", [P, D])
        power = sb("h_power", [P, 1])
        ss, ms, rstd = sb("h_ss", [P, 1]), sb("h_ms", [P, 1]), sb("h_rstd", [P, 1])
        o = sb("h_o", [P, 2, D])
        consts, powered = sem("h_consts"), sem("h_powered")
        loaded, stored = [[sem(f"h_{n}{p}") for p in range(2)] for n in ("loaded", "stored")]
        summed, squared, mean, rooted, normed, scaled = [sem("h_" + n) for n in ("summed", "squared", "mean", "rooted", "normed", "scaled")]

        def each(eng, step):
            with eng.Fori(0, NT // 2) as i:
                for p in range(2):
                    step(i, p, 2 * i + p)

        with nc.Block() as block:

            @block.sync
            def _(sp):
                sp.dma_start(ln[:], io["ln_final"].unsqueeze(0).to_broadcast([P, D])).then_inc(consts, 16)

                def step(i, p, t):
                    row, row1, free = sp.snap(t * P), sp.snap(t * P + S), sp.snap(done(t - 2, 2, 2))
                    sp.wait_ge(summed, free)
                    sp.dma_start(x[:, p, 0], scr["x1"][bass.ds(row, P), :]).then_inc(loaded[p], 16)
                    sp.dma_start(x[:, p, 1], scr["y"][bass.ds(row, P), :]).then_inc(loaded[p], 16)
                    sp.dma_start(x[:, p, 2], scr["y"][bass.ds(row1, P), :]).then_inc(loaded[p], 16)
                each(sp, step)

            @block.gpsimd
            def _(pool):
                pool.sem_inc(rooted, 2)
                pool.sem_inc(scaled, 2)
                pool.memset(power[:], -0.5).then_inc(powered, 1)
                pool.wait_ge(powered, 1)
                pool.wait_ge(consts, 16)

                def step(i, p, t):
                    pool.wait_ge(mean, done(t))
                    pool.wait_ge(normed, done(t - 1))
                    pool.tensor_tensor(rstd[:], ms[:], power[:], ALU.pow).then_inc(rooted, 1)
                    pool.wait_ge(normed, done(t))
                    pool.wait_ge(stored[p], landed(i))
                    pool.tensor_tensor(o[:, p], s1[:, p], ln[:], ALU.mult).then_inc(scaled, 1)
                each(pool, step)

            @block.scalar
            def _(act):
                act.sem_inc(squared, 2)
                for p in range(2):
                    act.sem_inc(stored[p], 16)

                def step(i, p, t):
                    act.wait_ge(summed, done(t, 2, 2))
                    act.wait_ge(mean, done(t - 1))
                    act.wait_ge(squared, done(t - 1))
                    act.activation(sq[:], s1[:, p], ACT.Square, accum_out=ss[:]).then_inc(squared, 1)
                    act.wait_ge(scaled, done(t))
                    act.dma_start(out[0, bass.ds(t * P, P), :], o[:, p]).then_inc(stored[p], 16)
                each(act, step)
                for p in range(2):
                    act.wait_ge(stored[p], landed(NT // 2))

            @block.vector
            def _(dve):
                for s, per in ((summed, 2), (mean, 1), (normed, 1)):
                    dve.sem_inc(s, 2 * per)

                def step(i, p, t):
                    dve.wait_ge(loaded[p], 48 * (i + 1))
                    dve.wait_ge(scaled, done(t - 2))
                    dve.tensor_tensor(s1[:, p], x[:, p, 1], x[:, p, 2], ALU.add).then_inc(summed, 1)
                    dve.wait_ge(summed, done(t, 1, 2))
                    dve.tensor_tensor(s1[:, p], s1[:, p], x[:, p, 0], ALU.add).then_inc(summed, 1)
                    dve.wait_ge(squared, done(t))
                    dve.wait_ge(rooted, done(t - 1))
                    dve.tensor_scalar(ms[:], ss[:], 1.0 / D, EPS, ALU.mult, ALU.add).then_inc(mean, 1)
                    dve.wait_ge(rooted, done(t))
                    dve.tensor_scalar(s1[:, p], s1[:, p], rstd[:], None, ALU.mult).then_inc(normed, 1)
                each(dve, step)


INPUTS = ["x", "ln_mix", "w_in", "dn_conv", "dn_A_log", "dn_dt_bias", "dn_norm", "attn_sink", "w_out", "ln_ffn", "w_group", "b_group",
          "w_expert", "b_expert", "w_gate_up", "w_down", "ln_final"]


def kernel(**inputs):
    import concourse.bacc as bacc
    from concourse.bass_utils import run_bass_kernel_spmd

    nc = bacc.Bacc("TRN2", target_bir_lowering=False, num_devices=1)
    arrays = {"in_" + n: np.ascontiguousarray(inputs[n]) for n in INPUTS}
    arrays.update({"in_" + n: a for n, a in TABLES.items()})
    io = {n[3:]: nc.dram_tensor(n, a.shape, mybir.dt.from_np(a.dtype), kind="ExternalInput").ap() for n, a in arrays.items()}
    out = nc.dram_tensor("out", (1, S, D), F32, kind="ExternalOutput").ap()
    program(nc, io, out)
    r = run_bass_kernel_spmd(nc, [arrays], core_ids=[0])
    return r.results[0]["out"]
```
